# Optimizing a Trainium2 kernel written in Bass

```python
import jax, jax.numpy as jnp
from jax import lax
import numpy as np
import jax
import jax.numpy as jnp

D_MODEL = 1024
BATCH = 1
SEQ = 512
DEPTH = 1

PLE_DIM = 256
D_MIX = D_MODEL
W_GRP = D_MIX // 4
N_HEADS_GRP = 4
HEAD_DIM = W_GRP // N_HEADS_GRP
GMLP_CHUNK = 128
RGLRU_CONV = 4
RGLRU_C = 8.0
HGRN_CHUNK = 64
POOL_WINDOWS = (2, 4, 8, 16)
D_FF = 2816
FFN_CONV = 3
EPS = 1e-6
COLS_A = 2 * W_GRP
COLS_B = 2 * W_GRP
COLS_C = 4 * W_GRP
COLS_D = W_GRP
OFF_B = COLS_A
OFF_C = OFF_B + COLS_B
OFF_D = OFF_C + COLS_C
D_PROJ = OFF_D + COLS_D


def rms_norm(x, g):
    xf = x.astype(jnp.float32)
    y = xf * lax.rsqrt(jnp.mean(xf * xf, axis=-1, keepdims=True) + EPS)
    return (y * g.astype(jnp.float32)).astype(x.dtype)

def causal_dwconv(x, w, b):
    k_width = w.shape[0]
    s = x.shape[1]
    xp = jnp.pad(x, ((0, 0), (k_width - 1, 0), (0, 0)))
    y = b
    for k in range(k_width):
        y = y + xp[:, k:k + s] * w[k]
    return y

def gmlp_mixer(ab, ln_g, ln_b, ws, bs):
    bsz, s, _ = ab.shape
    ab = jax.nn.gelu(ab)
    u, v = jnp.split(ab, 2, axis=-1)
    vf = v.astype(jnp.float32)
    mu = jnp.mean(vf, axis=-1, keepdims=True)
    var = jnp.mean(jnp.square(vf - mu), axis=-1, keepdims=True)
    vn = ((vf - mu) * lax.rsqrt(var + EPS) * ln_g.astype(jnp.float32) + ln_b.astype(jnp.float32)).astype(v.dtype)
    vn = vn.reshape(bsz, s // GMLP_CHUNK, GMLP_CHUNK, N_HEADS_GRP, HEAD_DIM)
    mask = jnp.tril(jnp.ones((GMLP_CHUNK, GMLP_CHUNK), dtype=bool))
    wm = jnp.where(mask, ws, jnp.zeros_like(ws))
    sv = jnp.einsum('hts,bnshd->bnthd', wm, vn) + bs.T[:, :, None]
    return u * sv.reshape(bsz, s, W_GRP)

def rglru_mixer(xb, gb, conv_w, conv_b, wa, ba, wx, bx, lam):
    bsz, s, _ = xb.shape
    xc = causal_dwconv(xb, conv_w, conv_b)
    xh = xc.reshape(bsz, s, N_HEADS_GRP, HEAD_DIM)
    r = jax.nn.sigmoid(jnp.einsum('bshd,hde->bshe', xh, wa).reshape(bsz, s, W_GRP) + ba)
    i = jax.nn.sigmoid(jnp.einsum('bshd,hde->bshe', xh, wx).reshape(bsz, s, W_GRP) + bx)
    log_a = -RGLRU_C * r.astype(jnp.float32) * jax.nn.softplus(-lam.astype(jnp.float32))
    a = jnp.exp(log_a)
    mult = jnp.sqrt(-jnp.expm1(2.0 * log_a))
    bterm = mult * (i * xc).astype(jnp.float32)

    def combine(c1, c2):
        a1, b1 = c1
        a2, b2 = c2
        return a1 * a2, a2 * b1 + b2

    _, h = lax.associative_scan(combine, (a, bterm), axis=1)
    return h.astype(xb.dtype) * jax.nn.gelu(gb)

def hgrn2_mixer(q, f, i, g, lb, norm_g):
    bsz, s, _ = q.shape
    n_chunks = s // HGRN_CHUNK
    qf = jax.nn.silu(q.astype(jnp.float32))
    fgate = lb + (1.0 - lb) * jax.nn.sigmoid(f.astype(jnp.float32))
    log_f = jnp.log(fgate)
    kf = 1.0 - fgate
    vf = i.astype(jnp.float32)

    def to_chunks(t):
        return t.reshape(bsz, n_chunks, HGRN_CHUNK, N_HEADS_GRP, HEAD_DIM).transpose(1, 0, 3, 2, 4)

    qc, kc, vc = to_chunks(qf), to_chunks(kf), to_chunks(vf)
    bc = jnp.cumsum(to_chunks(log_f), axis=3)
    mask = jnp.tril(jnp.ones((HGRN_CHUNK, HGRN_CHUNK), dtype=bool))[:, :, None]

    def step(state, xs):
        qq, kk, vv, bb = xs
        diff = bb[:, :, :, None, :] - bb[:, :, None, :, :]
        decay = jnp.exp(jnp.where(mask, diff, -jnp.inf))
        att = jnp.einsum('bhtd,bhsd,bhtsd->bhts', qq, kk, decay)
        o = jnp.einsum('bhts,bhsv->bhtv', att, vv) + jnp.einsum('bhtd,bhdv->bhtv', qq * jnp.exp(bb), state)
        bl = bb[:, :, -1:, :]
        new_state = jnp.exp(bl[:, :, 0, :])[..., None] * state + jnp.einsum('bhsd,bhsv->bhdv', kk * jnp.exp(bl - bb), vv)
        return new_state, o

    s0 = jnp.zeros((bsz, N_HEADS_GRP, HEAD_DIM, HEAD_DIM), jnp.float32)
    _, o = lax.scan(step, s0, (qc, kc, vc, bc))
    o = o.transpose(1, 0, 3, 2, 4).reshape(bsz, s, N_HEADS_GRP, HEAD_DIM)
    o = o * lax.rsqrt(jnp.mean(o * o, axis=-1, keepdims=True) + EPS) * norm_g.astype(jnp.float32)
    o = o.reshape(bsz, s, W_GRP) * jax.nn.silu(g.astype(jnp.float32))
    return o.astype(q.dtype)

def pool_mixer(xd, wd, scale):
    bsz, s, _ = xd.shape
    xf = xd.astype(jnp.float32)
    cs = jnp.cumsum(xf, axis=1)
    pos = jnp.arange(1, s + 1, dtype=jnp.float32)[None, :, None]
    outs = []
    for j, w in enumerate(POOL_WINDOWS):
        c = cs[..., j * HEAD_DIM:(j + 1) * HEAD_DIM]
        shifted = jnp.pad(c, ((0, 0), (w, 0), (0, 0)))[:, :s]
        mean = (c - shifted) / jnp.minimum(pos, float(w))
        outs.append(mean - xf[..., j * HEAD_DIM:(j + 1) * HEAD_DIM])
    pooled = jnp.stack(outs, axis=2)
    y = jnp.einsum('bsgd,gde->bsge', pooled, wd.astype(jnp.float32)).reshape(bsz, s, W_GRP)
    return (y * scale.astype(jnp.float32)).astype(xd.dtype)

def first_inputs(seed: int = 0) -> dict:
    key = jax.random.key(seed)
    ks = jax.random.split(key, 32)

    def nrm(k, shape, scale):
        return jax.random.normal(k, shape, jnp.float32) * scale

    u = jax.random.uniform(ks[14], (DEPTH, W_GRP), jnp.float32, 0.9, 0.999)
    a_base = u ** (1.0 / RGLRU_C)
    b_lam = jnp.log(a_base) - jnp.log1p(-a_base)
    return {
        "x": nrm(ks[0], (BATCH, SEQ, D_MODEL), 1.0),
        "p": nrm(ks[1], (DEPTH, BATCH, SEQ, PLE_DIM), 1.0),
        "norm1_g": 1.0 + nrm(ks[2], (DEPTH, D_MODEL), 0.02),
        "w_in": nrm(ks[3], (DEPTH, D_MODEL, D_PROJ), D_MODEL ** -0.5),
        "a_ln_g": 1.0 + nrm(ks[4], (DEPTH, W_GRP), 0.02),
        "a_ln_b": nrm(ks[5], (DEPTH, W_GRP), 0.02),
        "a_ws": nrm(ks[6], (DEPTH, N_HEADS_GRP, GMLP_CHUNK, GMLP_CHUNK), GMLP_CHUNK ** -0.5),
        "a_bs": 1.0 + nrm(ks[7], (DEPTH, N_HEADS_GRP, GMLP_CHUNK), 0.1),
        "b_conv_w": nrm(ks[8], (DEPTH, RGLRU_CONV, W_GRP), RGLRU_CONV ** -0.5),
        "b_conv_b": nrm(ks[9], (DEPTH, W_GRP), 0.02),
        "b_wa": nrm(ks[10], (DEPTH, N_HEADS_GRP, HEAD_DIM, HEAD_DIM), HEAD_DIM ** -0.5),
        "b_ba": nrm(ks[11], (DEPTH, W_GRP), 0.02),
        "b_wx": nrm(ks[12], (DEPTH, N_HEADS_GRP, HEAD_DIM, HEAD_DIM), HEAD_DIM ** -0.5),
        "b_bx": nrm(ks[13], (DEPTH, W_GRP), 0.02),
        "b_lam": b_lam,
        "c_lb": nrm(ks[15], (DEPTH, W_GRP), 0.5),
        "c_norm_g": 1.0 + nrm(ks[16], (DEPTH, HEAD_DIM), 0.02),
        "d_w": nrm(ks[17], (DEPTH, N_HEADS_GRP, HEAD_DIM, HEAD_DIM), HEAD_DIM ** -0.5),
        "d_scale": 1.0 + nrm(ks[18], (DEPTH, W_GRP), 0.1),
        "w_out": nrm(ks[19], (DEPTH, D_MIX, D_MODEL), D_MIX ** -0.5),
        "norm2_g": 1.0 + nrm(ks[20], (DEPTH, D_MODEL), 0.02),
        "w_up": nrm(ks[21], (DEPTH, D_MODEL, 2 * D_FF), D_MODEL ** -0.5),
        "ffn_conv_w": nrm(ks[22], (DEPTH, FFN_CONV, 2 * D_FF), FFN_CONV ** -0.5),
        "ffn_conv_b": nrm(ks[23], (DEPTH, 2 * D_FF), 0.02),
        "w_down": nrm(ks[24], (DEPTH, D_FF, D_MODEL), D_FF ** -0.5),
        "norm3_g": 1.0 + nrm(ks[25], (DEPTH, D_MODEL), 0.02),
        "w_pe": nrm(ks[26], (DEPTH, PLE_DIM, D_MODEL), PLE_DIM ** -0.5),
        "w_pg": nrm(ks[27], (DEPTH, D_MODEL, D_MODEL), D_MODEL ** -0.5),
        "final_g": 1.0 + nrm(ks[28], (D_MODEL,), 0.02),
    }

def first_block(x, p, norm1_g, w_in, a_ln_g, a_ln_b, a_ws, a_bs, b_conv_w, b_conv_b, b_wa, b_ba, b_wx, b_bx, b_lam, c_lb, c_norm_g, d_w, d_scale, w_out, norm2_g, w_up, ffn_conv_w, ffn_conv_b, w_down, norm3_g, w_pe, w_pg, final_g):
    lbs = jnp.cumsum(jax.nn.softmax(c_lb.astype(jnp.float32), axis=0), axis=0)
    lbs = lbs - lbs[0:1]
    for l in range(DEPTH):
        h = rms_norm(x, norm1_g[l])
        z = h @ w_in[l]
        y_a = gmlp_mixer(z[..., :OFF_B], a_ln_g[l], a_ln_b[l], a_ws[l], a_bs[l])
        y_b = rglru_mixer(z[..., OFF_B:OFF_B + W_GRP], z[..., OFF_B + W_GRP:OFF_C],
                          b_conv_w[l], b_conv_b[l], b_wa[l], b_ba[l], b_wx[l], b_bx[l], b_lam[l])
        zc = z[..., OFF_C:OFF_D]
        y_c = hgrn2_mixer(zc[..., :W_GRP], zc[..., W_GRP:2 * W_GRP], zc[..., 2 * W_GRP:3 * W_GRP],
                          zc[..., 3 * W_GRP:], lbs[l], c_norm_g[l])
        y_d = pool_mixer(z[..., OFF_D:], d_w[l], d_scale[l])
        mix = jnp.concatenate([y_a, y_b, y_c, y_d], axis=-1)
        x = x + mix @ w_out[l]
        hf = rms_norm(x, norm2_g[l]) @ w_up[l]
        hf = causal_dwconv(hf, ffn_conv_w[l], ffn_conv_b[l])
        gt, val = jnp.split(hf, 2, axis=-1)
        x = x + (jax.nn.gelu(gt) * val) @ w_down[l]
        gate = jax.nn.sigmoid(rms_norm(x, norm3_g[l]) @ w_pg[l])
        x = x + (p[l] @ w_pe[l]) * gate
    return rms_norm(x, final_g)


DEPTH_2 = 2

HEAD_DIM_2 = 64
ATTN_Q_HEADS = 8
ATTN_KV_HEADS = 2
ATTN_GROUP = ATTN_Q_HEADS // ATTN_KV_HEADS
ATTN_WIDTH = ATTN_Q_HEADS * HEAD_DIM_2
ATTN_KV_WIDTH = ATTN_KV_HEADS * HEAD_DIM_2
WINDOW = 128
ATTN_BLOCK = 128
RWKV_HEADS = 8
RWKV_WIDTH = RWKV_HEADS * HEAD_DIM_2
DECAY_LORA = 64
ICLR_LORA = 64
GATE_LORA = 128
RWKV_SIZES = (RWKV_WIDTH, RWKV_WIDTH, RWKV_WIDTH, DECAY_LORA, ICLR_LORA, GATE_LORA)
RWKV_COLS = sum(RWKV_SIZES)
RWKV_LN_EPS = 64e-5
RET_HEADS = 8
RET_WIDTH = RET_HEADS * HEAD_DIM_2
RET_CHUNK = 128
ROPE_BASE = 10000.0
N_BRANCH = 3
IN_SIZES = (ATTN_WIDTH, ATTN_KV_WIDTH, ATTN_KV_WIDTH, RWKV_COLS,
            RET_WIDTH, RET_WIDTH, RET_WIDTH, RET_WIDTH, N_BRANCH * D_MODEL)
IN_WIDTH = sum(IN_SIZES)
D_FF_2 = -((-8 * D_MODEL) // (3 * 256)) * 256
NORM_EPS = 1e-6


def _split(t, sizes):
    out, start = [], 0
    for s in sizes:
        out.append(t[..., start:start + s])
        start += s
    return out

def _rms(x, eps=NORM_EPS):
    xf = x.astype(jnp.float32)
    return (xf * lax.rsqrt(jnp.mean(xf * xf, axis=-1, keepdims=True) + eps)).astype(x.dtype)

def sliding_window_attention(q, k, v, sinks):
    B, T = q.shape[0], q.shape[1]
    C = ATTN_BLOCK
    NB = T // C
    qb = q.reshape(B, NB, C, ATTN_KV_HEADS, ATTN_GROUP, HEAD_DIM_2)

    def band(t):
        tb = t.reshape(B, NB, C, ATTN_KV_HEADS, HEAD_DIM_2)
        prev = jnp.concatenate([jnp.zeros_like(tb[:, :1]), tb[:, :-1]], axis=1)
        return jnp.concatenate([prev, tb], axis=2)

    kb, vb = band(k), band(v)
    s = jnp.einsum('bnqhgd,bnshd->bnhgqs', qb, kb).astype(jnp.float32) * (HEAD_DIM_2 ** -0.5)
    qi = jnp.arange(C)[:, None]
    si = jnp.arange(2 * C)[None, :]
    rel = qi + C - si
    key_pos = jnp.arange(NB)[:, None, None] * C + si[None] - C
    mask = (rel >= 0) & (rel < WINDOW) & (key_pos >= 0)
    s = jnp.where(mask[None, :, None, None], s, -jnp.inf)
    sink = sinks.astype(jnp.float32).reshape(ATTN_KV_HEADS, ATTN_GROUP)[None, None, :, :, None, None]
    m = jnp.maximum(jnp.max(s, axis=-1, keepdims=True), sink)
    p = jnp.exp(s - m)
    p = p / (jnp.sum(p, axis=-1, keepdims=True) + jnp.exp(sink - m))
    o = jnp.einsum('bnhgqs,bnshd->bnqhgd', p.astype(v.dtype), vb)
    return o.reshape(B, T, ATTN_WIDTH)

def rwkv7_time_mix(h, shift_mu, w0, w2, a0, a2, g2, k_k, k_a, r_k, lnx_g, lnx_b):
    B, T = h.shape[0], h.shape[1]
    H, N = RWKV_HEADS, HEAD_DIM_2
    h_prev = jnp.pad(h, ((0, 0), (1, 0), (0, 0)))[:, :-1]
    z = h + shift_mu * (h_prev - h)
    r, k, v, wd, ad, gd = _split(z, RWKV_SIZES)
    w_log = -jax.nn.softplus(-(w0 + jnp.tanh(wd) @ w2)) - 0.5
    decay = jnp.exp(-jnp.exp(w_log.astype(jnp.float32)))
    a = jax.nn.sigmoid(a0 + ad @ a2)
    g = jax.nn.sigmoid(gd) @ g2
    kk = (k * k_k).reshape(B, T, H, N).astype(jnp.float32)
    kk = kk / jnp.maximum(jnp.linalg.norm(kk, axis=-1, keepdims=True), 1e-12)
    k = k * (1.0 + (a - 1.0) * k_a)

    def heads(t):
        return t.reshape(B, T, H, N).astype(jnp.float32)

    r_h, k_h, v_h, a_h, w_h = heads(r), heads(k), heads(v), heads(a), heads(decay)
    xs = tuple(t.transpose(1, 0, 2, 3) for t in (r_h, w_h, k_h, v_h, -kk, kk * a_h))

    def step(S, inp):
        r_t, w_t, k_t, v_t, a_t, b_t = inp
        Sa = jnp.einsum('bhvk,bhk->bhv', S, a_t)
        S = S * w_t[:, :, None, :] + Sa[..., None] * b_t[:, :, None, :] + v_t[..., None] * k_t[:, :, None, :]
        return S, jnp.einsum('bhvk,bhk->bhv', S, r_t)

    S0 = jnp.zeros((B, H, N, N), jnp.float32)
    _, y = lax.scan(step, S0, xs)
    y = y.transpose(1, 0, 2, 3)
    mu = jnp.mean(y, axis=-1, keepdims=True)
    var = jnp.mean(jnp.square(y - mu), axis=-1, keepdims=True)
    y = ((y - mu) * lax.rsqrt(var + RWKV_LN_EPS)).reshape(B, T, RWKV_WIDTH)
    y = y * lnx_g.astype(jnp.float32) + lnx_b.astype(jnp.float32)
    bonus = jnp.sum(r_h * k_h * r_k.astype(jnp.float32), axis=-1, keepdims=True) * v_h
    y = (y + bonus.reshape(B, T, RWKV_WIDTH)) * g.astype(jnp.float32)
    return y.astype(h.dtype)

def _rotary(x, pos):
    half = HEAD_DIM_2 // 2
    inv_freq = 1.0 / (ROPE_BASE ** (jnp.arange(half, dtype=jnp.float32) * 2.0 / HEAD_DIM_2))
    ang = pos.astype(jnp.float32)[:, None] * inv_freq[None, :]
    cos, sin = jnp.cos(ang)[:, None, :], jnp.sin(ang)[:, None, :]
    x1, x2 = x[..., :half], x[..., half:]
    return jnp.concatenate([x1 * cos - x2 * sin, x2 * cos + x1 * sin], axis=-1)

def retention(q, k, v, gate):
    B, T = q.shape[0], q.shape[1]
    H, d, C = RET_HEADS, HEAD_DIM_2, RET_CHUNK
    NC = T // C
    pos = jnp.arange(T)
    qh = _rotary(q.reshape(B, T, H, d).astype(jnp.float32), pos)
    kh = _rotary(k.reshape(B, T, H, d).astype(jnp.float32), pos) * (d ** -0.5)
    vh = v.reshape(B, T, H, d).astype(jnp.float32)
    log_gamma = jnp.log1p(-jnp.power(2.0, -5.0 - jnp.arange(H, dtype=jnp.float32)))
    idx = jnp.arange(C, dtype=jnp.float32)
    diff = idx[:, None] - idx[None, :]
    dmat = jnp.where(diff >= 0, jnp.exp(log_gamma[:, None, None] * jnp.maximum(diff, 0.0)), 0.0)
    xi = jnp.exp(log_gamma[:, None] * (idx[None, :] + 1.0))
    zeta = jnp.exp(log_gamma[:, None] * (C - 1.0 - idx[None, :]))
    chunk_decay = jnp.exp(log_gamma * C)
    qc = qh.reshape(B, NC, C, H, d)
    kc = kh.reshape(B, NC, C, H, d)
    vc = vh.reshape(B, NC, C, H, d)
    s = jnp.einsum('bnihd,bnjhd->bnhij', qc, kc) * dmat
    inner = jnp.einsum('bnhij,bnjhe->bnihe', s, vc)
    kv = jnp.einsum('bnjhd,bnjhe,hj->nbhde', kc, vc, zeta)

    def step(R, kv_n):
        return R * chunk_decay[None, :, None, None] + kv_n, R

    _, r_prev = lax.scan(step, jnp.zeros((B, H, d, d), jnp.float32), kv)
    cross = jnp.einsum('bnihd,nbhde,hi->bnihe', qc, r_prev, xi)
    o = _rms((inner + cross).reshape(B, T, H, d)).reshape(B, T, RET_WIDTH)
    o = o * jax.nn.silu(gate.astype(jnp.float32))
    return o.astype(q.dtype)

def hybrid_layer(x, norm1_g, w_in, attn_q_norm_g, attn_k_norm_g, attn_sinks, w_attn_o,
                 rwkv_shift_mu, rwkv_w0, rwkv_w2, rwkv_a0, rwkv_a2, rwkv_g2, rwkv_k_k, rwkv_k_a,
                 rwkv_r_k, rwkv_lnx_g, rwkv_lnx_b, w_rwkv_o, w_ret_o, w_out,
                 norm2_g, w_ffn_gate, w_ffn_up, w_ffn_down):
    B, T, D = x.shape
    h = _rms(x) * norm1_g
    proj = h @ w_in
    aq, ak, av, rw, rq, rk, rv, rg, gates = _split(proj, IN_SIZES)
    aq = _rms(aq.reshape(B, T, ATTN_Q_HEADS, HEAD_DIM_2)) * attn_q_norm_g
    ak = _rms(ak.reshape(B, T, ATTN_KV_HEADS, HEAD_DIM_2)) * attn_k_norm_g
    av = av.reshape(B, T, ATTN_KV_HEADS, HEAD_DIM_2)
    o_a = sliding_window_attention(aq, ak, av, attn_sinks) @ w_attn_o
    o_b = rwkv7_time_mix(rw, rwkv_shift_mu, rwkv_w0, rwkv_w2, rwkv_a0, rwkv_a2, rwkv_g2,
                         rwkv_k_k, rwkv_k_a, rwkv_r_k, rwkv_lnx_g, rwkv_lnx_b) @ w_rwkv_o
    o_c = retention(rq, rk, rv, rg) @ w_ret_o
    g = jax.nn.sigmoid(gates).reshape(B, T, N_BRANCH, D)
    mixed = g[:, :, 0] * o_a + g[:, :, 1] * o_b + g[:, :, 2] * o_c
    x = x + mixed @ w_out
    h2 = _rms(x) * norm2_g
    x = x + (jax.nn.silu(h2 @ w_ffn_gate) * (h2 @ w_ffn_up)) @ w_ffn_down
    return x

def second_inputs(seed: int = 0) -> dict:
    key = jax.random.key(seed)
    ks = jax.random.split(key, 25)
    L = DEPTH_2

    def nrm(k, shape, scale):
        return jax.random.normal(k, shape, jnp.float32) * scale

    return {
        'x': nrm(ks[0], (BATCH, SEQ, D_MODEL), 1.0),
        'norm1_g': 1.0 + nrm(ks[1], (L, D_MODEL), 0.02),
        'w_in': nrm(ks[2], (L, D_MODEL, IN_WIDTH), D_MODEL ** -0.5),
        'attn_q_norm_g': 1.0 + nrm(ks[3], (L, HEAD_DIM_2), 0.02),
        'attn_k_norm_g': 1.0 + nrm(ks[4], (L, HEAD_DIM_2), 0.02),
        'attn_sinks': nrm(ks[5], (L, ATTN_Q_HEADS), 0.5),
        'w_attn_o': nrm(ks[6], (L, ATTN_WIDTH, D_MODEL), ATTN_WIDTH ** -0.5),
        'rwkv_shift_mu': jax.random.uniform(ks[7], (L, RWKV_COLS), jnp.float32),
        'rwkv_w0': jax.random.uniform(ks[8], (L, RWKV_WIDTH), jnp.float32, minval=-6.0, maxval=1.0),
        'rwkv_w2': nrm(ks[9], (L, DECAY_LORA, RWKV_WIDTH), 0.1 * DECAY_LORA ** -0.5),
        'rwkv_a0': nrm(ks[10], (L, RWKV_WIDTH), 0.1),
        'rwkv_a2': nrm(ks[11], (L, ICLR_LORA, RWKV_WIDTH), ICLR_LORA ** -0.5),
        'rwkv_g2': nrm(ks[12], (L, GATE_LORA, RWKV_WIDTH), GATE_LORA ** -0.5),
        'rwkv_k_k': 0.85 + nrm(ks[13], (L, RWKV_WIDTH), 0.02),
        'rwkv_k_a': 1.0 + nrm(ks[14], (L, RWKV_WIDTH), 0.02),
        'rwkv_r_k': nrm(ks[15], (L, RWKV_HEADS, HEAD_DIM_2), 0.1),
        'rwkv_lnx_g': 1.0 + nrm(ks[16], (L, RWKV_WIDTH), 0.02),
        'rwkv_lnx_b': nrm(ks[17], (L, RWKV_WIDTH), 0.02),
        'w_rwkv_o': nrm(ks[18], (L, RWKV_WIDTH, D_MODEL), RWKV_WIDTH ** -0.5),
        'w_ret_o': nrm(ks[19], (L, RET_WIDTH, D_MODEL), RET_WIDTH ** -0.5),
        'w_out': nrm(ks[20], (L, D_MODEL, D_MODEL), D_MODEL ** -0.5),
        'norm2_g': 1.0 + nrm(ks[21], (L, D_MODEL), 0.02),
        'w_ffn_gate': nrm(ks[22], (L, D_MODEL, D_FF_2), D_MODEL ** -0.5),
        'w_ffn_up': nrm(ks[23], (L, D_MODEL, D_FF_2), D_MODEL ** -0.5),
        'w_ffn_down': nrm(ks[24], (L, D_FF_2, D_MODEL), D_FF_2 ** -0.5),
    }

def second_block(x, norm1_g, w_in, attn_q_norm_g, attn_k_norm_g, attn_sinks, w_attn_o,
              rwkv_shift_mu, rwkv_w0, rwkv_w2, rwkv_a0, rwkv_a2, rwkv_g2, rwkv_k_k, rwkv_k_a,
              rwkv_r_k, rwkv_lnx_g, rwkv_lnx_b, w_rwkv_o, w_ret_o, w_out,
              norm2_g, w_ffn_gate, w_ffn_up, w_ffn_down):
    for l in range(DEPTH_2):
        x = hybrid_layer(x, norm1_g[l], w_in[l], attn_q_norm_g[l], attn_k_norm_g[l], attn_sinks[l],
                         w_attn_o[l], rwkv_shift_mu[l], rwkv_w0[l], rwkv_w2[l], rwkv_a0[l], rwkv_a2[l],
                         rwkv_g2[l], rwkv_k_k[l], rwkv_k_a[l], rwkv_r_k[l], rwkv_lnx_g[l], rwkv_lnx_b[l],
                         w_rwkv_o[l], w_ret_o[l], w_out[l], norm2_g[l], w_ffn_gate[l], w_ffn_up[l],
                         w_ffn_down[l])
    return x


def setup_inputs(seed=0):
    out = dict(first_inputs(seed))
    for name, value in second_inputs(seed + 1).items():
        if name != "x":
            out[name + "_2"] = value
    return out


def reference(
    x, p, norm1_g, w_in, a_ln_g, a_ln_b, a_ws, a_bs, b_conv_w, b_conv_b, b_wa, b_ba, b_wx, b_bx,
    b_lam, c_lb, c_norm_g, d_w, d_scale, w_out, norm2_g, w_up, ffn_conv_w, ffn_conv_b, w_down,
    norm3_g, w_pe, w_pg, final_g, norm1_g_2, w_in_2, attn_q_norm_g_2, attn_k_norm_g_2,
    attn_sinks_2, w_attn_o_2, rwkv_shift_mu_2, rwkv_w0_2, rwkv_w2_2, rwkv_a0_2, rwkv_a2_2,
    rwkv_g2_2, rwkv_k_k_2, rwkv_k_a_2, rwkv_r_k_2, rwkv_lnx_g_2, rwkv_lnx_b_2, w_rwkv_o_2,
    w_ret_o_2, w_out_2, norm2_g_2, w_ffn_gate_2, w_ffn_up_2, w_ffn_down_2,
):
    x = first_block(
        x, p, norm1_g, w_in, a_ln_g, a_ln_b, a_ws, a_bs, b_conv_w, b_conv_b, b_wa, b_ba, b_wx,
        b_bx, b_lam, c_lb, c_norm_g, d_w, d_scale, w_out, norm2_g, w_up, ffn_conv_w, ffn_conv_b,
        w_down, norm3_g, w_pe, w_pg, final_g,
    )
    return second_block(
        x, norm1_g_2, w_in_2, attn_q_norm_g_2, attn_k_norm_g_2, attn_sinks_2, w_attn_o_2,
        rwkv_shift_mu_2, rwkv_w0_2, rwkv_w2_2, rwkv_a0_2, rwkv_a2_2, rwkv_g2_2, rwkv_k_k_2,
        rwkv_k_a_2, rwkv_r_k_2, rwkv_lnx_g_2, rwkv_lnx_b_2, w_rwkv_o_2, w_ret_o_2, w_out_2,
        norm2_g_2, w_ffn_gate_2, w_ffn_up_2, w_ffn_down_2,
    )


_drawn_inputs = setup_inputs


def setup_inputs(seed=0):
    import zlib

    import numpy as np

    out = dict(_drawn_inputs(seed))
    spreads = {}
    factors = {'a_ln_g': 8.0,
     'a_ln_b': 7.787,
     'b_ba': 8.0,
     'b_bx': 8.0,
     'c_norm_g': 5.286,
     'norm2_g': 2.71,
     'norm3_g': 26.327,
     'attn_q_norm_g_2': 8.0,
     'attn_k_norm_g_2': 8.0,
     'attn_sinks_2': 147.906,
     'rwkv_w2_2': 8.0,
     'rwkv_a0_2': 3.614,
     'rwkv_k_k_2': 7.183,
     'rwkv_k_a_2': 5.912,
     'rwkv_lnx_g_2': 6.065,
     'rwkv_lnx_b_2': 5.984,
     'norm2_g_2': 2.706}
    for name, (base, spread) in spreads.items():
        noise = np.random.default_rng([zlib.crc32(name.encode()), seed]).standard_normal(out[name].shape)
        drawn = base * np.exp(spread * noise) if base else spread * noise
        out[name] = jnp.asarray(drawn.astype(out[name].dtype))
    for name, factor in factors.items():
        out[name] = (out[name] * factor).astype(out[name].dtype)
    return out
```

```python
from contextlib import ExitStack

import numpy as np
import concourse.bass as bass
from concourse import mybir

F32, F32R, U32 = mybir.dt.float32, mybir.dt.float32r, mybir.dt.uint32
ACT, ALU = mybir.ActivationFunctionType, mybir.AluOpType
AX = mybir.AxisListType

P = 128
T = 512
NT = T // P
D = 1024
DC = D // P
LAYERS = 2
HD = 64
CH = 64
FFC = 2816 // P
PARTS = (8, 8, 6)
EPS = 1e-6
LN_EPS = 64e-5
DECAY = float(np.exp(-0.5))

B1_IN, X_OUT, O_PAIRS, PE_PAIRS = 9, 4, 24, 8
FFN_PAIRS = sum(PARTS) + X_OUT * len(PARTS)
B1_PAIRS = B1_IN + X_OUT + FFN_PAIRS + PE_PAIRS
RW_PAIRS, RET_PAIRS, AT_PAIRS = 7, 8, 3
LAYER_PAIRS = RW_PAIRS + RET_PAIRS + AT_PAIRS + O_PAIRS + X_OUT + FFN_PAIRS

G_N1, G_N2, G_N3, G_FIN, G_L = 0, 1, 2, 3, 4

V_MU, V_W0, V_A0, V_KK, V_KA, V_RK, V_LNG, V_LNB, V_GQ, V_GK, V_SINK = 0, 14, 18, 22, 26, 30, 34, 38, 42, 43, 44
V_N = 52
U_CW, U_CB, U_BA, U_BX, U_LAM, U_CN, U_DS, U_FW, U_FB = 0, 8, 10, 12, 14, 16, 18, 20, 20 + 3 * 2 * FFC
U_N = U_FB + 2 * FFC


def shape_constants():
    i = np.arange(P)
    row_head = i // HD
    c = {}
    c["ident"] = np.eye(P)
    c["headones"] = (row_head[:, None] == row_head[None, :]) * 1.0
    c["ones"] = np.ones((P, P))
    c["eps"] = np.tile(np.array([EPS, LN_EPS]), (P, 1))
    half = HD // 2
    swap = np.where(i % HD < half, i + half, i - half)
    c["swap"] = (swap[:, None] == i[None, :]) * 1.0
    inv = (1.0 / (np.float32(10000.0) ** (np.arange(half, dtype=np.float32) * np.float32(2.0) / np.float32(HD)))).astype(np.float32)
    ang = (np.arange(T, dtype=np.float32)[None, :] * inv[i % half][:, None]).astype(np.float32)
    c["cos"] = np.cos(ang)
    c["sin"] = np.where((i % HD < half)[:, None], -np.sin(ang), np.sin(ang))
    lg = np.log1p(-np.power(2.0, -5.0 - np.arange(8)))
    head = 2 * np.arange(4)[None, :] + row_head[:, None]
    c["xi"] = np.exp(lg[head][:, :, None] * (i[None, None, :] + 1.0))
    diff = i[None, :] - i[:, None]
    dm = np.where(diff >= 0, np.exp(lg[:, None, None] * np.maximum(diff, 0)), 0.0) * HD ** -0.5
    c["dmat"] = np.stack([dm[p::2].transpose(1, 0, 2) for p in range(2)], 1)
    c["zeta"] = np.exp(lg[None, :] * (P - 1.0 - i[:, None])) * HD ** -0.5
    c["cdecay"] = np.exp(lg[head] * P)
    same = (i[:, None] // CH) == (i[None, :] // CH)
    strict, incl = same & (diff > 0), same & (diff >= 0)
    c["rwmask"] = np.stack([strict, incl, strict, incl], 1)
    lev = [(i[:, None] // (2 * m) == i[None, :] // (2 * m)) & (i[:, None] % (2 * m) < m) & (i[None, :] % (2 * m) >= m)
           for m in (1, 2, 4, 8, 16, 32, 64)]
    c["lev"] = np.stack(lev[:6], 1)
    c["hgmask"] = np.stack(lev + [np.eye(P, dtype=bool)], 1).astype(np.uint32)
    t = np.arange(T)
    c["reset64"] = np.tile((t % CH != 0) * 1.0, (P, 1))
    c["reset128"] = np.tile((t % P != 0) * 1.0, (P, 1))
    si = np.arange(2 * P)
    rel = i[:, None] + P - si[None, :]
    ok = [(rel >= 0) & (rel < P) & (n * P + si[None, :] - P >= 0) for n in range(NT)]
    c["atmask"] = np.where(np.stack(ok, 1), 0.0, -1e30)
    win = np.array([[2, 4], [8, 16]])[:, row_head].T
    c["invcnt"] = 1.0 / np.minimum(t[None, None, :] + 1.0, win[:, :, None])
    c["causal"] = (diff >= 0) * 1.0
    return {k: np.ascontiguousarray(v if v.dtype == np.uint32 else v.astype(np.float32)) for k, v in c.items()}


KEEP = [("ident", (P,)), ("headones", (P,)), ("ones", (P,)), ("eps", (2,)), ("gains", (9, DC)), ("vec2", (V_N,))]
FIRST = [("hgmask", (8, P)), ("reset128", (T,)), ("invcnt", (2, T)), ("causal", (P,)), ("vec1", (U_N,)),
         ("wa", (2, P)), ("wx", (2, P)), ("dw", (2, P)), ("ws", (4, P)), ("lng", (2 * P,)), ("lnb", (2 * P,)),
         ("bs", (2, P))]
RWKV = [("w2", (4, P)), ("a2", (4, P)), ("g2", (4, P)), ("rwmask", (4, P)), ("lev", (6, P)), ("reset64", (T,))]
RETAT = [("swap", (P,)), ("cos", (T,)), ("sin", (T,)), ("xi", (4, P)), ("dmat", (2, 4, P)), ("zeta", (8,)), ("cdecay", (4,)),
         ("atmask", (NT, 2 * P))]


def build(nc, dram, out):
    ctx = ExitStack()
    with ctx:
        at = [16512]

        def place(name, shape, dt=F32, offset=None):
            n = 4 * int(np.prod(shape))
            if offset is None:
                offset = at[0]
                at[0] += (n + 31) // 32 * 32
            return nc.alloc_sbuf_tensor_at(name, [P, *shape], dt, offset=offset), offset

        x, _ = place("x", (DC, T))
        xg_hi, _ = place("xg_hi", (DC, T), F32R)
        xg_lo, _ = place("xg_lo", (DC, T), F32R)
        raw, _ = place("raw", (2, DC * P))
        w_hi, _ = place("w_hi", (2, DC * P), F32R)
        w_lo, _ = place("w_lo", (2, DC * P), F32R)
        rstd, _ = place("rstd", (T,))
        sumsq, _ = place("sumsq", (T,))
        K = {}
        for name, shape in KEEP:
            K[name], _ = place(name, shape)
        base = at[0]

        for name, shape in FIRST:
            K[name], _ = place(name, shape, U32 if name == "hgmask" else F32)
        z, _ = place("z", (18, T))
        y_hi, _ = place("y_hi", (DC, T), F32R)
        y_lo, _ = place("y_lo", (DC, T), F32R)
        m1 = {}
        for name, shape in (("ta", (2, T)), ("tb", (2, T)), ("tc", (2, T)), ("td", (2, T + 16)), ("te", (2, T)), ("tf", (2, T)),
                            ("tg", (2, T)), ("th", (2, T))):
            m1[name], _ = place("m1_" + name, shape)
        att, _ = place("att", (2, 2, 4, P))
        sml, _ = place("sml", (64,))
        S1, _ = place("S1", (2, P))
        assert at[0] <= 229376, at[0]

        at[0] = base
        for name, shape in RWKV:
            K[name], _ = place(name, shape)
        end = at[0]
        at[0] = base
        for name, shape in RETAT:
            K[name], _ = place(name, shape)
        at[0] = max(end, at[0])
        z_rw, rw_at = place("z_rw", (14, T))
        z_rt, rt_at = place("z_rt", (16, T))
        scratch = at[0]
        C4 = 4 * 4 * T
        y1_hi, _ = place("y1_hi", (4, T), F32R, offset=rw_at)
        y1_lo, _ = place("y1_lo", (4, T), F32R, offset=rw_at + C4)
        z_at, _ = place("z_at", (6, T), offset=rw_at + 2 * C4)
        y2_hi, _ = place("y2_hi", (4, T), F32R, offset=rt_at)
        y2_lo, _ = place("y2_lo", (4, T), F32R, offset=rt_at + C4)
        hid_hi, _ = place("hid_hi", (DC, T), F32R, offset=rt_at)
        hid_lo, _ = place("hid_lo", (DC, T), F32R, offset=rt_at + 2 * C4)
        emb_at = base + 24 * 1024
        emb_hi, _ = place("emb_hi", (2, T), F32R, offset=emb_at)
        emb_lo, _ = place("emb_lo", (2, T), F32R, offset=emb_at + C4 // 2)
        emb, _ = place("emb", (2, T), F32, offset=emb_at + C4)
        assert emb_at + 3 * C4 // 2 <= rt_at and base + 4 * sum(int(np.prod(shape)) for _, shape in FIRST) <= emb_at

        rw = {}
        for name, shape in (("AR", (4, 2, P)), ("bon", (4, P)), ("g", (4, P)), ("sq", (4, P)), ("tokB", (T,)),
                            ("tokK", (T,)), ("tokV", (T,)), ("W", (T,)), ("U", (T,)), ("S", (4, P)), ("th", (P,)),
                            ("sg", (P,)), ("pc", (4, 2))):
            rw[name], _ = place("rw_" + name, shape)
        lo_at, hi_at = at[0], at[0] + 2 * C4
        for k, name in enumerate(("kp", "b", "kk", "Lr", "Lp", "Dl", "eP", "eM")):
            rw[name], _ = place("rw_" + name, (4, P), offset=lo_at + 4 * T * k)
        rw["SC"], _ = place("rw_SC", (8, 4, P), offset=lo_at)
        for k, name in enumerate(("G", "X", "Y", "TL")):
            rw[name], _ = place("rw_" + name, (8, P), offset=hi_at + 4 * T * 2 * k)
        for k, name in enumerate(("BT", "KT", "BH", "KH", "VT")):
            rw[name], _ = place("rw_" + name, (4, P), offset=hi_at + 4 * T * (2 + k))
        assert hi_at + 2 * C4 <= 229376, hi_at

        at[0] = scratch
        mixed, _ = place("mixed", (DC, T))
        ffn = {}
        for name in ("sq", "t", "act", "h"):
            ffn[name], _ = place("ffn_" + name, (T,))
        mixer = at[0]
        for name, shape in (("pad", (2, T + 2)), ("cv", (2, T))):
            ffn[name], _ = place("ffn_" + name, shape)

        rstd_fin, sumsq_fin = ffn["cv"][:, 0, :], ffn["cv"][:, 1, :]
        at[0] = mixer
        rt = {}
        for name, shape in (("t1", (4, P)), ("t2", (4, P)), ("qr", (4, P)), ("kr", (4, P)), ("qx", (4, P)),
                            ("kz", (T,)), ("vt", (T,)), ("R", (4, P)), ("o", (4, P)), ("ST", (2, 4, P)), ("sq", (4, P)),
                            ("gs", (4, P))):
            rt[name], _ = place("rt_" + name, shape)
        assert at[0] <= 229376, at[0]

        at[0] = mixer
        an = {}
        for name, shape in (("sq", (5, P)), ("rs", (5, P)), ("q", (4, P)), ("k", (2, 2, P)), ("v", (2, P)), ("vf", (P,)),
                            ("s", (2, 4, 2 * P)), ("pT", (8, 2, P)), ("o", (4, P)), ("mx", (8,)), ("nm", (8,)),
                            ("sum", (8,)), ("es", (8,))):
            an[name], _ = place("an_" + name, shape)
        assert at[0] <= 229376, at[0]

        acc = [ctx.enter_context(nc.psum_tensor(f"acc{s}", [P, T], F32)) for s in range(2)]
        bank = [ctx.enter_context(nc.psum_tensor(f"bank{s}", [P, T], F32)) for s in range(6)]

        def sem(name):
            return ctx.enter_context(nc.semaphore(name))

        raw_in = [sem(f"raw_in{s}") for s in range(2)]
        w_split = [sem(f"w_split{s}") for s in range(2)]
        hi_done = [sem(f"hi_done{s}") for s in range(2)]
        slot_done = [sem(f"slot_done{s}") for s in range(2)]
        acc_free = [sem(f"acc_free{s}") for s in range(2)]
        keep_in, first_in, layer_in, retat_in = sem("keep_in"), sem("first_in"), sem("layer_in"), sem("retat_in")
        sumsq_ready, stat_ready, root_ready = sem("sumsq_ready"), sem("stat_ready"), sem("root_ready")
        xg_ready, hid_ready = sem("xg_ready"), sem("hid_ready")
        y_ready, x_in, squared = sem("y_ready"), [sem(f"x_in{c}") for c in range(DC)], sem("squared")
        h_pre, h_act = sem("h_pre"), sem("h_act")
        x_final, stored = sem("x_final"), sem("stored")
        pool_turn, act_turn, pe_turn, dve_turn = sem("pool_turn"), sem("act_turn"), sem("pe_turn"), sem("dve_turn")
        s1 = {n: sem("b1_" + n) for n in (
            "z", "vT", "iev", "act1", "vn", "wm", "sv", "conv", "ri", "sig", "la", "ea", "mlt", "scan", "hx", "hl", "lf", "lv",
            "ex", "qk", "sc", "scev", "kh", "khT", "khv", "o", "kv", "st", "on", "os", "osq", "pool", "dwy", "sqr",
            "gel", "sil")}
        s2 = {n: sem("rw_" + n) for n in (
            "z", "lora_in", "lora", "pre", "sig", "kkr", "nrm_in", "nrm", "rn", "root", "L", "exp", "ops", "tr", "tok",
            "sc", "scev", "g1", "x", "xev", "tl", "y", "yi", "xg", "xgev", "w", "wev", "u", "uev", "st", "stev", "yo",
            "ysb", "ysum", "yc", "ysq", "yvar", "yroot", "done")}
        s3 = {n: sem("rt_" + n) for n in (
            "z", "sw", "vf", "vT", "rot", "sc", "st", "ktr", "kz", "vt", "o", "rev", "osb", "osum", "root", "silu", "done")}
        s4 = {n: sem("an_" + n) for n in (
            "z", "vT", "sq", "ss", "root", "qk", "sc", "s", "mx", "p", "pn", "pT", "pTe", "o", "done", "dup")}
        o_gate, o_sig = sem("o_gate"), sem("o_sig")
        load_wait = 16

        def bc(ap, n):
            return ap.unsqueeze(2).to_broadcast([ap.shape[0], ap.shape[1], n])

        def mid(ap, n):
            return ap.unsqueeze(1).to_broadcast([ap.shape[0], n, ap.shape[1]])

        def r3(ap, k):
            return ap.rearrange("p (a b) -> p a b", a=k)

        def bits(ap):
            return ap.bitcast(F32)

        def tile_of(t, a, k, n):
            return t[:, a:a + k, bass.ts(n, P)]

        block = ctx.enter_context(nc.Block())

        @block.sync
        def _(sp):
            def load(pairs, names, I0, index=None, from_pair=0):
                def one(i):
                    for s in range(2):
                        src = dram[names[s]] if index is None else dram[names[s]][index]
                        n = src.shape[-1]
                        sp.wait_ge(w_split[s], I0 + i + 1)
                        sp.sem_inc(pe_turn, 1)
                        sp.dma_start(raw[:, s, 0:n], src[i + from_pair, s] if len(src.shape) == 4 else src[i + from_pair]).then_inc(raw_in[s], 16)
                with sp.Fori(0, pairs) as i:
                    one(i)

            for name, _ in KEEP[:-1]:
                sp.dma_start(K[name][:], dram[name]).then_inc(keep_in, 16)
            for c in range(DC):
                sp.dma_start(x[:, c, :], dram["x"][c]).then_inc(x_in[c], 16)
            I = 0
            load(2, ("w1_in", "w1_in"), I)
            for name, _ in FIRST:
                sp.dma_start(K[name][:], dram[name]).then_inc(first_in, 16)
            load(B1_IN - 2, ("w1_in", "w1_in"), I + 2, from_pair=2); I += B1_IN
            load(X_OUT, ("w1_out", "w1_out"), I); I += X_OUT
            for k, n in enumerate(PARTS):
                load(n, (f"w1_up{k}",) * 2, I); I += n
                load(X_OUT, (f"w1_down{k}",) * 2, I); I += X_OUT
            sp.dma_start(emb[:], dram["p"]).then_inc(first_in, 16)
            load(PE_PAIRS, ("w1_pg", "w1_pe"), I); I += PE_PAIRS
            with sp.Fori(0, LAYERS) as l:
                I = B1_PAIRS + l * LAYER_PAIRS
                sp.dma_start(K["vec2"][:], dram["vec2"][l]).then_inc(layer_in, 16)
                for name, _ in RWKV:
                    sp.dma_start(K[name][:], dram[name][l] if len(dram[name].shape) > 1 + len(dict(RWKV)[name]) else dram[name]).then_inc(layer_in, 16)
                for n, name in ((RW_PAIRS, "w2_rw"), (RET_PAIRS, "w2_ret"), (AT_PAIRS, "w2_at")):
                    load(n, (name, name), I, l); I = I + n
                sp.wait_ge(s2["done"], l * NT + NT)
                sp.sem_inc(pe_turn, 1)
                for name, _ in RETAT:
                    sp.dma_start(K[name][:], dram[name]).then_inc(retat_in, 16)
                load(O_PAIRS, ("w2_gate", "w2_o"), I, l); I = I + O_PAIRS
                load(X_OUT, ("w2_out", "w2_out"), I, l); I = I + X_OUT
                for k, n in enumerate(PARTS):
                    load(n, (f"w2_up{k}",) * 2, I, l); I = I + n
                    load(X_OUT, (f"w2_down{k}",) * 2, I, l); I = I + X_OUT
            for c in range(DC):
                sp.wait_ge(x_final, DC * (LAYERS - 1) + c + 1)
                sp.dma_start(out[c], x[:, c, :]).then_inc(stored, 16)
            sp.wait_ge(stored, 16 * DC)

        @block.gpsimd
        def _(pool):
            for s in range(2):
                pool.sem_inc(w_split[s], 1)

            def split(pairs, widths, I0):
                with pool.Fori(0, pairs) as i:
                    for s in range(2):
                        n = widths[s] * P
                        pool.wait_ge(raw_in[s], 16 * (I0 + i + 1))
                        pool.wait_ge(hi_done[s], I0 + i + 1)
                        pool.sem_inc(pool_turn, 1)
                        nc.gpsimd.tensor_scalar(w_hi[:, s, 0:n], raw[:, s, 0:n], 1.0, 0.0, ALU.mult, ALU.add)
                        pool.wait_ge(slot_done[s], I0 + i + 1)
                        pool.sem_inc(pool_turn, 1)
                        pool.drain()
                        nc.gpsimd.tensor_tensor(w_lo[:, s, 0:n], raw[:, s, 0:n], bits(w_hi[:, s, 0:n]),
                                                ALU.subtract).then_inc(w_split[s], 1)

            def ffn_split(I):
                for n in PARTS:
                    split(n, (DC, DC), I); I = I + n
                    split(X_OUT, (n, n), I); I = I + X_OUT
                return I

            split(B1_IN + X_OUT, (DC, DC), 0)
            I = ffn_split(B1_IN + X_OUT)
            split(PE_PAIRS, (DC, 2), I)
            with pool.Fori(0, LAYERS) as l:
                I = B1_PAIRS + l * LAYER_PAIRS
                split(RW_PAIRS + RET_PAIRS + AT_PAIRS, (DC, DC), I); I = I + RW_PAIRS + RET_PAIRS + AT_PAIRS
                split(O_PAIRS, (DC, 4), I); I = I + O_PAIRS
                split(X_OUT, (DC, DC), I); I = I + X_OUT
                ffn_split(I)

        @block.tensor
        def _(pe):
            for s in range(2):
                pe.sem_inc(slot_done[s], 1)
                pe.sem_inc(hi_done[s], 1)

            def mm(o, a, b, first, last, shared=False):
                return nc.tensor.matmul(o, a, b, start=first, stop=last, skip_group_check=shared)

            def slot(s, I, a, chunks):
                hi, lo = a
                pe.wait_ge(w_split[s], I + 2)
                pe.wait_ge(acc_free[s], I + 1)
                pe.sem_inc(pe_turn, 1)
                n = len(chunks)
                for m, v in ((0, hi), (0, lo), (1, hi)):
                    w = (w_hi, w_lo)[m]
                    for k, c in enumerate(chunks):
                        last = mm(acc[s][:], w[:, s, k * P:(k + 1) * P], v[:, c, :], v is hi and m == 0 and k == 0, m == 1 and k == n - 1)
                    if v is lo:
                        last.then_inc(hi_done[s], 1)
                last.then_inc(slot_done[s], 1)

            def late(s, I, a, chunks, ready, count, order=None):
                pe.wait_ge(w_split[s], I + 2)
                pe.wait_ge(acc_free[s], I + 1)
                pe.sem_inc(pe_turn, 1)
                n = len(chunks)
                for i, k in enumerate(order or range(n)):
                    w, c = slice(k * P, (k + 1) * P), chunks[k]
                    pe.wait_ge(ready, count + i + 1)
                    pe.sem_inc(pe_turn, 1)
                    mm(acc[s][:], w_hi[:, s, w], a[0][:, c, :], i == 0, False)
                    last_hi = mm(acc[s][:], w_hi[:, s, w], a[1][:, c, :], False, False)
                    last = mm(acc[s][:], w_lo[:, s, w], a[0][:, c, :], False, i == n - 1)
                last_hi.then_inc(hi_done[s], 1)
                last.then_inc(slot_done[s], 1)

            def normed(pairs, I, count, stat):
                late(0, I, xg, full, xg_ready, count)
                stats(stat)
                slot(1, I, xg, full)
                slots(pairs - 1, I + 1, xg, full)

            def hid_slots(I, n, count):
                late(0, I, hid, range(n), hid_ready, count)
                slot(1, I, hid, range(n))
                slots(X_OUT - 1, I + 1, hid, range(n))

            def slots(pairs, I0, a, chunks):
                with pe.Fori(0, pairs) as i:
                    for s in range(2):
                        slot(s, I0 + i, a, chunks)

            xg, hid, yy, em = (xg_hi, xg_lo), (hid_hi, hid_lo), (y_hi, y_lo), (emb_hi, emb_lo)
            y1, y2, four = (y1_hi, y1_lo), (y2_hi, y2_lo), range(4)
            full = range(DC)

            def stats(count):
                pe.wait_ge(sumsq_ready, count)
                pe.sem_inc(pe_turn, 1)
                mm(bank[5][:], K["ones"][:], sumsq[:], True, True).then_inc(stat_ready, 1)

            def feed_forward(I, hid0, xg0, stat):
                for k, n in enumerate(PARTS):
                    if k == 0:
                        normed(n, I, xg0, stat)
                    else:
                        slots(n, I, xg, full)
                    I = I + n
                    hid_slots(I, n, hid0 + sum(PARTS[:k])); I = I + X_OUT
                return I

            def head_sums(o, v):
                return mm(o, K["headones"][:], v, True, True)

            pe.wait_ge(keep_in, load_wait * (len(KEEP) - 1))
            late(0, 0, xg, full, xg_ready, 0)
            stats(1)
            slot(1, 0, xg, full)

            def pair(i):
                for s in range(2):
                    slot(s, i, xg, full)

            def transposed(b, src):
                for n in range(NT):
                    for c in range(2):
                        last = nc.tensor.transpose(bank[b + n // 2][:, (2 * (n % 2) + c) * P:(2 * (n % 2) + c + 1) * P],
                                                   src[:, c, n * P:(n + 1) * P], K["ident"][:])
                last.then_inc(s1["vT"], 1)

            pair(1)
            pair(2)
            pe.wait_ge(first_in, load_wait * len(FIRST))
            pe.wait_ge(s1["conv"], 1)
            for k, name in enumerate(("wa", "wx")):
                for j in range(2):
                    last = mm(bank[2 + 2 * k + j][:], K[name][:, j, :], m1["ta"][:, j, :], True, True)
            last.then_inc(s1["ri"], 1)
            pair(3)
            pe.wait_ge(s1["z"], 3)
            transposed(0, m1["tg"])
            pair(4)
            pe.wait_ge(s1["vn"], 1)
            pe.wait_ge(s1["wm"], 1)
            vtok = z[:, 14:16, :].rearrange("p a b -> p (a b)").rearrange("p (n c) -> p n c", n=NT)
            for j in range(2):
                for n in range(NT):
                    for p in range(2):
                        h = 2 * j + p
                        last = mm(bank[j][p * HD:(p + 1) * HD, n * P:(n + 1) * P], vtok[:, n, h * HD:(h + 1) * HD],
                                  K["ws"][:, h, :], True, True)
            last.then_inc(s1["sv"], 1)
            pair(5)
            pair(6)
            pe.wait_ge(s1["z"], 7)
            pe.wait_ge(s1["sig"], 1)
            transposed(4, m1["th"])
            pair(7)
            pair(8)
            count = 0
            for lev in range(8):
                pe.wait_ge(s1["qk"], lev + 1)
                for half in range(2):
                    if count >= 2:
                        pe.wait_ge(s1["scev"], count - 1)
                    elif count == 0:
                        pe.wait_ge(s1["gel"], 1)
                    for p in range(2):
                        for tile in range(2):
                            for j in range(2):
                                sl = slice((2 * half + tile) * P, (2 * half + tile + 1) * P)
                                r = slice(p * HD, (p + 1) * HD)
                                kk, qq = (m1[("tc", "th")[lev % 2]], m1[("tb", "tg")[lev % 2]]) if lev < 7 else (m1["te"], z[:, 6:8, :])
                                last = mm(bank[2 * (count % 2) + p][:, (2 * tile + j) * P:(2 * tile + j + 1) * P],
                                          kk[r, j, sl], qq[r, j, sl], True, True)
                    last.then_inc(s1["sc"], 1)
                    count += 1
            pe.wait_ge(s1["kh"], 1)
            pe.wait_ge(s1["scev"], 16)
            for n in range(NT):
                for j in range(2):
                    o = bank[n // 2][:, (2 * (n % 2) + j) * P:(2 * (n % 2) + j + 1) * P]
                    last = nc.tensor.transpose(o, m1["tb"][:, j, n * P:(n + 1) * P], K["ident"][:])
            last.then_inc(s1["khT"], 1)
            pe.wait_ge(s1["khv"], 1)
            pe.wait_ge(s1["iev"], 1)
            itok = z[:, 16:18, :].rearrange("p (s t) c -> p s (t c)", s=1)[:, 0, :].rearrange("p (n c) -> p n c", n=NT)
            khtok = m1["tc"][:].rearrange("p (s t) c -> p s (t c)", s=1)[:, 0, :].rearrange("p (n c) -> p n c", n=NT)
            for n in range(NT):
                if n == 1:
                    pe.wait_ge(s1["pool"], 1)
                    for j in range(2):
                        last = mm(bank[4 + j][:], K["dw"][:, j, :], m1["th"][:, j, :], True, True)
                    last.then_inc(s1["dwy"], 1)
                pe.wait_ge(s1["st"], n + 1)
                for j in range(2):
                    sl = slice(n * P, (n + 1) * P)
                    mm(bank[2 + j][:, sl], S1[:, j, :], m1["tf"][:, j, sl], n == 0, False, True)
                    for p in range(2):
                        h = 2 * j + p
                        last = mm(bank[2 + j][p * HD:(p + 1) * HD, sl], itok[:, n, h * HD:(h + 1) * HD],
                                  att[:, n // 2, p, 2 * (n % 2) + j, :], False, True, True)
                for j in range(2):
                    last = mm(bank[n % 2][:, j * P:(j + 1) * P], khtok[:, n, j * P:(j + 1) * P],
                              itok[:, n, j * P:(j + 1) * P], True, True)
                last.then_inc(s1["kv"], 1)
            pe.wait_ge(s1["osq"], 1)
            for j in range(2):
                last = head_sums(bank[j][:], m1["ta"][:, j, :])
            last.then_inc(s1["on"], 1)
            late(0, B1_IN, yy, full, y_ready, 0, (0, 1, 2, 3, 6, 7, 4, 5))
            slot(1, B1_IN, yy, full)
            slots(X_OUT - 1, B1_IN + 1, yy, full)
            I = feed_forward(B1_IN + X_OUT, 0, DC, 2)
            late(0, I, xg, full, xg_ready, 2 * DC)
            stats(3)
            slot(1, I, em, range(2))
            with pe.Fori(1, PE_PAIRS) as i:
                slot(0, I + i, xg, full)
                slot(1, I + i, em, range(2))
            stats(4)
            with pe.Fori(0, LAYERS) as l:
                I = B1_PAIRS + l * LAYER_PAIRS
                normed(RW_PAIRS, I, DC * (2 * l + 3), 2 * l + 5); I = I + RW_PAIRS
                pe.wait_ge(layer_in, load_wait * (1 + len(RWKV)) * (l + 1))
                pe.sem_inc(pe_turn, 1)
                with pe.Fori(0, NT) as n:
                    it, F = l * NT + n, I + 2 * n

                    def after(name, k, per=1):
                        pe.wait_ge(s2[name], it * per + k)
                        pe.sem_inc(pe_turn, 1)

                    slot(0, F, xg, full)
                    after("lora_in", 1)
                    for j in range(4):
                        mm(bank[0][:, j * P:(j + 1) * P], K["w2"][:, j, :], rw["th"][:], True, True)
                        mm(bank[1][:, j * P:(j + 1) * P], K["a2"][:, j, :], rw["th"][:], True, True)
                        last = mm(bank[2][:, j * P:(j + 1) * P], K["g2"][:, j, :], rw["sg"][:], True, True)
                    last.then_inc(s2["lora"], 1)
                    slot(1, F, xg, full)
                    slot(0, F + 1, xg, full)
                    after("nrm_in", 1)
                    head_sums(bank[0][:], rw["sq"][:].rearrange("p a b -> p (a b)"))
                    head_sums(bank[1][:], rw["bon"][:].rearrange("p a b -> p (a b)")).then_inc(s2["nrm"], 1)
                    slot(1, F + 1, xg, full)
                    after("ops", 1)
                    for src, b in (("BH", 0), ("KH", 1), ("VT", 2)):
                        for j in range(4):
                            last = nc.tensor.transpose(bank[b][:, j * P:(j + 1) * P], rw[src][:, j, :], K["ident"][:])
                    last.then_inc(s2["tr"], 1)
                    for h in range(8):
                        j, p = h // 2, h % 2
                        r = slice(p * HD, (p + 1) * HD)
                        b = bank[3 + p]
                        if h >= 2:
                            after("scev", h - 1, 8)
                        ar = rw["AR"][r, j, :, :].rearrange("p a b -> p (a b)")
                        mm(b[:, 0:2 * P], rw["BT"][r, j, :], ar, True, True)
                        mm(b[:, 2 * P:4 * P], rw["KT"][r, j, :], ar, True, True).then_inc(s2["sc"], 1)
                    after("g1", 1)
                    after("tok", 1)
                    for h in range(8):
                        last = nc.tensor.transpose(bank[h // 4][:, (h % 4) * P:(h % 4 + 1) * P], rw["G"][:, h, :], K["ident"][:])
                        if h % 4 == 3:
                            last.then_inc(s2["x"], 1)
                    for lev in range(1, 6):
                        after("tl", lev, 5)
                        for half in range(2):
                            if lev == 1:
                                after("xev", half + 1, 2)
                            else:
                                after("xgev", 2 * (lev - 2) + half + 1, 10)
                            for h in range(4 * half, 4 * half + 4):
                                last = mm(bank[3 + half][:, (h % 4) * P:(h % 4 + 1) * P], rw["TL"][:, h, :], rw["X"][:, h, :], True, True)
                            last.then_inc(s2["y"], 1)
                        for half in range(2):
                            after("yi", 2 * (lev - 1) + half + 1, 10)
                            for h in range(4 * half, 4 * half + 4):
                                c = slice((h % 4) * P, (h % 4 + 1) * P)
                                if lev < 5:
                                    mm(bank[half][:, c], rw["G"][:, h, :], rw["Y"][:, h, :], True, True)
                                last = mm(bank[(2, 5)[half]][:, c], rw["Y"][:, h, :], rw["G"][:, h, :], True, True)
                            last.then_inc(s2["xg"], 1)
                    after("xgev", 10, 10)
                    for c in range(2):
                        cs = slice(c * CH, (c + 1) * CH)
                        after("stev", c + 1, 3)
                        for j in range(4):
                            mm(bank[3][cs, j * P:(j + 1) * P], rw["AR"][:, j, 0, cs], rw["S"][:, j, :], j == 0, False, True)
                        for h in range(8):
                            last = mm(bank[3][cs, h * HD:(h + 1) * HD], rw["SC"][:, h, 2, cs], rw["tokV"][:, h * HD:(h + 1) * HD],
                                      False, h == 7, True)
                        last.then_inc(s2["w"], 1)
                        after("wev", c + 1, 2)
                        for h in range(8):
                            last = mm(bank[4][cs, h * HD:(h + 1) * HD], rw["G"][:, h, cs], rw["W"][:, h * HD:(h + 1) * HD],
                                      True, True)
                        last.then_inc(s2["u"], 1)
                        for j in range(4):
                            mm(bank[0][:, j * P + c * CH:j * P + (c + 1) * CH], rw["S"][:, j, :], rw["AR"][:, j, 1, cs],
                               c == 0 and j == 0, False, True)
                        after("uev", c + 1, 2)
                        for j in range(4):
                            js = slice(j * P, (j + 1) * P)
                            mm(bank[1][:, js], rw["tokB"][cs, js], rw["U"][cs, js], True, False)
                            last = mm(bank[1][:, js], rw["tokK"][cs, js], rw["tokV"][cs, js], False, True)
                        last.then_inc(s2["st"], 1)
                    for h in range(8):
                        j, p = h // 2, h % 2
                        o = bank[0][p * HD:(p + 1) * HD, j * P:(j + 1) * P]
                        mm(o, rw["U"][:, h * HD:(h + 1) * HD], rw["SC"][:, h, 1, :], False, False, True)
                        last = mm(o, rw["tokV"][:, h * HD:(h + 1) * HD], rw["SC"][:, h, 3, :], False, h == 7, True)
                    last.then_inc(s2["yo"], 1)
                    after("ysb", 1)
                    head_sums(bank[2][:], rw["W"][:]).then_inc(s2["ysum"], 1)
                    after("ysq", 1)
                    head_sums(bank[5][:], rw["sq"][:].rearrange("p a b -> p (a b)")).then_inc(s2["yvar"], 1)
                I = I + RET_PAIRS
                slots(AT_PAIRS, I, xg, full); I = I + AT_PAIRS
                pe.wait_ge(s2["done"], l * NT + NT)
                pe.sem_inc(pe_turn, 1)
                pe.wait_ge(retat_in, load_wait * len(RETAT) * (l + 1))
                pe.sem_inc(pe_turn, 1)
                with pe.Fori(0, NT) as n:
                    it, F = l * NT + n, I + 2 * n

                    def after(name, k, per=1):
                        pe.wait_ge(s3[name], it * per + k)
                        pe.sem_inc(pe_turn, 1)

                    pe.wait_ge(s3["z"], l + 1)
                    after("rev", 1, 2)
                    mm(bank[0][:], K["swap"][:], tile_of(z_rt, 0, 4, n), True, True)
                    mm(bank[1][:], K["swap"][:], tile_of(z_rt, 4, 4, n), True, True).then_inc(s3["sw"], 1)
                    after("vf", 1)
                    for j in range(4):
                        last = nc.tensor.transpose(bank[5][:, j * P:(j + 1) * P], rt["o"][:, j, :], K["ident"][:])
                    last.then_inc(s3["vT"], 1)
                    slot(0, F, xg, full)
                    after("rot", 1)
                    for p in range(2):
                        r = slice(p * HD, (p + 1) * HD)
                        for j in range(4):
                            mm(bank[2 + p][:, j * P:(j + 1) * P], rt["kr"][r, j, :], rt["qr"][r, j, :], True, True)
                    for j in range(4):
                        last = nc.tensor.transpose(bank[4][:, j * P:(j + 1) * P], rt["kr"][:, j, :], K["ident"][:])
                    last.then_inc(s3["sc"], 1)
                    slot(1, F, y1, four)
                    after("kz", 1)
                    after("vt", 1)
                    for j in range(4):
                        js = slice(j * P, (j + 1) * P)
                        mm(bank[0][:, js], rt["R"][:, j, :], rt["qx"][:, j, :], j == 0, False, True)
                    for h in range(8):
                        j, p = h // 2, h % 2
                        mm(bank[0][p * HD:(p + 1) * HD, j * P:(j + 1) * P], rt["vt"][:, h * HD:(h + 1) * HD],
                           rt["ST"][:, p, j, :], False, h == 7, True)
                    for j in range(4):
                        js = slice(j * P, (j + 1) * P)
                        last = mm(bank[1][:, js], rt["kz"][:, js], rt["vt"][:, js], True, True)
                    last.then_inc(s3["o"], 1)
                    after("osb", 1)
                    head_sums(bank[5][:], rt["sq"][:].rearrange("p a b -> p (a b)")).then_inc(s3["osum"], 1)
                    slot(0, F + 1, xg, full)
                    slot(1, F + 1, y1, four)
                I = I + 2 * NT
                pe.wait_ge(s3["done"], l * NT + NT)
                pe.sem_inc(pe_turn, 1)
                with pe.Fori(0, NT) as n:
                    it, F = l * NT + n, I + 2 * n

                    def after(name, k, per=1):
                        pe.wait_ge(s4[name], it * per + k)
                        pe.sem_inc(pe_turn, 1)

                    after("sq", 1)
                    head_sums(bank[0][:], an["sq"][:, 0:4, :].rearrange("p a b -> p (a b)"))
                    head_sums(bank[1][:, 0:P], an["sq"][:, 4, :]).then_inc(s4["ss"], 1)
                    nc.tensor.transpose(bank[5][:, 0:P], an["vf"][:], K["ident"][:]).then_inc(s4["vT"], 1)
                    slot(0, F, xg, full)
                    after("qk", 1)
                    after("dup", 1)
                    for p in range(2):
                        r = slice(p * HD, (p + 1) * HD)
                        for j in range(4):
                            last = mm(bank[2 * p + j // 2][:, (j % 2) * 2 * P:(j % 2 + 1) * 2 * P], an["q"][r, j, :],
                                      an["k"][r, j // 2, :, :].rearrange("p a b -> p (a b)"), True, True)
                    last.then_inc(s4["sc"], 1)
                    slot(1, F, y2, four)
                    slot(0, F + 1, xg, full)
                    after("pn", 1)
                    for h in range(8):
                        j, p = h // 2, h % 2
                        for b in range(2):
                            last = nc.tensor.transpose(bank[h // 2][:, (2 * p + b) * P:(2 * p + b + 1) * P],
                                                       an["s"][:, p, j, b * P:(b + 1) * P], K["ident"][:])
                    last.then_inc(s4["pT"], 1)
                    slot(1, F + 1, y2, four)
                    after("pTe", 1)
                    for h in range(8):
                        j, p = h // 2, h % 2
                        kv = h // 4
                        for b in range(2):
                            last = mm(bank[4][p * HD:(p + 1) * HD, j * P:(j + 1) * P], an["v"][:, b, kv * HD:(kv + 1) * HD],
                                      an["pT"][:, h, b, :], b == 0, b == 1)
                    last.then_inc(s4["o"], 1)
                I = I + 2 * NT
                pe.wait_ge(s4["done"], l * NT + NT)
                pe.sem_inc(pe_turn, 1)
                with pe.Fori(0, DC) as j:
                    slot(0, I + j, xg, full)
                    slot(1, I + j, y1, four)
                I = I + DC
                hid0 = FFC + l * (DC + FFC)
                hid_slots(I, DC, hid0); I = I + X_OUT
                feed_forward(I, hid0 + DC, DC * (2 * l + 4), 2 * l + 6)

        @block.vector
        def _(dve):
            v = nc.vector
            for s in range(2):
                dve.sem_inc(acc_free[s], 1)

            def tt(o, a, b, op=ALU.mult):
                return v.tensor_tensor(o, a, b, op)

            def done(s, I):
                dve.wait_ge(slot_done[s], I + 2)

            def splitted(hi, lo, src):
                v.tensor_copy(hi, src)
                dve.drain()
                return tt(lo, src, bits(hi), ALU.subtract)

            def norm_chunk(j, gain):
                v.tensor_scalar(ffn["t"][:], x[:, j, :], gain, None, ALU.mult)
                tt(ffn["sq"][:], x[:, j, :], x[:, j, :])
                dve.drain()
                v.tensor_copy(xg_hi[:, j, :], ffn["t"][:])
                tt(sumsq[:], sumsq[:], ffn["sq"][:], ALU.add)
                dve.drain()
                tt(xg_lo[:, j, :], ffn["t"][:], bits(xg_hi[:, j, :]), ALU.subtract).then_inc(xg_ready, 1)

            def gain_of(g, j):
                return K["gains"][:, g, bass.ds(j, 1)]

            def norm_end(count_root):
                dve.drain()
                dve.sem_inc(sumsq_ready, 1)
                dve.wait_ge(root_ready, count_root)
                dve.sem_inc(dve_turn, 1)

            def add_to_x(I0, gain=None, final=False):
                if gain is not None:
                    v.memset(sumsq[:], 0.0)
                    dve.drain()
                with dve.Fori(0, X_OUT) as i:
                    for s in range(2):
                        j = 2 * i + s
                        done(s, I0 + i)
                        tt(x[:, j, :], x[:, j, :], acc[s][:], ALU.add).then_inc(acc_free[s], 1)
                        dve.drain()
                        if final:
                            dve.sem_inc(x_final, 1)
                        if gain is not None:
                            norm_chunk(j, gain_of(gain, j))

            def scaled(s, I, dst):
                done(s, I)
                return tt(dst, acc[s][:], rstd[:])

            def hidden(j, gate, val):
                tt(ffn["h"][:], gate, val)
                dve.drain()
                splitted(hid_hi[:, j, :], hid_lo[:, j, :], ffn["h"][:]).then_inc(hid_ready, 1)

            def swiglu(I, pre0, gain):
                for k, n in enumerate(PARTS):
                    with dve.Fori(0, n) as i:
                        scaled(0, I + i, ffn["t"][:]).then_inc(acc_free[0], 1)
                        dve.drain()
                        dve.sem_inc(h_pre, 1)
                        scaled(1, I + i, ffn["sq"][:]).then_inc(acc_free[1], 1)
                        dve.drain()
                        dve.wait_ge(h_act, pre0 + i + 1)
                        hidden(i, ffn["act"][:], ffn["sq"][:])
                    I, pre0 = I + n, pre0 + n
                    dve.drain()
                    last = k == len(PARTS) - 1
                    add_to_x(I, gain if last else None, last); I = I + X_OUT
                return I

            def ms(ap, val=0.0):
                return v.memset(ap, val)

            ms(sumsq[:])
            dve.wait_ge(keep_in, load_wait * (len(KEEP) - 1))
            dve.drain()
            for c in range(DC):
                dve.wait_ge(x_in[c], load_wait)
                v.tensor_scalar(ffn["t"][:], x[:, c, :], K["gains"][:, G_N1, c:c + 1], None, ALU.mult)
                dve.drain()
                splitted(xg_hi[:, c, :], xg_lo[:, c, :], ffn["t"][:]).then_inc(xg_ready, 1)
                dve.wait_ge(squared, c + 1)
                tt(sumsq[:], sumsq[:], mixed[:, c, :], ALU.add)
                dve.drain()
            norm_end(1)
            ms(S1[:])
            ms(m1["td"][:])
            ms(att[:])
            dve.wait_ge(first_in, load_wait * len(FIRST))

            def take(i, dst):
                for s in range(2):
                    scaled(s, i, dst[:, s, :]).then_inc(acc_free[s], 1)
                dve.drain()
                dve.sem_inc(s1["z"], 1)

            take(0, z[:, 2:4, :])
            vtok = z[:, 14:16, :].rearrange("p (s t) c -> p s (t c)", s=1)[:, 0, :].rearrange("p (n c) -> p n c", n=NT)
            itok = z[:, 16:18, :].rearrange("p (s t) c -> p s (t c)", s=1)[:, 0, :].rearrange("p (n c) -> p n c", n=NT)
            khtok = m1["tc"][:].rearrange("p (s t) c -> p s (t c)", s=1)[:, 0, :].rearrange("p (n c) -> p n c", n=NT)
            vec = K["vec1"]

            def col(k):
                return vec[:, k:k + 1]

            for j in range(2):
                v.tensor_copy(m1["td"][:, j, 16:], z[:, 2 + j, :])
            dve.drain()
            for j in range(2):
                v.tensor_scalar(m1["ta"][:, j, :], m1["td"][:, j, 16:16 + T], col(U_CW + 4 * j + 3), col(U_CB + j), ALU.mult, ALU.add)
            dve.drain()
            for k in range(3):
                for j in range(2):
                    v.scalar_tensor_tensor(m1["ta"][:, j, :], m1["td"][:, j, 13 + k:13 + k + T], col(U_CW + 4 * j + k),
                                           m1["ta"][:, j, :], ALU.mult, ALU.add)
                dve.drain()
            dve.sem_inc(s1["conv"], 1)
            lam, lp = vec[:, U_LAM:U_LAM + 2], [sml[:, 8 + 2 * k:10 + 2 * k] for k in range(8)]
            v.tensor_scalar(lp[0], lam, -1.0, 0.0, ALU.mult, ALU.max)
            v.tensor_scalar(lp[1], lam, -1.0, None, ALU.mult)
            dve.drain()
            tt(lp[1], lp[1], lam, ALU.min)
            dve.drain()
            dve.sem_inc(s1["la"], 1)
            take(1, z[:, 4:6, :])
            tt(K["ws"][:], K["ws"][:], mid(K["causal"][:], 4)).then_inc(s1["wm"], 1)
            dve.wait_ge(s1["ea"], 1)
            v.tensor_scalar(lp[3], lp[2], 2.0, None, ALU.add)
            dve.drain()
            v.reciprocal(lp[3], lp[3])
            dve.drain()
            tt(lp[3], lp[3], lp[2])
            dve.drain()
            tt(lp[4], lp[3], lp[3])
            ms(lp[5], 1.0 / 19)
            dve.drain()
            for k in range(17, 0, -2):
                tt(lp[5], lp[5], lp[4])
                dve.drain()
                v.tensor_scalar(lp[5], lp[5], 1.0 / k, None, ALU.add)
                dve.drain()
            tt(lp[5], lp[5], lp[3])
            dve.drain()
            v.scalar_tensor_tensor(lp[0], lp[5], 2.0, lp[0], ALU.mult, ALU.add)
            dve.drain()
            v.tensor_scalar(lp[0], lp[0], 8.0, None, ALU.mult)
            take(2, m1["tg"])
            dve.wait_ge(s1["sig"], 1)
            for j in range(2):
                v.tensor_scalar(z[:, 2 + j, :], z[:, 2 + j, :], lp[0][:, j:j + 1], None, ALU.mult)
            tt(m1["ta"][:], m1["ta"][:], m1["te"][:])
            dve.drain()
            dve.sem_inc(s1["mlt"], 1)
            take(3, z[:, 0:2, :])
            dve.wait_ge(s1["act1"], 2)
            st = sml[:, 24:48].rearrange("p (n c) -> p n c", n=NT)
            ag = sml[:, 48:56].rearrange("p (n c) -> p n c", n=NT)
            for n in range(NT):
                v.bn_stats(st[:, n, :], vtok[:, n, :])
            dve.drain()
            for n in range(NT):
                v.bn_aggr(ag[:, n, :], st[:, n, :])
            dve.drain()
            dve.sem_inc(s1["lv"], 1)
            dve.wait_ge(s1["scan"], 1)
            tt(m1["tb"][:], m1["tb"][:], m1["td"][:, :, 0:T])
            dve.drain()
            dve.sem_inc(s1["hx"], 1)
            dve.wait_ge(s1["sqr"], 1)
            for n in range(NT):
                v.tensor_scalar(vtok[:, n, :], vtok[:, n, :], ag[:, n, 0:1], sml[:, n:n + 1], ALU.subtract, ALU.mult)
            dve.drain()
            tt(vtok, vtok, mid(K["lng"][:], NT))
            dve.drain()
            tt(vtok, vtok, mid(K["lnb"][:], NT), ALU.add)
            dve.drain()
            dve.sem_inc(s1["vn"], 1)
            take(4, z[:, 8:10, :])
            zf = z[:, 8:10, :]
            v.scalar_tensor_tensor(m1["tf"][:], zf, -1.0, zf, ALU.mult, ALU.min)
            dve.drain()
            dve.sem_inc(s1["lf"], 1)
            dve.wait_ge(s1["hl"], 1)
            tt(m1["ta"][:], m1["ta"][:], m1["tb"][:])
            dve.drain()
            for j in range(2):
                v.tensor_tensor_scan(m1["tb"][:, j, :], m1["tc"][:, j, :], m1["ta"][:, j, :], 0.0, ALU.mult, ALU.add)
            dve.drain()
            tt(m1["tb"][:], m1["tb"][:], z[:, 4:6, :])
            dve.drain()
            for j in range(2):
                splitted(y_hi[:, 2 + j, :], y_lo[:, 2 + j, :], m1["tb"][:, j, :])
            dve.wait_ge(s1["sil"], 1)
            v.scalar_tensor_tensor(m1["ta"][:], zf, 0.0, m1["tf"][:], ALU.min, ALU.subtract)
            dve.drain()
            lf = m1["td"][:, :, 0:T]
            for j in range(2):
                v.tensor_tensor_scan(lf[:, j, :], K["reset128"][:], m1["ta"][:, j, :], 0.0, ALU.mult, ALU.add)
            take(5, z[:, 6:8, :])
            dve.wait_ge(s1["act1"], 3)
            dve.wait_ge(s1["sv"], 1)
            for j in range(2):
                tt(r3(m1["tg"][:, j, :], NT), r3(bank[j][:], NT), mid(K["bs"][:, j, :], NT), ALU.add)
            dve.drain()
            dve.sem_inc(s1["gel"], 1)
            for j in range(2):
                tt(m1["tg"][:, j, :], m1["tg"][:, j, :], z[:, j, :])
            dve.drain()
            for j in range(2):
                splitted(y_hi[:, j, :], y_lo[:, j, :], m1["tg"][:, j, :])
            dve.drain()
            dve.sem_inc(y_ready, 4)
            take(6, m1["th"])
            def decays(lev):
                m, e = 1 << lev, m1[("ta", "tf")[lev % 2]]
                for j in range(2):
                    lj = lf[:, j, :].rearrange("p (b m) -> p b m", m=2 * m)
                    tt(e[:, j, :].rearrange("p (b m) -> p b m", m=2 * m), lj, lj[:, :, m - 1:m].to_broadcast([P, T // (2 * m), 2 * m]), ALU.subtract)
                dve.drain()
                v.scalar_tensor_tensor(e[:], e[:], -1.0, e[:], ALU.mult, ALU.min)
                dve.drain()
                dve.sem_inc(s1["ex"], 1)

            def decayed(lev):
                m, e, k = 1 << lev, m1[("ta", "tf")[lev % 2]], lev % 2
                for second, dst, src in ((1, ("tb", "tg")[k], z[:, 6:8, :]), (0, ("tc", "th")[k], m1["te"][:])):
                    o, a, b = m1[dst][:], e[:], src
                    if lev >= 2:
                        o, a, b = (t.rearrange("p j (b s m) -> p (j b) s m", s=2, m=m)[:, :, second, :] for t in (o, a, b))
                    tt(o, a, b)
                dve.drain()

            def chosen(lev):
                for half in range(2):
                    dve.wait_ge(s1["sc"], 2 * lev + half + 1)
                    for p in range(2):
                        v.copy_predicated(att[:, half, p], mid(K["hgmask"][:, lev, :], 4), r3(bank[2 * half + p][:], 4))
                    dve.drain()
                    dve.sem_inc(s1["scev"], 1)

            decays(0)
            for lev in range(7):
                if lev == 0:
                    take(7, z[:, 10:12, :])
                if lev == 1:
                    take(8, z[:, 12:14, :])
                if lev < 6:
                    decays(lev + 1)
                dve.wait_ge(s1["hl"], lev + 2)
                if lev == 1:
                    dve.wait_ge(s1["vT"], 2)
                decayed(lev)
                dve.sem_inc(s1["qk"], 1)
                if lev > 0:
                    chosen(lev - 1)
            dve.sem_inc(s1["qk"], 1)
            for j in range(2):
                lj = r3(lf[:, j, :], NT)
                tt(r3(m1["ta"][:, j, :], NT), lj[:, :, P - 1:P].to_broadcast([P, NT, P]), lj, ALU.subtract)
            dve.drain()
            dve.sem_inc(s1["ex"], 1)
            chosen(6)
            chosen(7)
            dve.wait_ge(s1["hl"], 9)
            for j in range(2):
                v.tensor_copy(sml[:, 56 + 4 * j:60 + 4 * j], r3(m1["tf"][:, j, :], NT)[:, :, P - 1])
            tt(m1["tb"][:], m1["ta"][:], m1["te"][:])
            dve.drain()
            dve.sem_inc(s1["kh"], 1)
            tt(m1["tf"][:], m1["tf"][:], z[:, 6:8, :])
            dve.wait_ge(s1["khT"], 1)
            for n in range(NT):
                v.tensor_copy(khtok[:, n, :], bank[n // 2][:, (n % 2) * 2 * P:(n % 2 + 1) * 2 * P])
            dve.drain()
            dve.sem_inc(s1["khv"], 1)
            dve.sem_inc(s1["st"], 1)
            dve.drain()
            ms(m1["td"][:, :, 0:16])
            pads = z[:, 0:3, :].rearrange("p (s t) c -> p s (t c)", s=1)[:, 0, 0:2 * (T + 16)].rearrange("p (j c) -> p j c", j=2)
            ms(pads[:, :, 0:16])
            v.tensor_copy(m1["td"][:, :, 16:], z[:, 12:14, :])
            dve.drain()

            def double(dst, src, w, rows, j):
                tt(dst[rows, j, 16:16 + T], src[rows, j, 16:16 + T], src[rows, j, 16 - w:16 - w + T], ALU.add)

            top, low, both = slice(0, HD), slice(HD, P), slice(0, P)
            A, B = m1["td"], pads
            double(B, A, 1, both, 0)
            double(B, A, 1, both, 1)
            dve.drain()
            v.tensor_copy(A[top, 0, 16:], B[top, 0, 16:])
            double(A, B, 2, low, 0)
            double(A, B, 2, both, 1)
            dve.drain()
            double(B, A, 4, both, 1)
            dve.drain()
            v.tensor_copy(A[top, 1, 16:], B[top, 1, 16:])
            double(A, B, 8, low, 1)
            dve.drain()
            for j in range(2):
                tt(m1["th"][:, j, :], A[:, j, 16:], K["invcnt"][:, j, :])
            dve.drain()
            tt(m1["th"][:], m1["th"][:], z[:, 12:14, :], ALU.subtract)
            dve.drain()
            dve.sem_inc(s1["pool"], 1)
            for n in range(NT):
                dve.wait_ge(s1["kv"], n + 1)
                if n < NT - 1:
                    for j in range(2):
                        for p in range(2):
                            r, c = slice(p * HD, (p + 1) * HD), slice(p * HD, (p + 1) * HD)
                            v.scalar_tensor_tensor(S1[r, j, c], S1[r, j, c], sml[r, 56 + 4 * j + n:57 + 4 * j + n],
                                                   bank[n % 2][r, j * P + p * HD:j * P + (p + 1) * HD], ALU.mult, ALU.add)
                    dve.drain()
                    dve.sem_inc(s1["st"], 1)
                if n == 1:
                    dve.wait_ge(s1["dwy"], 1)
                    for j in range(2):
                        v.tensor_scalar(m1["tg"][:, j, :], bank[4 + j][:], col(U_DS + j), None, ALU.mult)
                    dve.drain()
                    for j in range(2):
                        splitted(y_hi[:, 6 + j, :], y_lo[:, 6 + j, :], m1["tg"][:, j, :]).then_inc(y_ready, 1)
            for j in range(2):
                v.tensor_copy(m1["tb"][:, j, :], bank[2 + j][:])
            dve.drain()
            tt(m1["ta"][:], m1["tb"][:], m1["tb"][:])
            dve.drain()
            dve.sem_inc(s1["osq"], 1)
            dve.wait_ge(s1["o"], 1)
            tt(m1["tb"][:], m1["tb"][:], m1["ta"][:])
            dve.drain()
            for j in range(2):
                v.scalar_tensor_tensor(m1["tb"][:, j, :], m1["tb"][:, j, :], col(U_CN + j), z[:, 10 + j, :], ALU.mult, ALU.mult)
            dve.drain()
            for j in range(2):
                splitted(y_hi[:, 4 + j, :], y_lo[:, 4 + j, :], m1["tb"][:, j, :]).then_inc(y_ready, 1)
            dve.drain()
            ms(ffn["pad"][:, :, 0:2])
            add_to_x(B1_IN, G_N2)
            norm_end(2)
            I, pre = B1_IN + X_OUT, 0
            fw = vec[:, U_FW:U_FW + 6 * FFC].rearrange("p (i s k) -> p i s k", s=2, k=3)
            fb = vec[:, U_FB:U_FB + 2 * FFC].rearrange("p (i s) -> p i s", s=2)
            for k, n in enumerate(PARTS):
                with dve.Fori(0, n) as i:
                    c = i + sum(PARTS[:k])
                    for s in range(2):
                        pad, cv = ffn["pad"][:, s, :], ffn["cv"][:, s, :]
                        if s == 0:
                            dve.wait_ge(h_act, pre + i) if k else None
                        scaled(s, I + i, pad[:, 2:]).then_inc(acc_free[s], 1)
                        dve.drain()
                        v.tensor_scalar(cv, pad[:, 2:], fw[:, bass.ds(c, 1), s, 2], fb[:, bass.ds(c, 1), s], ALU.mult, ALU.add)
                        for d in range(2):
                            dve.drain()
                            v.scalar_tensor_tensor(cv, pad[:, d:d + T], fw[:, bass.ds(c, 1), s, d], cv, ALU.mult, ALU.add)
                        dve.drain()
                        if s == 0:
                            dve.sem_inc(h_pre, 1)
                    dve.wait_ge(h_act, pre + i + 1)
                    hidden(i, ffn["act"][:], ffn["cv"][:, 1, :])
                    dve.drain()
                I, pre = I + n, pre + n
                dve.drain()
                add_to_x(I, G_N3 if k == len(PARTS) - 1 else None); I = I + X_OUT
            dve.wait_ge(first_in, load_wait * (len(FIRST) + 1))
            for j in range(2):
                splitted(emb_hi[:, j, :], emb_lo[:, j, :], emb[:, j, :])
            norm_end(3)
            ms(sumsq[:])
            ms(sumsq_fin)
            dve.drain()

            def embedding_gate(j):
                scaled(0, I + j, ffn["t"][:]).then_inc(acc_free[0], 1)
                dve.drain()
                dve.sem_inc(h_pre, 1)

            def embedding(j):
                dve.wait_ge(h_act, FFC + j + 1)
                done(1, I + j)
                tt(ffn["h"][:], acc[1][:], ffn["act"][:]).then_inc(acc_free[1], 1)
                dve.drain()

            def finished(j):
                tt(x[:, j, :], x[:, j, :], ffn["h"][:], ALU.add)
                dve.drain()
                tt(ffn["sq"][:], x[:, j, :], x[:, j, :])
                dve.drain()
                v.tensor_scalar(x[:, j, :], x[:, j, :], gain_of(G_FIN, j), None, ALU.mult)
                tt(sumsq[:], sumsq[:], ffn["sq"][:], ALU.add)
                dve.drain()
                tt(ffn["sq"][:], x[:, j, :], x[:, j, :])
                v.tensor_scalar(mixed[:, j, :], x[:, j, :], gain_of(G_L, j), None, ALU.mult)
                dve.drain()
                tt(sumsq_fin, sumsq_fin, ffn["sq"][:], ALU.add)

            embedding_gate(0)
            embedding(0)
            with dve.Fori(0, PE_PAIRS - 1) as j:
                embedding_gate(j + 1)
                finished(j)
                embedding(j + 1)
            with dve.Fori(PE_PAIRS - 1, PE_PAIRS) as j:
                finished(j)
            dve.drain()
            dve.sem_inc(sumsq_ready, 1)
            for c in range(DC):
                if c == DC // 2:
                    dve.wait_ge(root_ready, 4)
                    v.tensor_copy(rstd_fin, rstd[:])
                    tt(sumsq[:], sumsq_fin, rstd[:])
                    dve.drain()
                    tt(sumsq[:], sumsq[:], rstd[:])
                    dve.drain()
                    dve.sem_inc(sumsq_ready, 1)
                splitted(xg_hi[:, c, :], xg_lo[:, c, :], mixed[:, c, :]).then_inc(xg_ready, 1)
            for c in range(DC):
                tt(x[:, c, :], x[:, c, :], rstd_fin)
            dve.drain()
            vec2 = K["vec2"]

            def pcol(k, n=4):
                return vec2[:, k:k + n]

            with dve.Fori(0, LAYERS) as l:
                I = B1_PAIRS + l * LAYER_PAIRS
                dve.wait_ge(layer_in, load_wait * (1 + len(RWKV)) * (l + 1))
                dve.wait_ge(root_ready, 2 * l + 5)
                tt(rstd[:], rstd[:], rstd_fin)
                dve.drain()
                hz, dz = rw["SC"][:].rearrange("p (s a) b c -> p s (a b c)", s=4), rw["W"]
                for s in range(2):
                    ms(hz[:, s, 0:1])
                dve.drain()
                with dve.Fori(0, RW_PAIRS) as i:
                    for s in range(2):
                        j = 2 * i + s
                        scaled(s, I + i, hz[:, s, 1:T + 1]).then_inc(acc_free[s], 1)
                        dve.drain()
                        tt(dz[:], hz[:, s, 0:T], hz[:, s, 1:T + 1], ALU.subtract)
                        dve.drain()
                        v.scalar_tensor_tensor(z_rw[:, j, :], dz[:], vec2[:, bass.ds(V_MU + j, 1)], hz[:, s, 1:T + 1], ALU.mult, ALU.add)
                        dve.drain()
                I = I + RW_PAIRS
                ms(rw["S"][:])
                ms(rw["W"][:])
                ms(rw["U"][:])
                dve.drain()
                dve.sem_inc(s2["z"], 1)
                with dve.Fori(0, NT) as n:
                    it, F = l * NT + n, I + 2 * n

                    def after(name, k, per=1):
                        dve.wait_ge(s2[name], it * per + k)

                    def take(s, k):
                        scaled(s, F + k, z_rt[:, bass.ds(4 * n + 2 * k + s, 1), :].rearrange("p a b -> p (a b)")).then_inc(acc_free[s], 1)

                    def say(name, k=1):
                        dve.drain()
                        dve.sem_inc(s2[name], k)

                    zr, zk, zv = (tile_of(z_rw, a, 4, n) for a in (0, 4, 8))
                    say("stev")
                    tt(rw["kk"][:], zk, bc(pcol(V_KK), P))
                    dve.drain()
                    tt(rw["sq"][:], rw["kk"][:], rw["kk"][:])
                    after("lora", 1)
                    tt(rw["kp"][:], r3(bank[0][:], 4), bc(pcol(V_W0), P), ALU.add)
                    tt(rw["b"][:], r3(bank[1][:], 4), bc(pcol(V_A0), P), ALU.add)
                    say("pre")
                    take(0, 0)
                    v.tensor_copy(rw["g"][:], r3(bank[2][:], 4))
                    after("sig", 1)
                    flat = [rw[k][:].rearrange("p a b -> p (a b)") for k in ("Lr", "kp")]
                    v.tensor_tensor_scan(flat[0], K["reset64"][:], flat[1], 0.0, ALU.mult, ALU.add)
                    dve.drain()
                    tt(rw["Lp"][:], rw["Lr"][:], rw["kp"][:], ALU.subtract)
                    lr = rw["Lr"][:].rearrange("p a (c t) -> p (a c) t", c=2)
                    tt(rw["Dl"][:].rearrange("p a (c t) -> p (a c) t", c=2), lr[:, :, CH - 1:CH].to_broadcast([P, 8, CH]), lr, ALU.subtract)
                    say("L")
                    take(1, 0)
                    v.scalar_tensor_tensor(rw["kp"][:], rw["b"][:], -1.0, bc(pcol(V_KA), P), ALU.add, ALU.mult)
                    dve.drain()
                    v.scalar_tensor_tensor(rw["kp"][:], rw["kp"][:], 1.0, zk, ALU.add, ALU.mult)
                    dve.drain()
                    tt(rw["bon"][:], zr, rw["kp"][:])
                    dve.drain()
                    tt(rw["bon"][:], rw["bon"][:], bc(pcol(V_RK), P))
                    say("nrm_in")
                    take(0, 1)
                    after("nrm", 1)
                    v.tensor_scalar(rw["sq"][:], r3(bank[0][:], 4), 1e-24, None, ALU.max)
                    tt(rw["bon"][:], r3(bank[1][:], 4), zv)
                    say("rn")
                    take(1, 1)
                    after("root", 1)
                    tt(rw["kk"][:], rw["kk"][:], rw["sq"][:])
                    dve.drain()
                    tt(rw["b"][:], rw["b"][:], rw["kk"][:])
                    after("exp", 1)
                    v.scalar_tensor_tensor(rw["AR"][:, :, 0, :], rw["kk"][:], -1.0, rw["Lp"][:], ALU.mult, ALU.mult)
                    tt(rw["AR"][:, :, 1, :], zr, rw["eP"][:])
                    v.tensor_copy(rw["pc"][:], rw["eP"][:].rearrange("p a (c t) -> p a c t", c=2)[:, :, :, CH - 1])
                    dve.drain()
                    tt(rw["BT"][:], rw["b"][:], rw["eM"][:])
                    tt(rw["KT"][:], rw["kp"][:], rw["eM"][:])
                    tt(rw["BH"][:], rw["b"][:], rw["Dl"][:])
                    tt(rw["KH"][:], rw["kp"][:], rw["Dl"][:])
                    v.tensor_copy(rw["VT"][:], zv)
                    say("ops")
                    for h in range(8):
                        after("sc", h + 1, 8)
                        tt(rw["SC"][:, h], r3(bank[3 + h % 2][:], 4), K["rwmask"][:])
                        say("scev")
                    tl = rw["SC"][:, :, 0, :]
                    tt(rw["G"][:], tl, mid(K["lev"][:, 0, :], 8))
                    dve.drain()
                    tt(rw["G"][:], rw["G"][:], mid(K["ident"][:], 8), ALU.add)
                    dve.drain()
                    after("tr", 1)
                    dve.sem_inc(s2["g1"], 1)
                    for lev in range(1, 6):
                        if lev > 1:
                            after("y", 2 * (lev - 1), 10)
                        tt(rw["TL"][:], tl, mid(K["lev"][:, lev, :], 8))
                        say("tl")
                        for half in range(2):
                            after("y", 2 * (lev - 1) + half + 1, 10)
                            tt(rw["Y"][:, 4 * half:4 * half + 4], r3(bank[3 + half][:], 4), mid(K["ident"][:], 4), ALU.add)
                            say("yi")
                    for c in range(2):
                        after("st", c + 1, 2)
                        tt(rw["S"][:], rw["S"][:], bc(rw["pc"][:, :, c], P))
                        dve.drain()
                        for p in range(2):
                            r = slice(p * HD, (p + 1) * HD)
                            tt(rw["S"][r, :, r], rw["S"][r, :, r], r3(bank[1][r, :], 4)[:, :, r], ALU.add)
                        say("stev")
                    after("yo", 1)
                    yv = r3(rw["W"][:], 4)
                    v.tensor_copy(yv, r3(bank[0][:], 4))
                    say("ysb")
                    after("ysum", 1)
                    v.scalar_tensor_tensor(yv, r3(bank[2][:], 4), -1.0 / HD, yv, ALU.mult, ALU.add)
                    dve.drain()
                    tt(rw["sq"][:], yv, yv)
                    say("ysq")
                    after("yroot", 1)
                    tt(yv, yv, rw["sq"][:])
                    dve.drain()
                    tt(yv, yv, bc(pcol(V_LNG), P))
                    dve.drain()
                    tt(yv, yv, bc(pcol(V_LNB), P), ALU.add)
                    dve.drain()
                    tt(yv, yv, rw["bon"][:], ALU.add)
                    dve.drain()
                    tt(yv, yv, rw["g"][:])
                    dve.drain()
                    splitted(tile_of(y1_hi, 0, 4, n), tile_of(y1_lo, 0, 4, n), yv)
                    say("done")
                I = I + RET_PAIRS
                with dve.Fori(0, AT_PAIRS) as i:
                    for s in range(2):
                        scaled(s, I + i, z_at[:, 2 * i + s, :]).then_inc(acc_free[s], 1)
                I = I + AT_PAIRS

                def gate(i, first):
                    scaled(0, first + i, ffn["t"][:]).then_inc(acc_free[0], 1)
                    dve.drain()
                    dve.sem_inc(o_gate, 1)

                def branch(i, first, dst):
                    dve.wait_ge(o_sig, l * O_PAIRS + i + 1)
                    done(1, first + i)
                    tt(dst, acc[1][:], ffn["act"][:]).then_inc(acc_free[1], 1)
                    dve.drain()

                O = I
                dve.wait_ge(retat_in, load_wait * len(RETAT) * (l + 1))
                ms(rt["R"][:])
                dve.drain()
                dve.sem_inc(s3["z"], 1)
                with dve.Fori(0, NT) as n:
                    it = l * NT + n

                    def after(name, k, per=1):
                        dve.wait_ge(s3[name], it * per + k)

                    def say(name, k=1):
                        dve.drain()
                        dve.sem_inc(s3[name], k)

                    say("rev")
                    cosn, sinn = (mid(K[k][:, bass.ts(n, P)], 4) for k in ("cos", "sin"))
                    for a, dst in ((0, "qr"), (4, "kr")):
                        tt(rt["t1"][:], tile_of(z_rt, a, 4, n), cosn)
                        if a == 0:
                            after("sw", 1)
                        tt(rt["t2"][:], r3(bank[a // 4][:], 4), sinn)
                        dve.drain()
                        tt(rt[dst][:], rt["t1"][:], rt["t2"][:], ALU.add)
                        dve.drain()
                    tt(rt["qx"][:], rt["qr"][:], K["xi"][:])
                    say("rot")
                    gate(2 * n, O)
                    after("sc", 1)
                    for p in range(2):
                        tt(rt["ST"][:, p], r3(bank[2 + p][:], 4), K["dmat"][:, p])
                    tt(r3(rt["kz"][:], 8), r3(bank[4][:], 8), bc(K["zeta"][:], HD))
                    say("kz")
                    branch(2 * n, O, mixed[:, 2 * n, :])
                    after("o", 1)
                    v.tensor_copy(rt["o"][:], r3(bank[0][:], 4))
                    dve.drain()
                    tt(rt["sq"][:], rt["o"][:], rt["o"][:])
                    say("osb")
                    tt(rt["R"][:], rt["R"][:], bc(K["cdecay"][:], P))
                    dve.drain()
                    for p in range(2):
                        r = slice(p * HD, (p + 1) * HD)
                        tt(rt["R"][r, :, r], rt["R"][r, :, r], r3(bank[1][r, :], 4)[:, :, r], ALU.add)
                    say("rev")
                    after("root", 1)
                    tt(rt["o"][:], rt["o"][:], rt["sq"][:])
                    dve.drain()
                    after("silu", 1)
                    tt(rt["o"][:], rt["o"][:], rt["gs"][:])
                    dve.drain()
                    splitted(tile_of(y2_hi, 0, 4, n), tile_of(y2_lo, 0, 4, n), rt["o"][:])
                    gate(2 * n + 1, O)
                    branch(2 * n + 1, O, mixed[:, 2 * n + 1, :])
                    say("done")
                ms(an["k"][:])
                ms(an["v"][:])
                dve.drain()
                dve.sem_inc(s4["z"], 1)
                with dve.Fori(0, NT) as n:
                    it = l * NT + n

                    def after(name, k, per=1):
                        dve.wait_ge(s4[name], it * per + k)

                    def add_branch(k):
                        j = 2 * n + k
                        branch(DC + j, O, ffn["sq"][:])
                        tt(mixed[:, j, :], mixed[:, j, :], ffn["sq"][:], ALU.add)
                        dve.drain()

                    def say(name, k=1):
                        dve.drain()
                        dve.sem_inc(s4[name], k)

                    zqk = tile_of(z_at, 0, 5, n)
                    tt(an["sq"][:], zqk, zqk)
                    v.tensor_copy(an["vf"][:], z_at[:, 5, bass.ts(n, P)])
                    say("sq")
                    v.tensor_copy(an["v"][:, 0, :], an["v"][:, 1, :])
                    v.tensor_copy(an["k"][:, :, 0, :], an["k"][:, :, 1, :])
                    dve.drain()
                    after("vT", 1)
                    v.tensor_copy(an["v"][:, 1, :], bank[5][:, 0:P])
                    after("root", 1)
                    v.scalar_tensor_tensor(an["q"][:], tile_of(z_at, 0, 4, n), pcol(V_GQ, 1), an["rs"][:, 0:4, :], ALU.mult, ALU.mult)
                    for kv in range(2):
                        r = slice(kv * HD, (kv + 1) * HD)
                        v.scalar_tensor_tensor(an["k"][r, kv, 1, :], z_at[r, 4, bass.ts(n, P)], vec2[r, V_GK:V_GK + 1], an["rs"][r, 4, :],
                                               ALU.mult, ALU.mult)
                    say("qk")
                    gate(DC + 2 * n, O)
                    after("sc", 1)
                    mask = K["atmask"][:, n, :]
                    for p in range(2):
                        for b in range(2):
                            v.scalar_tensor_tensor(an["s"][:, p, 2 * b:2 * b + 2, :], r3(bank[2 * p + b][:], 2), HD ** -0.5, mid(mask, 2),
                                                   ALU.mult, ALU.add)
                    dve.drain()
                    s8 = an["s"][:].rearrange("p a b c -> p (a b) c")
                    v.tensor_reduce(an["mx"][:], s8, AX.X, ALU.max)
                    dve.drain()
                    tt(an["mx"][:], an["mx"][:], pcol(V_SINK, 8), ALU.max)
                    dve.drain()
                    v.tensor_scalar(an["nm"][:], an["mx"][:], -1.0, None, ALU.mult)
                    tt(an["es"][:], pcol(V_SINK, 8), an["mx"][:], ALU.subtract)
                    say("mx")
                    add_branch(0)
                    after("p", 1)
                    tt(an["sum"][:], an["sum"][:], an["es"][:], ALU.add)
                    dve.drain()
                    v.reciprocal(an["sum"][:], an["sum"][:])
                    dve.drain()
                    tt(s8, s8, bc(an["sum"][:], 2 * P))
                    say("pn")
                    gate(DC + 2 * n + 1, O)
                    add_branch(1)
                    after("o", 1)
                    v.tensor_copy(an["o"][:], r3(bank[4][:], 4))
                    dve.drain()
                    splitted(tile_of(y1_hi, 0, 4, n), tile_of(y1_lo, 0, 4, n), an["o"][:])
                    say("done")
                with dve.Fori(0, DC) as j:
                    gate(2 * DC + j, O)
                    branch(2 * DC + j, O, ffn["h"][:])
                    tt(ffn["h"][:], ffn["h"][:], mixed[:, j, :], ALU.add)
                    dve.drain()
                    splitted(hid_hi[:, j, :], hid_lo[:, j, :], ffn["h"][:]).then_inc(hid_ready, 1)
                I = I + O_PAIRS
                dve.drain()
                add_to_x(I, G_L + 1 + 2 * l); I = I + X_OUT
                norm_end(2 * l + 6)
                swiglu(I, FFC + PE_PAIRS + l * FFC, G_L + 2 + 2 * l)
                ms(rstd_fin, 1.0)
                dve.drain()
                dve.sem_inc(sumsq_ready, 1)

        @block.scalar
        def _(act):
            def fn(o, i, f, **kw):
                return nc.scalar.activation(o, i, f, **kw)

            def rsqrt(o, sums, n, eps=None):
                if eps is None:
                    fn(o, sums, ACT.Ln)
                else:
                    fn(o, sums, ACT.Ln, scale=1.0 / n, bias=K["eps"][:, eps:eps + 1])
                act.drain()
                return fn(o, o, ACT.Exp, scale=-0.5)

            def roots(count):
                act.wait_ge(stat_ready, count)
                act.sem_inc(act_turn, 1)
                rsqrt(rstd[:], bank[5][:], D, 0).then_inc(root_ready, 1)

            def gates(n, pre0, f, src="t"):
                with act.Fori(0, n) as i:
                    act.wait_ge(h_pre, pre0 + i + 1)
                    act.sem_inc(act_turn, 1)
                    fn(ffn["act"][:], ffn["t"][:] if src == "t" else ffn["cv"][:, 0, :], f).then_inc(h_act, 1)

            act.wait_ge(keep_in, load_wait * (len(KEEP) - 1))
            for c in range(DC):
                act.wait_ge(x_in[c], load_wait)
                fn(mixed[:, c, :], x[:, c, :], ACT.Square).then_inc(squared, 1)
            roots(1)
            act.wait_ge(first_in, load_wait * len(FIRST))
            vec = K["vec1"]
            lp = [sml[:, 8 + 2 * k:10 + 2 * k] for k in range(8)]
            act.wait_ge(s1["la"], 1)
            fn(lp[2], lp[1], ACT.Exp).then_inc(s1["ea"], 1)
            act.wait_ge(s1["z"], 2)
            fn(z[:, 4:6, :], z[:, 4:6, :], ACT.Gelu_apprx_tanh).then_inc(s1["act1"], 1)
            act.wait_ge(s1["ri"], 1)
            for j in range(2):
                fn(z[:, 2 + j, :], bank[2 + j][:], ACT.Sigmoid, bias=vec[:, U_BA + j:U_BA + j + 1])
            for j in range(2):
                last = fn(m1["te"][:, j, :], bank[4 + j][:], ACT.Sigmoid, bias=vec[:, U_BX + j:U_BX + j + 1])
            last.then_inc(s1["sig"], 1)
            act.wait_ge(s1["vT"], 1)
            for b in range(2):
                last = fn(z[:, 14 + b, :], bank[b][:], ACT.Gelu_apprx_tanh)
            last.then_inc(s1["act1"], 1)
            act.wait_ge(s1["z"], 4)
            fn(z[:, 0:2, :], z[:, 0:2, :], ACT.Gelu_apprx_tanh).then_inc(s1["act1"], 1)
            act.wait_ge(s1["mlt"], 1)
            fn(m1["tc"][:], z[:, 2:4, :], ACT.Exp, scale=-1.0)
            fn(m1["tb"][:], z[:, 2:4, :], ACT.Tanh)
            act.drain()
            inv = m1["td"][:, :, 0:T]
            fn(inv, m1["tb"][:], ACT.Ln, bias=1.0)
            act.drain()
            fn(inv, inv, ACT.Exp, scale=-1.0).then_inc(s1["scan"], 1)
            act.wait_ge(s1["lv"], 1)
            ag = sml[:, 48:56].rearrange("p (n c) -> p n c", n=NT)
            rsqrt(sml[:, 0:4], ag[:, :, 1], 1, 0).then_inc(s1["sqr"], 1)
            act.wait_ge(s1["hx"], 1)
            fn(m1["tb"][:], m1["tb"][:], ACT.Sqrt, scale=2.0).then_inc(s1["hl"], 1)
            act.wait_ge(s1["lf"], 1)
            fn(m1["te"][:], z[:, 8:10, :], ACT.Sigmoid, scale=-1.0)
            fn(m1["tf"][:], m1["tf"][:], ACT.Exp)
            act.drain()
            fn(m1["tf"][:], m1["tf"][:], ACT.Ln, bias=1.0).then_inc(s1["sil"], 1)
            act.wait_ge(s1["z"], 6)
            fn(z[:, 6:8, :], z[:, 6:8, :], ACT.Silu)
            act.wait_ge(s1["vT"], 2)
            for b in range(2):
                last = fn(z[:, 16 + b, :], bank[4 + b][:], ACT.Copy)
            last.then_inc(s1["iev"], 1)
            act.wait_ge(s1["z"], 8)
            fn(z[:, 10:12, :], z[:, 10:12, :], ACT.Silu)
            for lev in range(7):
                act.wait_ge(s1["ex"], lev + 1)
                e = m1[("ta", "tf")[lev % 2]]
                fn(e[:], e[:], ACT.Exp).then_inc(s1["hl"], 1)
            act.wait_ge(s1["ex"], 8)
            fn(m1["tf"][:], m1["td"][:, :, 0:T], ACT.Exp)
            fn(m1["ta"][:], m1["ta"][:], ACT.Exp).then_inc(s1["hl"], 1)
            act.wait_ge(s1["on"], 1)
            for j in range(2):
                last = rsqrt(m1["ta"][:, j, :], bank[j][:], HD, 0)
            last.then_inc(s1["o"], 1)
            roots(2)
            gates(FFC, 0, ACT.Gelu_apprx_tanh, "cv")
            roots(3)
            gates(PE_PAIRS, FFC, ACT.Sigmoid)
            roots(4)
            with act.Fori(0, LAYERS) as l:
                roots(2 * l + 5)
                act.wait_ge(s2["z"], l + 1)
                act.sem_inc(act_turn, 1)
                with act.Fori(0, NT) as n:
                    it = l * NT + n

                    def after(name, k, per=1):
                        act.wait_ge(s2[name], it * per + k)
                        act.sem_inc(act_turn, 1)

                    fn(rw["th"][0:HD, :], z_rw[0:HD, 12, bass.ts(n, P)], ACT.Tanh)
                    fn(rw["th"][HD:P, :], z_rw[HD:P, 12, bass.ts(n, P)], ACT.Copy)
                    fn(rw["sg"][:], z_rw[:, 13, bass.ts(n, P)], ACT.Sigmoid).then_inc(s2["lora_in"], 1)
                    after("pre", 1)
                    fn(rw["kp"][:], rw["kp"][:], ACT.Sigmoid)
                    fn(rw["b"][:], rw["b"][:], ACT.Sigmoid).then_inc(s2["sig"], 1)
                    after("L", 1)
                    fn(rw["eP"][:], rw["Lr"][:], ACT.Exp, scale=-DECAY)
                    fn(rw["eM"][:], rw["Lr"][:], ACT.Exp, scale=DECAY)
                    fn(rw["Lp"][:], rw["Lp"][:], ACT.Exp, scale=-DECAY)
                    fn(rw["Dl"][:], rw["Dl"][:], ACT.Exp, scale=-DECAY).then_inc(s2["exp"], 1)
                    after("rn", 1)
                    rsqrt(rw["sq"][:], rw["sq"][:], 1).then_inc(s2["root"], 1)
                    after("tr", 1)
                    fn(rw["tokB"][:], bank[0][:], ACT.Copy)
                    fn(rw["tokK"][:], bank[1][:], ACT.Copy)
                    fn(rw["tokV"][:], bank[2][:], ACT.Copy).then_inc(s2["tok"], 1)
                    for half in range(2):
                        after("x", half + 1, 2)
                        fn(rw["X"][:, 4 * half:4 * half + 4], r3(bank[half][:], 4), ACT.Copy).then_inc(s2["xev"], 1)
                    for lev in range(1, 6):
                        for half in range(2):
                            after("xg", 2 * (lev - 1) + half + 1, 10)
                            if lev < 5:
                                fn(rw["X"][:, 4 * half:4 * half + 4], r3(bank[half][:], 4), ACT.Copy)
                            fn(rw["G"][:, 4 * half:4 * half + 4], r3(bank[(2, 5)[half]][:], 4), ACT.Copy).then_inc(s2["xgev"], 1)
                    for c in range(2):
                        cs = slice(c * CH, (c + 1) * CH)
                        after("w", c + 1, 2)
                        fn(rw["W"][cs, :], bank[3][cs, :], ACT.Copy).then_inc(s2["wev"], 1)
                        after("u", c + 1, 2)
                        fn(rw["U"][cs, :], bank[4][cs, :], ACT.Copy).then_inc(s2["uev"], 1)
                    after("yvar", 1)
                    rsqrt(rw["sq"][:], r3(bank[5][:], 4), HD, 1).then_inc(s2["yroot"], 1)

                def gate_sigmoid(i):
                    act.wait_ge(o_gate, l * O_PAIRS + i + 1)
                    act.sem_inc(act_turn, 1)
                    fn(ffn["act"][:], ffn["t"][:], ACT.Sigmoid).then_inc(o_sig, 1)

                act.wait_ge(s3["z"], l + 1)
                act.sem_inc(act_turn, 1)
                with act.Fori(0, NT) as n:
                    it = l * NT + n

                    def after(name, k, per=1):
                        act.wait_ge(s3[name], it * per + k)
                        act.sem_inc(act_turn, 1)

                    after("rev", 1, 2)
                    fn(rt["o"][:], tile_of(z_rt, 12, 4, n), ACT.Copy).then_inc(s3["vf"], 1)
                    fn(rt["gs"][:], tile_of(z_rt, 8, 4, n), ACT.Silu).then_inc(s3["silu"], 1)
                    after("vT", 1)
                    fn(rt["vt"][:], bank[5][:], ACT.Copy).then_inc(s3["vt"], 1)
                    gate_sigmoid(2 * n)
                    after("osum", 1)
                    rsqrt(rt["sq"][:], r3(bank[5][:], 4), HD, 0).then_inc(s3["root"], 1)
                    gate_sigmoid(2 * n + 1)
                with act.Fori(0, NT) as n:
                    it = l * NT + n

                    def after(name, k, per=1):
                        act.wait_ge(s4[name], it * per + k)
                        act.sem_inc(act_turn, 1)

                    after("ss", 1)
                    rsqrt(an["rs"][:, 0:4, :], r3(bank[0][:], 4), HD, 0)
                    rsqrt(an["rs"][:, 4, :], bank[1][:, 0:P], HD, 0).then_inc(s4["root"], 1)
                    after("qk", 1)
                    for kv in range(2):
                        r, q = slice(kv * HD, (kv + 1) * HD), slice((1 - kv) * HD, (2 - kv) * HD)
                        last = fn(an["k"][q, kv, 1, :], an["k"][r, kv, 1, :], ACT.Copy)
                    last.then_inc(s4["dup"], 1)
                    gate_sigmoid(DC + 2 * n)
                    after("mx", 1)
                    s8 = an["s"][:].rearrange("p a b c -> p (a b) c")
                    fn(an["es"][:], an["es"][:], ACT.Exp)
                    for h in range(8):
                        last = fn(s8[:, h, :], s8[:, h, :], ACT.Exp, bias=an["nm"][:, h:h + 1], accum_out=an["sum"][:, h:h + 1])
                    act.drain()
                    act.sem_inc(s4["p"], 1)
                    gate_sigmoid(DC + 2 * n + 1)
                    after("pT", 1)
                    for b in range(4):
                        last = fn(an["pT"][:, 2 * b:2 * b + 2].rearrange("p a b c -> p (a b c)"), bank[b][:], ACT.Copy)
                    last.then_inc(s4["pTe"], 1)
                with act.Fori(0, DC) as i:
                    gate_sigmoid(2 * DC + i)
                roots(2 * l + 6)
                gates(FFC, FFC + PE_PAIRS + l * FFC, ACT.Silu)



def slots(w, order=None):
    k, n = w.shape[0] // P, w.shape[1] // P
    s = w.reshape(k, P, n, P).transpose(2, 1, 0, 3)
    if order is not None:
        s = s[np.asarray(order)]
    return np.ascontiguousarray(s).reshape(-1, 2, P, k * P)


def columns(v):
    return np.ascontiguousarray(v.reshape(-1, P).T)


def per_head(v):
    return np.concatenate([v, v]).reshape(P, 1)


def block_diagonal(w):
    o = np.zeros((P, 2, P), w.dtype)
    for h in range(4):
        p = slice((h % 2) * HD, (h % 2 + 1) * HD)
        o[p, h // 2, p] = w[h]
    return o


def lay_out(a):
    d = dict(shape_constants())
    x, f = a["x"][0], {k: v[0] for k, v in a.items() if not k.endswith("_2") and k not in ("x", "final_g")}
    d["x"] = np.ascontiguousarray(x.T).reshape(DC, P, T)
    d["p"] = np.ascontiguousarray(f["p"][0].T.reshape(2, P, T).transpose(1, 0, 2))
    g = [f["norm1_g"], f["norm2_g"], f["norm3_g"], a["final_g"]]
    for l in range(LAYERS):
        g += [a["norm1_g_2"][l], a["norm2_g_2"][l]]
    g.append(a["norm1_g_2"][0])
    d["gains"] = np.ascontiguousarray(np.stack([columns(v) for v in g], 1))
    d["w1_in"] = slots(f["w_in"], [4, 5, 6, 7, 2, 3, 0, 1, 10, 11, 8, 9, 12, 13, 14, 15, 16, 17])
    d["w1_out"] = slots(f["w_out"])
    both = [c for j in range(FFC) for c in (j, FFC + j)]

    def ffn(name, up, down):
        pairs, at = slots(up, both), 0
        for k, n in enumerate(PARTS):
            d[f"{name}_up{k}"] = np.ascontiguousarray(pairs[at:at + n])
            d[f"{name}_down{k}"] = slots(down[at * P:(at + n) * P])
            at += n

    ffn("w1", f["w_up"], f["w_down"])
    d["w1_pg"] = slots(f["w_pg"]).reshape(DC, P, DC * P)
    d["w1_pe"] = slots(f["w_pe"]).reshape(DC, P, 2 * P)
    conv = f["ffn_conv_w"].reshape(3, 2, FFC, P).transpose(3, 2, 1, 0).reshape(P, -1)
    convb = f["ffn_conv_b"].reshape(2, FFC, P).transpose(2, 1, 0).reshape(P, -1)
    d["vec1"] = np.ascontiguousarray(np.concatenate([
        f["b_conv_w"].reshape(4, 2, P).transpose(2, 1, 0).reshape(P, 8), columns(f["b_conv_b"]), columns(f["b_ba"]),
        columns(f["b_bx"]), columns(f["b_lam"]), per_head(f["c_norm_g"]), per_head(f["c_norm_g"]), columns(f["d_scale"]),
        conv, convb], 1))
    d["wa"], d["wx"], d["dw"] = (block_diagonal(f[k]) for k in ("b_wa", "b_wx", "d_w"))
    d["ws"] = np.ascontiguousarray(f["a_ws"].transpose(2, 0, 1))
    d["lng"], d["lnb"] = (np.ascontiguousarray(np.broadcast_to(f[k], (P, 2 * P))) for k in ("a_ln_g", "a_ln_b"))
    d["bs"] = np.ascontiguousarray(np.repeat(f["a_bs"].reshape(2, 2, P).transpose(1, 0, 2), HD, axis=0))

    per_layer = {}

    def keep(name, v):
        per_layer.setdefault(name, []).append(v)

    for l in range(LAYERS):
        w = {k[:-2]: v[l] for k, v in a.items() if k.endswith("_2")}
        s = slots(w["w_in"]).reshape(-1, P, DC * P)

        def take(order):
            return s[np.asarray(order)].reshape(-1, 2, P, DC * P)

        keep("w2_rw", take(range(6, 20)))
        keep("w2_ret", take([*range(20, 28), *range(32, 36), *range(28, 32)]))
        keep("w2_at", take(range(0, 6)))
        keep("w2_gate", s[np.asarray([36 + b * DC + j for b in (1, 2, 0) for j in range(DC)])])
        o = np.stack([slots(w[k]).reshape(DC, P, 4 * P) for k in ("w_rwkv_o", "w_ret_o", "w_attn_o")])
        keep("w2_o", o.reshape(3 * DC, P, 4 * P))
        keep("w2_out", slots(w["w_out"]))
        gate, up = slots(w["w_ffn_gate"]).reshape(FFC, P, DC * P), slots(w["w_ffn_up"]).reshape(FFC, P, DC * P)
        pairs, at = np.stack([gate, up], 1), 0
        for k, n in enumerate(PARTS):
            keep(f"w2_up{k}", pairs[at:at + n])
            keep(f"w2_down{k}", slots(w["w_ffn_down"][at * P:(at + n) * P]))
            at += n
        sink = np.broadcast_to(w["attn_sinks"].reshape(4, 2).T.reshape(1, 8), (P, 8))
        keep("vec2", np.concatenate([columns(w["rwkv_shift_mu"]), *(columns(w["rwkv_" + k]) for k in (
            "w0", "a0", "k_k", "k_a")), columns(w["rwkv_r_k"]), columns(w["rwkv_lnx_g"]), columns(w["rwkv_lnx_b"]),
            per_head(w["attn_q_norm_g"]), per_head(w["attn_k_norm_g"]), sink], 1))
        zero = np.zeros((HD, T), np.float32)
        keep("w2", np.concatenate([w["rwkv_w2"], zero]).reshape(P, 4, P))
        keep("a2", np.concatenate([zero, w["rwkv_a2"]]).reshape(P, 4, P))
        keep("g2", w["rwkv_g2"].reshape(P, 4, P))
    for name, v in per_layer.items():
        d[name] = np.ascontiguousarray(np.stack(v))
    return d


def kernel(**inputs):
    import concourse.bacc as bacc
    from concourse.bass_utils import run_bass_kernel_spmd

    nc = bacc.Bacc("TRN2", target_bir_lowering=False, num_devices=1)
    arrays, dram = {}, {}
    for name, v in lay_out({k: np.asarray(v) for k, v in inputs.items()}).items():
        arrays["in_" + name] = v
        dram[name] = nc.dram_tensor("in_" + name, v.shape, mybir.dt.from_np(v.dtype), kind="ExternalInput").ap()
    out = nc.dram_tensor("out_x", (DC, P, T), F32, kind="ExternalOutput").ap()
    build(nc, dram, out)
    r = run_bass_kernel_spmd(nc, [arrays], core_ids=[0])
    return np.ascontiguousarray(r.results[0]["out_x"].reshape(D, T).T).reshape(1, T, D)
```

```python
from contextlib import ExitStack

import numpy as np
import concourse.bass as bass
from concourse import mybir

F32, F32R, U32 = mybir.dt.float32, mybir.dt.float32r, mybir.dt.uint32
ACT, ALU = mybir.ActivationFunctionType, mybir.AluOpType
AX = mybir.AxisListType

P = 128
T = 512
NT = T // P
D = 1024
DC = D // P
LAYERS = 2
HD = 64
CH = 64
FFC = 2816 // P
PARTS = (8, 8, 6)
EPS = 1e-6
LN_EPS = 64e-5
DECAY = float(np.exp(-0.5))

B1_IN, X_OUT, O_PAIRS, PE_PAIRS = 9, 4, 24, 8
FFN_PAIRS = sum(PARTS) + X_OUT * len(PARTS)
B1_PAIRS = B1_IN + X_OUT + FFN_PAIRS + PE_PAIRS
RW_PAIRS, RET_PAIRS, AT_PAIRS = 7, 8, 3
LAYER_PAIRS = RW_PAIRS + RET_PAIRS + AT_PAIRS + O_PAIRS + X_OUT + FFN_PAIRS

G_N1, G_N2, G_N3, G_FIN, G_L = 0, 1, 2, 3, 4

V_MU, V_W0, V_A0, V_KK, V_KA, V_RK, V_LNG, V_LNB, V_GQ, V_GK, V_SINK = 0, 14, 18, 22, 26, 30, 34, 38, 42, 43, 44
V_N = 52
U_CW, U_CB, U_BA, U_BX, U_LAM, U_CN, U_DS, U_FW, U_FB = 0, 8, 10, 12, 14, 16, 18, 20, 20 + 3 * 2 * FFC
U_N = U_FB + 2 * FFC


def shape_constants():
    i = np.arange(P)
    row_head = i // HD
    c = {}
    c["ident"] = np.eye(P)
    c["headones"] = (row_head[:, None] == row_head[None, :]) * 1.0
    c["ones"] = np.ones((P, P))
    c["eps"] = np.tile(np.array([EPS, LN_EPS]), (P, 1))
    half = HD // 2
    swap = np.where(i % HD < half, i + half, i - half)
    c["swap"] = (swap[:, None] == i[None, :]) * 1.0
    inv = (1.0 / (np.float32(10000.0) ** (np.arange(half, dtype=np.float32) * np.float32(2.0) / np.float32(HD)))).astype(np.float32)
    ang = (np.arange(T, dtype=np.float32)[None, :] * inv[i % half][:, None]).astype(np.float32)
    c["cos"] = np.cos(ang)
    c["sin"] = np.where((i % HD < half)[:, None], -np.sin(ang), np.sin(ang))
    lg = np.log1p(-np.power(2.0, -5.0 - np.arange(8)))
    head = 2 * np.arange(4)[None, :] + row_head[:, None]
    c["xi"] = np.exp(lg[head][:, :, None] * (i[None, None, :] + 1.0))
    diff = i[None, :] - i[:, None]
    dm = np.where(diff >= 0, np.exp(lg[:, None, None] * np.maximum(diff, 0)), 0.0) * HD ** -0.5
    c["dmat"] = np.stack([dm[p::2].transpose(1, 0, 2) for p in range(2)], 1)
    c["zeta"] = np.exp(lg[None, :] * (P - 1.0 - i[:, None])) * HD ** -0.5
    c["cdecay"] = np.exp(lg[head] * P)
    same = (i[:, None] // CH) == (i[None, :] // CH)
    strict, incl = same & (diff > 0), same & (diff >= 0)
    c["rwmask"] = np.stack([strict, incl, strict, incl], 1)
    lev = [(i[:, None] // (2 * m) == i[None, :] // (2 * m)) & (i[:, None] % (2 * m) < m) & (i[None, :] % (2 * m) >= m)
           for m in (1, 2, 4, 8, 16, 32, 64)]
    c["lev"] = np.stack(lev[:6], 1)
    c["hgmask"] = np.stack(lev + [np.eye(P, dtype=bool)], 1).astype(np.uint32)
    t = np.arange(T)
    c["reset64"] = np.tile((t % CH != 0) * 1.0, (P, 1))
    c["reset128"] = np.tile((t % P != 0) * 1.0, (P, 1))
    si = np.arange(2 * P)
    rel = i[:, None] + P - si[None, :]
    ok = [(rel >= 0) & (rel < P) & (n * P + si[None, :] - P >= 0) for n in range(NT)]
    c["atmask"] = np.where(np.stack(ok, 1), 0.0, -1e30)
    win = np.array([[2, 4], [8, 16]])[:, row_head].T
    c["invcnt"] = 1.0 / np.minimum(t[None, None, :] + 1.0, win[:, :, None])
    c["causal"] = (diff >= 0) * 1.0
    return {k: np.ascontiguousarray(v if v.dtype == np.uint32 else v.astype(np.float32)) for k, v in c.items()}


KEEP = [("ident", (P,)), ("headones", (P,)), ("ones", (P,)), ("eps", (2,)), ("gains", (9, DC)), ("vec2", (V_N,))]
FIRST = [("hgmask", (8, P)), ("reset128", (T,)), ("invcnt", (2, T)), ("causal", (P,)), ("vec1", (U_N,)),
         ("wa", (2, P)), ("wx", (2, P)), ("dw", (2, P)), ("ws", (4, P)), ("lng", (2 * P,)), ("lnb", (2 * P,)),
         ("bs", (2, P))]
RWKV = [("w2", (4, P)), ("a2", (4, P)), ("g2", (4, P)), ("rwmask", (4, P)), ("lev", (6, P)), ("reset64", (T,))]
RETAT = [("swap", (P,)), ("cos", (T,)), ("sin", (T,)), ("xi", (4, P)), ("dmat", (2, 4, P)), ("zeta", (8,)), ("cdecay", (4,)),
         ("atmask", (NT, 2 * P))]


def build(nc, dram, out):
    ctx = ExitStack()
    with ctx:
        at = [16512]

        def place(name, shape, dt=F32, offset=None):
            n = 4 * int(np.prod(shape))
            if offset is None:
                offset = at[0]
                at[0] += (n + 31) // 32 * 32
            return nc.alloc_sbuf_tensor_at(name, [P, *shape], dt, offset=offset), offset

        x, _ = place("x", (DC, T))
        xg_hi, _ = place("xg_hi", (DC, T), F32R)
        xg_lo, _ = place("xg_lo", (DC, T), F32R)
        junk, _ = place("junk", (1,))
        raw, _ = place("raw", (2, DC * P))
        w_hi, _ = place("w_hi", (2, DC * P), F32R)
        w_lo, _ = place("w_lo", (2, DC * P), F32R)
        rstd, _ = place("rstd", (T,))
        sumsq, sumsq_at = place("sumsq", (T,))
        K = {}
        for name, shape in KEEP:
            K[name], _ = place(name, shape)
        base = at[0]

        for name, shape in FIRST:
            K[name], _ = place(name, shape, U32 if name == "hgmask" else F32)
        z, _ = place("z", (18, T))
        y_hi, _ = place("y_hi", (DC, T), F32R)
        y_lo, _ = place("y_lo", (DC, T), F32R)
        m1 = {}
        for name, shape in (("ta", (2, T)), ("tb", (2, T)), ("tc", (2, T)), ("td", (2, T + 16)), ("te", (2, T)), ("tf", (2, T)),
                            ("tg", (2, T)), ("th", (2, T))):
            m1[name], _ = place("m1_" + name, shape)
        att, _ = place("att", (2, 2, 4, P))
        sml, _ = place("sml", (64,))
        S1, _ = place("S1", (2, P))
        assert at[0] <= 229376, at[0]

        at[0] = base
        for name, shape in RWKV:
            K[name], _ = place(name, shape)
        end = at[0]
        at[0] = base
        for name, shape in RETAT:
            K[name], _ = place(name, shape)
        at[0] = max(end, at[0])
        z_rw, rw_at = place("z_rw", (14, T))
        z_rt, rt_at = place("z_rt", (16, T))
        scratch = at[0]
        C4 = 4 * 4 * T
        y1_hi, _ = place("y1_hi", (4, T), F32R, offset=rw_at)
        y1_lo, _ = place("y1_lo", (4, T), F32R, offset=rw_at + C4)
        z_at, _ = place("z_at", (6, T), offset=rw_at + 2 * C4)
        y2_hi, _ = place("y2_hi", (4, T), F32R, offset=rt_at)
        y2_lo, _ = place("y2_lo", (4, T), F32R, offset=rt_at + C4)
        hid_hi, _ = place("hid_hi", (DC, T), F32R, offset=rt_at)
        hid_lo, _ = place("hid_lo", (DC, T), F32R, offset=rt_at + 2 * C4)
        emb_at = base + 24 * 1024
        emb_hi, _ = place("emb_hi", (2, T), F32R, offset=emb_at)
        emb_lo, _ = place("emb_lo", (2, T), F32R, offset=emb_at + C4 // 2)
        emb, _ = place("emb", (2, T), F32, offset=emb_at + C4)
        assert emb_at + 3 * C4 // 2 <= rt_at and base + 4 * sum(int(np.prod(shape)) for _, shape in FIRST) <= emb_at

        rw = {}
        for name, shape in (("AR", (4, 2, P)), ("bon", (4, P)), ("sq", (4, P)), ("tokB", (T,)),
                            ("tokK", (T,)), ("tokV", (T,)), ("tokA", (T,)), ("W", (T,)), ("U", (T,)), ("S", (4, P)),
                            ("pc", (4, 2))):
            rw[name], _ = place("rw_" + name, shape)
        lo_at, hi_at = at[0], at[0] + 2 * C4
        for k, name in enumerate(("kp", "b", "kk", "Lr", "Lp", "Dl", "eP", "eM")):
            rw[name], _ = place("rw_" + name, (4, P), offset=lo_at + 4 * T * k)
        rw["SC"], _ = place("rw_SC", (8, 4, P), offset=lo_at)
        for k, name in enumerate(("G", "Y", "X", "TL")):
            rw[name], _ = place("rw_" + name, (8, P), offset=hi_at + 4 * T * 2 * k)
        for k, name in enumerate(("BT", "KT", "BH", "KH", "VT")):
            rw[name], _ = place("rw_" + name, (4, P), offset=hi_at + 4 * T * (2 + k))
        assert hi_at + 2 * C4 <= 229376, hi_at

        at[0] = scratch
        mixed, _ = place("mixed", (DC, T))
        ffn = {}
        for name in ("sq", "t", "act", "h"):
            ffn[name], h_at = place("ffn_" + name, (T,))
        mixer = at[0]
        for name, shape in (("pad", (2, T + 2)), ("cv", (2, T))):
            ffn[name], _ = place("ffn_" + name, shape)

        rstd_fin, sumsq_fin = ffn["cv"][:, 0, :], ffn["cv"][:, 1, :]
        at[0] = mixer
        rt = {}
        for name, shape in (("t1", (4, P)), ("t2", (4, P)), ("qr", (4, P)), ("kr", (4, P)), ("qx", (4, P)),
                            ("kz", (T,)), ("vt", (T,)), ("R", (4, P)), ("o", (4, P)), ("ST", (2, 4, P)), ("sq", (4, P)),
                            ("gs", (4, P))):
            rt[name], _ = place("rt_" + name, shape)
        end_rt = at[0]

        at[0] = mixer
        an = {}
        an["q"], _ = place("an_q", (4, P), offset=h_at)
        an["kw"], _ = place("an_kw", (2, 2 * P), offset=sumsq_at)
        for name, shape in (("v", (2, P)), ("s", (2, 4, 2 * P)), ("pT", (8, 2, P)), ("o", (4, P)), ("mx", (8,)),
                            ("nm", (8,)), ("sum", (8,)), ("es", (8,))):
            an[name], _ = place("an_" + name, shape)
        at[0] = max(end_rt, at[0])
        an["k"], _ = place("an_k", (2, P + T))
        assert at[0] <= 229376, at[0]
        at[0] = mixer
        an["rs"], _ = place("an_rs", (4, T))
        an["sq"], _ = place("an_sq", (5, T))
        assert at[0] <= end_rt, at[0]

        acc = [ctx.enter_context(nc.psum_tensor(f"acc{s}", [P, T], F32)) for s in range(2)]
        bank = [ctx.enter_context(nc.psum_tensor(f"bank{s}", [P, T], F32)) for s in range(6)]

        def sem(name):
            return ctx.enter_context(nc.semaphore(name))

        raw_in = [sem(f"raw_in{s}") for s in range(2)]
        w_split = [sem(f"w_split{s}") for s in range(2)]
        hi_done = [sem(f"hi_done{s}") for s in range(2)]
        slot_done = [sem(f"slot_done{s}") for s in range(2)]
        acc_free = [sem(f"acc_free{s}") for s in range(2)]
        keep_in, first_in, layer_in, retat_in = sem("keep_in"), sem("first_in"), sem("layer_in"), sem("retat_in")
        sumsq_ready, stat_ready, root_ready = sem("sumsq_ready"), sem("stat_ready"), sem("root_ready")
        xg_ready, hid_ready = sem("xg_ready"), sem("hid_ready")
        y_ready, x_in, squared = sem("y_ready"), [sem(f"x_in{c}") for c in range(DC)], sem("squared")
        h_pre, h_act = sem("h_pre"), sem("h_act")
        x_final, stored = sem("x_final"), sem("stored")
        pool_turn, act_turn, pe_turn, dve_turn = sem("pool_turn"), sem("act_turn"), sem("pe_turn"), sem("dve_turn")
        s1 = {n: sem("b1_" + n) for n in (
            "z", "vT", "iev", "act1", "vn", "wm", "sv", "conv", "ri", "sig", "la", "ea", "mlt", "scan", "hx", "hl", "lf", "lv",
            "ex", "qk", "sc", "scev", "kh", "khT", "khv", "o", "kv", "st", "on", "os", "osq", "pool", "dwy", "sqr",
            "gel", "sil")}
        s2 = {n: sem("rw_" + n) for n in (
            "z", "lora_in", "lora", "pre", "sig", "kkr", "nrm_in", "nrm", "rn", "root", "L", "exp", "opk", "ops", "tr", "tok",
            "sc", "scev", "g1", "x", "xev", "tl", "y", "yi", "g", "gev", "xt", "w", "wev", "ah", "ahev", "u", "uev", "sread", "st", "stev", "yo",
            "ysb", "ysum", "yc", "ysq", "yvar", "yroot", "done")}
        s3 = {n: sem("rt_" + n) for n in (
            "z", "sw", "vf", "vT", "rot", "sc", "st", "ktr", "kz", "vt", "o", "rev", "osb", "osum", "root", "silu", "done")}
        s4 = {n: sem("an_" + n) for n in (
            "sq", "ss", "root", "kn", "qc", "sc", "mx", "p", "pn", "pT", "pTe", "o", "done")}
        o_gate, o_sig = sem("o_gate"), sem("o_sig")
        load_wait = 16

        def bc(ap, n):
            return ap.unsqueeze(2).to_broadcast([ap.shape[0], ap.shape[1], n])

        def mid(ap, n):
            return ap.unsqueeze(1).to_broadcast([ap.shape[0], n, ap.shape[1]])

        def r3(ap, k):
            return ap.rearrange("p (a b) -> p a b", a=k)

        def bits(ap):
            return ap.bitcast(F32)

        def tile_of(t, a, k, n):
            return t[:, a:a + k, bass.ts(n, P)]

        block = ctx.enter_context(nc.Block())

        @block.sync
        def _(sp):
            def load(pairs, names, I0, index=None, from_pair=0):
                def one(i):
                    for s in range(2):
                        src = dram[names[s]] if index is None else dram[names[s]][index]
                        n = src.shape[-1]
                        sp.wait_ge(w_split[s], I0 + i + 1)
                        sp.sem_inc(pe_turn, 1)
                        sp.dma_start(raw[:, s, 0:n], src[i + from_pair, s] if len(src.shape) == 4 else src[i + from_pair]).then_inc(raw_in[s], 16)
                with sp.Fori(0, pairs) as i:
                    one(i)

            for name, _ in KEEP[:-1]:
                sp.dma_start(K[name][:], dram[name]).then_inc(keep_in, 16)
            I = 0
            for c in range(DC):
                if c == 2:
                    load(1, ("w1_in", "w1_in"), I)
                sp.dma_start(x[:, c, :], dram["x"][c]).then_inc(x_in[c], 16)
            load(1, ("w1_in", "w1_in"), I + 1, from_pair=1)
            for name, _ in FIRST:
                sp.dma_start(K[name][:], dram[name]).then_inc(first_in, 16)
            load(B1_IN - 2, ("w1_in", "w1_in"), I + 2, from_pair=2); I += B1_IN
            load(X_OUT, ("w1_out", "w1_out"), I); I += X_OUT
            sp.dma_start(emb[:], dram["p"]).then_inc(first_in, 16)
            for k, n in enumerate(PARTS):
                load(n, (f"w1_up{k}",) * 2, I); I += n
                load(X_OUT, (f"w1_down{k}",) * 2, I); I += X_OUT
            load(PE_PAIRS, ("w1_pg", "w1_pe"), I); I += PE_PAIRS
            with sp.Fori(0, LAYERS) as l:
                I = B1_PAIRS + l * LAYER_PAIRS
                sp.dma_start(K["vec2"][:], dram["vec2"][l]).then_inc(layer_in, 16)
                for name, _ in RWKV:
                    sp.dma_start(K[name][:], dram[name][l] if len(dram[name].shape) > 1 + len(dict(RWKV)[name]) else dram[name]).then_inc(layer_in, 16)
                for n, name in ((RW_PAIRS, "w2_rw"), (RET_PAIRS, "w2_ret"), (AT_PAIRS, "w2_at")):
                    load(n, (name, name), I, l); I = I + n
                sp.wait_ge(s2["done"], l * NT + NT)
                sp.sem_inc(pe_turn, 1)
                for name, _ in RETAT:
                    sp.dma_start(K[name][:], dram[name]).then_inc(retat_in, 16)
                load(O_PAIRS, ("w2_gate", "w2_o"), I, l); I = I + O_PAIRS
                load(X_OUT, ("w2_out", "w2_out"), I, l); I = I + X_OUT
                for k, n in enumerate(PARTS):
                    load(n, (f"w2_up{k}",) * 2, I, l); I = I + n
                    load(X_OUT, (f"w2_down{k}",) * 2, I, l); I = I + X_OUT
            for c in range(DC):
                sp.wait_ge(x_final, DC * (LAYERS - 1) + c + 1)
                sp.dma_start(out[c], x[:, c, :]).then_inc(stored, 16)
            sp.wait_ge(stored, 16 * DC)

        @block.gpsimd
        def _(pool):
            for s in range(2):
                pool.sem_inc(w_split[s], 1)

            def split(pairs, widths, I0):
                with pool.Fori(0, pairs) as i:
                    for s in range(2):
                        n = widths[s] * P
                        pool.wait_ge(raw_in[s], 16 * (I0 + i + 1))
                        pool.wait_ge(hi_done[s], I0 + i + 1)
                        pool.sem_inc(pool_turn, 1)
                        nc.gpsimd.tensor_scalar(w_hi[:, s, 0:n], raw[:, s, 0:n], 1.0, 0.0, ALU.mult, ALU.add)
                        pool.wait_ge(slot_done[s], I0 + i + 1)
                        pool.sem_inc(pool_turn, 1)
                        pool.drain()
                        nc.gpsimd.tensor_tensor(w_lo[:, s, 0:n], raw[:, s, 0:n], bits(w_hi[:, s, 0:n]),
                                                ALU.subtract).then_inc(w_split[s], 1)

            def ffn_split(I):
                for n in PARTS:
                    split(n, (DC, DC), I); I = I + n
                    split(X_OUT, (n, n), I); I = I + X_OUT
                return I

            split(B1_IN + X_OUT, (DC, DC), 0)
            I = ffn_split(B1_IN + X_OUT)
            split(PE_PAIRS, (DC, 2), I)
            with pool.Fori(0, LAYERS) as l:
                I = B1_PAIRS + l * LAYER_PAIRS
                split(RW_PAIRS + RET_PAIRS + AT_PAIRS, (DC, DC), I); I = I + RW_PAIRS + RET_PAIRS + AT_PAIRS
                split(O_PAIRS, (DC, 4), I); I = I + O_PAIRS
                split(X_OUT, (DC, DC), I); I = I + X_OUT
                ffn_split(I)

        @block.tensor
        def _(pe):
            for s in range(2):
                pe.sem_inc(slot_done[s], 1)
                pe.sem_inc(hi_done[s], 1)

            def mm(o, a, b, first, last, shared=False):
                return nc.tensor.matmul(o, a, b, start=first, stop=last, skip_group_check=shared)

            def slot(s, I, a, chunks):
                hi, lo = a
                pe.wait_ge(w_split[s], I + 2)
                pe.wait_ge(acc_free[s], I + 1)
                pe.sem_inc(pe_turn, 1)
                n = len(chunks)
                for m, v in ((0, hi), (0, lo), (1, hi)):
                    w = (w_hi, w_lo)[m]
                    for k, c in enumerate(chunks):
                        last = mm(acc[s][:], w[:, s, k * P:(k + 1) * P], v[:, c, :], v is hi and m == 0 and k == 0, m == 1 and k == n - 1)
                    if v is lo:
                        last.then_inc(hi_done[s], 1)
                last.then_inc(slot_done[s], 1)

            def late(s, I, a, chunks, ready, count, order=None):
                pe.wait_ge(w_split[s], I + 2)
                pe.wait_ge(acc_free[s], I + 1)
                pe.sem_inc(pe_turn, 1)
                n = len(chunks)
                for i, k in enumerate(order or range(n)):
                    w, c = slice(k * P, (k + 1) * P), chunks[k]
                    pe.wait_ge(ready, count + i + 1)
                    pe.sem_inc(pe_turn, 1)
                    mm(acc[s][:], w_hi[:, s, w], a[0][:, c, :], i == 0, False)
                    last_hi = mm(acc[s][:], w_hi[:, s, w], a[1][:, c, :], False, False)
                    last = mm(acc[s][:], w_lo[:, s, w], a[0][:, c, :], False, i == n - 1)
                last_hi.then_inc(hi_done[s], 1)
                last.then_inc(slot_done[s], 1)

            def normed(pairs, I, count, stat):
                late(0, I, xg, full, xg_ready, count)
                stats(stat)
                slot(1, I, xg, full)
                slots(pairs - 1, I + 1, xg, full)

            def hid_slots(I, n, count):
                late(0, I, hid, range(n), hid_ready, count)
                slot(1, I, hid, range(n))
                slots(X_OUT - 1, I + 1, hid, range(n))

            def slots(pairs, I0, a, chunks):
                with pe.Fori(0, pairs) as i:
                    for s in range(2):
                        slot(s, I0 + i, a, chunks)

            xg, hid, yy, em = (xg_hi, xg_lo), (hid_hi, hid_lo), (y_hi, y_lo), (emb_hi, emb_lo)
            y1, y2, four = (y1_hi, y1_lo), (y2_hi, y2_lo), range(4)
            full = range(DC)

            def stats(count):
                pe.wait_ge(sumsq_ready, count)
                pe.sem_inc(pe_turn, 1)
                mm(bank[5][:], K["ones"][:], sumsq[:], True, True).then_inc(stat_ready, 1)

            def feed_forward(I, hid0, xg0, stat):
                for k, n in enumerate(PARTS):
                    if k == 0:
                        normed(n, I, xg0, stat)
                    else:
                        slots(n, I, xg, full)
                    I = I + n
                    hid_slots(I, n, hid0 + sum(PARTS[:k])); I = I + X_OUT
                return I

            def head_sums(o, v):
                return mm(o, K["headones"][:], v, True, True)

            pe.wait_ge(keep_in, load_wait * (len(KEEP) - 1))
            late(0, 0, xg, full, xg_ready, 0)
            stats(1)
            slot(1, 0, xg, full)

            def pair(i):
                for s in range(2):
                    slot(s, i, xg, full)

            def transposed(b, src):
                for n in range(NT):
                    for c in range(2):
                        last = nc.tensor.transpose(bank[b + n // 2][:, (2 * (n % 2) + c) * P:(2 * (n % 2) + c + 1) * P],
                                                   src[:, c, n * P:(n + 1) * P], K["ident"][:])
                last.then_inc(s1["vT"], 1)

            pair(1)
            pair(2)
            pe.wait_ge(first_in, load_wait * len(FIRST))
            pe.wait_ge(s1["conv"], 1)
            for k, name in enumerate(("wa", "wx")):
                for j in range(2):
                    last = mm(bank[2 + 2 * k + j][:], K[name][:, j, :], m1["ta"][:, j, :], True, True)
            last.then_inc(s1["ri"], 1)
            pair(3)
            pe.wait_ge(s1["z"], 3)
            transposed(0, m1["tg"])
            pair(4)
            pair(5)
            pe.wait_ge(s1["vn"], 1)
            pe.wait_ge(s1["wm"], 1)
            vtok = z[:, 14:16, :].rearrange("p a b -> p (a b)").rearrange("p (n c) -> p n c", n=NT)
            for j in range(2):
                for n in range(NT):
                    for p in range(2):
                        h = 2 * j + p
                        last = mm(bank[j][p * HD:(p + 1) * HD, n * P:(n + 1) * P], vtok[:, n, h * HD:(h + 1) * HD],
                                  K["ws"][:, h, :], True, True)
            last.then_inc(s1["sv"], 1)
            pair(6)
            pe.wait_ge(s1["z"], 7)
            pe.wait_ge(s1["sig"], 1)
            transposed(4, m1["th"])
            pair(7)
            pair(8)
            count = 0
            for lev in range(8):
                pe.wait_ge(s1["qk"], lev + 1)
                for half in range(2):
                    if count >= 2:
                        pe.wait_ge(s1["scev"], count - 1)
                    elif count == 0:
                        pe.wait_ge(s1["gel"], 1)
                    for p in range(2):
                        for tile in range(2):
                            for j in range(2):
                                sl = slice((2 * half + tile) * P, (2 * half + tile + 1) * P)
                                r = slice(p * HD, (p + 1) * HD)
                                kk, qq = (m1[("tc", "th")[lev % 2]], m1[("tb", "tg")[lev % 2]]) if lev < 7 else (m1["te"], z[:, 6:8, :])
                                last = mm(bank[2 * (count % 2) + p][:, (2 * tile + j) * P:(2 * tile + j + 1) * P],
                                          kk[r, j, sl], qq[r, j, sl], True, True)
                    last.then_inc(s1["sc"], 1)
                    count += 1
            pe.wait_ge(s1["kh"], 1)
            pe.wait_ge(s1["scev"], 16)
            for n in range(NT):
                for j in range(2):
                    o = bank[n // 2][:, (2 * (n % 2) + j) * P:(2 * (n % 2) + j + 1) * P]
                    last = nc.tensor.transpose(o, m1["tb"][:, j, n * P:(n + 1) * P], K["ident"][:])
            last.then_inc(s1["khT"], 1)
            pe.wait_ge(s1["khv"], 1)
            pe.wait_ge(s1["iev"], 1)
            itok = z[:, 16:18, :].rearrange("p (s t) c -> p s (t c)", s=1)[:, 0, :].rearrange("p (n c) -> p n c", n=NT)
            khtok = m1["tc"][:].rearrange("p (s t) c -> p s (t c)", s=1)[:, 0, :].rearrange("p (n c) -> p n c", n=NT)
            for n in range(NT):
                if n == 1:
                    pe.wait_ge(s1["pool"], 1)
                    for j in range(2):
                        last = mm(bank[4 + j][:], K["dw"][:, j, :], m1["th"][:, j, :], True, True)
                    last.then_inc(s1["dwy"], 1)
                pe.wait_ge(s1["st"], n + 1)
                for j in range(2):
                    sl = slice(n * P, (n + 1) * P)
                    mm(bank[2 + j][:, sl], S1[:, j, :], m1["tf"][:, j, sl], n == 0, False, True)
                    for p in range(2):
                        h = 2 * j + p
                        last = mm(bank[2 + j][p * HD:(p + 1) * HD, sl], itok[:, n, h * HD:(h + 1) * HD],
                                  att[:, n // 2, p, 2 * (n % 2) + j, :], False, True, True)
                for j in range(2):
                    last = mm(bank[n % 2][:, j * P:(j + 1) * P], khtok[:, n, j * P:(j + 1) * P],
                              itok[:, n, j * P:(j + 1) * P], True, True)
                last.then_inc(s1["kv"], 1)
            pe.wait_ge(s1["osq"], 1)
            for j in range(2):
                last = head_sums(bank[j][:], m1["ta"][:, j, :])
            last.then_inc(s1["on"], 1)
            late(0, B1_IN, yy, full, y_ready, 0, (0, 1, 2, 3, 6, 7, 4, 5))
            slot(1, B1_IN, yy, full)
            slots(X_OUT - 1, B1_IN + 1, yy, full)
            I = feed_forward(B1_IN + X_OUT, 0, DC, 2)
            late(0, I, xg, full, xg_ready, 2 * DC)
            stats(3)
            slot(1, I, em, range(2))
            with pe.Fori(1, PE_PAIRS) as i:
                slot(0, I + i, xg, full)
                slot(1, I + i, em, range(2))
            stats(4)
            with pe.Fori(0, LAYERS) as l:
                I = B1_PAIRS + l * LAYER_PAIRS
                normed(RW_PAIRS, I, DC * (2 * l + 3), 2 * l + 5); I = I + RW_PAIRS
                pe.wait_ge(s2["lora_in"], l + 1)
                pe.sem_inc(pe_turn, 1)
                pe.wait_ge(layer_in, load_wait * (1 + len(RWKV)) * (l + 1))
                pe.sem_inc(pe_turn, 1)
                with pe.Fori(0, NT) as n:
                    it, F = l * NT + n, I + 2 * n

                    def after(name, k, per=1):
                        pe.wait_ge(s2[name], it * per + k)
                        pe.sem_inc(pe_turn, 1)

                    for j in range(4):
                        mm(bank[0][:, j * P:(j + 1) * P], K["w2"][:, j, :], z_rw[:, 12, bass.ts(n, P)], True, True)
                        mm(bank[1][:, j * P:(j + 1) * P], K["a2"][:, j, :], z_rw[:, 12, bass.ts(n, P)], True, True)
                        last = mm(bank[2][:, j * P:(j + 1) * P], K["g2"][:, j, :], z_rw[:, 13, bass.ts(n, P)], True, True)
                    last.then_inc(s2["lora"], 1)
                    slot(0, F, xg, full)
                    slot(1, F, xg, full)
                    after("nrm_in", 1)
                    head_sums(bank[0][:], rw["sq"][:].rearrange("p a b -> p (a b)"))
                    head_sums(bank[1][:], rw["bon"][:].rearrange("p a b -> p (a b)")).then_inc(s2["nrm"], 1)
                    slot(0, F + 1, xg, full)
                    after("opk", 1)
                    for src, b in (("KH", 1), ("VT", 2), ("BH", 0)):
                        if src == "BH":
                            slot(1, F + 1, xg, full)
                            after("ops", 1)
                        for j in range(4):
                            nc.tensor.transpose(bank[b][:, j * P:(j + 1) * P], rw[src][:, j, :], K["ident"][:])
                    for j in range(4):
                        last = nc.tensor.transpose(bank[5][:, j * P:(j + 1) * P], rw["AR"][:, j, 0, :], K["ident"][:])
                    last.then_inc(s2["tr"], 1)
                    for h in range(8):
                        j, p = h // 2, h % 2
                        r = slice(p * HD, (p + 1) * HD)
                        b = bank[3 + p]
                        if h >= 2:
                            after("scev", h - 1, 8)
                        ar = rw["AR"][r, j, :, :].rearrange("p a b -> p (a b)")
                        mm(b[:, 0:2 * P], rw["BT"][r, j, :], ar, True, True)
                        mm(b[:, 2 * P:4 * P], rw["KT"][r, j, :], ar, True, True).then_inc(s2["sc"], 1)
                    after("tok", 1)
                    for h in range(8):
                        if h % 4 == 0:
                            after("g1", h // 4 + 1, 2)
                        last = nc.tensor.transpose(bank[h // 4][:, (h % 4) * P:(h % 4 + 1) * P], rw["G"][:, h, :], K["ident"][:])
                        if h % 4 == 3:
                            last.then_inc(s2["x"], 1)
                    for lev in range(1, 6):
                        after("tl", lev, 5)
                        for half in range(2):
                            if lev == 1:
                                after("xev", half + 1, 2)
                            else:
                                after("xt", 2 * (lev - 2) + half + 1, 8)
                            for h in range(4 * half, 4 * half + 4):
                                last = mm(bank[3 + half][:, (h % 4) * P:(h % 4 + 1) * P], rw["TL"][:, h, :], rw["X"][:, h, :], True, True)
                            last.then_inc(s2["y"], 1)
                        for half in range(2):
                            if lev > 1:
                                after("gev", 2 * (lev - 2) + half + 1, 10)
                            after("yi", 2 * (lev - 1) + half + 1, 10)
                            for h in range(4 * half, 4 * half + 4):
                                last = mm(bank[(2, 5)[half]][:, (h % 4) * P:(h % 4 + 1) * P], rw["Y"][:, h, :], rw["G"][:, h, :], True, True)
                            last.then_inc(s2["g"], 1)
                    for h in range(8):
                        last = mm(bank[3][:, h * HD:(h + 1) * HD], rw["SC"][:, h, 2, :], rw["tokV"][:, h * HD:(h + 1) * HD], True, True)
                    last.then_inc(s2["w"], 1)
                    after("gev", 10, 10)
                    for h in range(8):
                        j, p = h // 2, h % 2
                        last = mm(bank[5][p * HD:(p + 1) * HD, j * P:(j + 1) * P], rw["tokA"][:, h * HD:(h + 1) * HD], rw["G"][:, h, :], True, True)
                    last.then_inc(s2["ah"], 1)
                    after("wev", 1)
                    for c in range(2):
                        cs, ub = slice(c * CH, (c + 1) * CH), bank[(4, 3)[c]]
                        for h in range(8):
                            mm(ub[cs, h * HD:(h + 1) * HD], rw["G"][:, h, cs], rw["W"][:, h * HD:(h + 1) * HD], h == 0, False, True)
                        if c == 0:
                            after("ahev", 1)
                        after("stev", c + 1, 3)
                        for j in range(4):
                            last = mm(ub[cs, j * P:(j + 1) * P], rw["bon"][:, j, cs], rw["S"][:, j, :], False, j == 3, True)
                        last.then_inc(s2["u"], 1)
                        for j in range(4):
                            last = mm(bank[0][:, j * P + c * CH:j * P + (c + 1) * CH], rw["S"][:, j, :], rw["AR"][:, j, 1, cs],
                                      c == 0 and j == 0, False, True)
                        last.then_inc(s2["sread"], 1)
                        if c == 0:
                            for h in range(8):
                                j, p = h // 2, h % 2
                                mm(bank[0][p * HD:(p + 1) * HD, j * P:(j + 1) * P], rw["tokV"][:, h * HD:(h + 1) * HD], rw["SC"][:, h, 3, :],
                                   False, False, True)
                        after("uev", c + 1, 2)
                        for j in range(4):
                            js = slice(j * P, (j + 1) * P)
                            mm(bank[1][:, js], rw["tokB"][cs, js], rw["U"][cs, js], True, False)
                            last = mm(bank[1][:, js], rw["tokK"][cs, js], rw["tokV"][cs, js], False, True)
                        last.then_inc(s2["st"], 1)
                    for h in range(8):
                        j, p = h // 2, h % 2
                        o = bank[0][p * HD:(p + 1) * HD, j * P:(j + 1) * P]
                        last = mm(o, rw["U"][:, h * HD:(h + 1) * HD], rw["SC"][:, h, 1, :], False, h == 7, True)
                    last.then_inc(s2["yo"], 1)
                    after("ysb", 1)
                    head_sums(r3(bank[2][:], 4), tile_of(z_rw, 4, 4, n)).then_inc(s2["ysum"], 1)
                    after("ysq", 1)
                    head_sums(bank[5][:], rw["U"][:]).then_inc(s2["yvar"], 1)
                I = I + RET_PAIRS
                for i in range(AT_PAIRS):
                    slot(0, I + i, xg, full)
                    if i > 0:
                        pe.wait_ge(s4["sq"], AT_PAIRS * l + i)
                        pe.sem_inc(pe_turn, 1)
                        for c in range(2 * i - 2, 2 * i):
                            last = head_sums(bank[c][:], an["sq"][:, c, :])
                        last.then_inc(s4["ss"], 1)
                    slot(1, I + i, xg, full)
                I = I + AT_PAIRS
                pe.wait_ge(s4["sq"], AT_PAIRS * l + AT_PAIRS)
                pe.sem_inc(pe_turn, 1)
                head_sums(bank[4][:], an["sq"][:, 4, :])
                for n in range(NT):
                    last = nc.tensor.transpose(bank[5][:, n * P:(n + 1) * P], z_at[:, 5, n * P:(n + 1) * P], K["ident"][:])
                last.then_inc(s4["ss"], 1)
                pe.wait_ge(s4["root"], AT_PAIRS * l + 2)
                pe.sem_inc(pe_turn, 1)
                pe.wait_ge(s2["done"], l * NT + NT)
                pe.sem_inc(pe_turn, 1)
                pe.wait_ge(retat_in, load_wait * len(RETAT) * (l + 1))
                pe.sem_inc(pe_turn, 1)
                with pe.Fori(0, NT) as n:
                    it, F = l * NT + n, I + 2 * n

                    def after(name, k, per=1):
                        pe.wait_ge(s3[name], it * per + k)
                        pe.sem_inc(pe_turn, 1)

                    pe.wait_ge(s3["z"], l + 1)
                    after("rev", 1, 2)
                    mm(bank[0][:], K["swap"][:], tile_of(z_rt, 0, 4, n), True, True)
                    mm(bank[1][:], K["swap"][:], tile_of(z_rt, 4, 4, n), True, True).then_inc(s3["sw"], 1)
                    after("vf", 1)
                    pe.wait_ge(s4["root"], AT_PAIRS * l + AT_PAIRS)
                    pe.sem_inc(pe_turn, 1)
                    for j in range(4):
                        last = nc.tensor.transpose(bank[5][:, j * P:(j + 1) * P], rt["o"][:, j, :], K["ident"][:])
                    last.then_inc(s3["vT"], 1)
                    slot(0, F, xg, full)
                    after("rot", 1)
                    for p in range(2):
                        r = slice(p * HD, (p + 1) * HD)
                        for j in range(4):
                            mm(bank[2 + p][:, j * P:(j + 1) * P], rt["kr"][r, j, :], rt["qr"][r, j, :], True, True)
                    for j in range(4):
                        last = nc.tensor.transpose(bank[4][:, j * P:(j + 1) * P], rt["kr"][:, j, :], K["ident"][:])
                    last.then_inc(s3["sc"], 1)
                    slot(1, F, y1, four)
                    after("kz", 1)
                    after("vt", 1)
                    for j in range(4):
                        js = slice(j * P, (j + 1) * P)
                        mm(bank[0][:, js], rt["R"][:, j, :], rt["qx"][:, j, :], j == 0, False, True)
                    for h in range(8):
                        j, p = h // 2, h % 2
                        mm(bank[0][p * HD:(p + 1) * HD, j * P:(j + 1) * P], rt["vt"][:, h * HD:(h + 1) * HD],
                           rt["ST"][:, p, j, :], False, h == 7, True)
                    for j in range(4):
                        js = slice(j * P, (j + 1) * P)
                        last = mm(bank[1][:, js], rt["kz"][:, js], rt["vt"][:, js], True, True)
                    last.then_inc(s3["o"], 1)
                    after("osb", 1)
                    head_sums(bank[5][:], rt["sq"][:].rearrange("p a b -> p (a b)")).then_inc(s3["osum"], 1)
                    slot(0, F + 1, xg, full)
                    slot(1, F + 1, y1, four)
                I = I + 2 * NT
                pe.wait_ge(s3["rev"], 2 * (l * NT + NT))
                pe.sem_inc(pe_turn, 1)
                with pe.Fori(0, NT) as n:
                    it, F = l * NT + n, I + 2 * n

                    def after(name, k, per=1):
                        pe.wait_ge(s4[name], it * per + k)
                        pe.sem_inc(pe_turn, 1)

                    after("qc", 1)
                    for p in range(2):
                        r = slice(p * HD, (p + 1) * HD)
                        for j in range(4):
                            last = mm(bank[2 * p + j // 2][:, (j % 2) * 2 * P:(j % 2 + 1) * 2 * P], an["q"][r, j, :],
                                      an["kw"][r, j // 2, :], True, True)
                        last.then_inc(s4["sc"], 1)
                    slot(0, F, xg, full)
                    pe.wait_ge(s3["done"], l * NT + NT)
                    pe.sem_inc(pe_turn, 1)
                    slot(1, F, y2, four)
                    slot(0, F + 1, xg, full)
                    for p in range(2):
                        after("pn", p + 1, 2)
                        for j in range(4):
                            for b in range(2):
                                last = nc.tensor.transpose(bank[2 * p + j // 2][:, (2 * (j % 2) + b) * P:(2 * (j % 2) + b + 1) * P],
                                                           an["s"][:, p, j, b * P:(b + 1) * P], K["ident"][:])
                        last.then_inc(s4["pT"], 1)
                    slot(1, F + 1, y2, four)
                    after("pTe", 1)
                    for h in range(8):
                        j, p = h // 2, h % 2
                        kv = h // 4
                        for b in range(2):
                            last = mm(bank[4][p * HD:(p + 1) * HD, j * P:(j + 1) * P], an["v"][:, b, kv * HD:(kv + 1) * HD],
                                      an["pT"][:, 4 * p + j, b, :], b == 0, b == 1)
                    last.then_inc(s4["o"], 1)
                I = I + 2 * NT
                pe.wait_ge(s4["done"], l * NT + NT)
                pe.sem_inc(pe_turn, 1)
                with pe.Fori(0, DC) as j:
                    slot(0, I + j, xg, full)
                    slot(1, I + j, y1, four)
                I = I + DC
                hid0 = FFC + l * (DC + FFC)
                hid_slots(I, DC, hid0); I = I + X_OUT
                feed_forward(I, hid0 + DC, DC * (2 * l + 4), 2 * l + 6)

        @block.vector
        def _(dve):
            v = nc.vector
            for s in range(2):
                dve.sem_inc(acc_free[s], 1)

            def tt(o, a, b, op=ALU.mult):
                return v.tensor_tensor(o, a, b, op)

            def done(s, I):
                dve.wait_ge(slot_done[s], I + 2)

            def splitted(hi, lo, src):
                v.tensor_copy(hi, src)
                dve.drain()
                return tt(lo, src, bits(hi), ALU.subtract)

            def norm_chunk(j, gain):
                v.tensor_scalar(ffn["t"][:], x[:, j, :], gain, None, ALU.mult)
                tt(ffn["sq"][:], x[:, j, :], x[:, j, :])
                dve.drain()
                v.tensor_copy(xg_hi[:, j, :], ffn["t"][:])
                tt(sumsq[:], sumsq[:], ffn["sq"][:], ALU.add)
                dve.drain()
                tt(xg_lo[:, j, :], ffn["t"][:], bits(xg_hi[:, j, :]), ALU.subtract).then_inc(xg_ready, 1)

            def gain_of(g, j):
                return K["gains"][:, g, bass.ds(j, 1)]

            def norm_end(count_root):
                dve.drain()
                dve.sem_inc(sumsq_ready, 1)
                dve.wait_ge(root_ready, count_root)
                dve.sem_inc(dve_turn, 1)

            def add_to_x(I0, gain=None, final=False):
                if gain is not None:
                    v.memset(sumsq[:], 0.0)
                    dve.drain()
                with dve.Fori(0, X_OUT) as i:
                    for s in range(2):
                        j = 2 * i + s
                        done(s, I0 + i)
                        tt(x[:, j, :], x[:, j, :], acc[s][:], ALU.add).then_inc(acc_free[s], 1)
                        dve.drain()
                        if final:
                            dve.sem_inc(x_final, 1)
                        if gain is not None:
                            norm_chunk(j, gain_of(gain, j))

            def scaled(s, I, dst):
                done(s, I)
                return tt(dst, acc[s][:], rstd[:])

            def hidden(j, gate, val):
                tt(ffn["h"][:], gate, val)
                dve.drain()
                splitted(hid_hi[:, j, :], hid_lo[:, j, :], ffn["h"][:]).then_inc(hid_ready, 1)

            def swiglu(I, pre0, gain):
                for k, n in enumerate(PARTS):
                    with dve.Fori(0, n) as i:
                        scaled(0, I + i, ffn["t"][:]).then_inc(acc_free[0], 1)
                        dve.drain()
                        dve.sem_inc(h_pre, 1)
                        scaled(1, I + i, ffn["sq"][:]).then_inc(acc_free[1], 1)
                        dve.drain()
                        dve.wait_ge(h_act, pre0 + i + 1)
                        hidden(i, ffn["act"][:], ffn["sq"][:])
                    I, pre0 = I + n, pre0 + n
                    dve.drain()
                    last = k == len(PARTS) - 1
                    add_to_x(I, gain if last else None, last); I = I + X_OUT
                return I

            def ms(ap, val=0.0):
                return v.memset(ap, val)

            ms(sumsq[:])
            dve.wait_ge(keep_in, load_wait * (len(KEEP) - 1))
            dve.drain()
            for c in range(DC):
                dve.wait_ge(x_in[c], load_wait)
                v.tensor_scalar(ffn["t"][:], x[:, c, :], K["gains"][:, G_N1, c:c + 1], None, ALU.mult)
                dve.drain()
                splitted(xg_hi[:, c, :], xg_lo[:, c, :], ffn["t"][:]).then_inc(xg_ready, 1)
                dve.wait_ge(squared, c + 1)
                tt(sumsq[:], sumsq[:], mixed[:, c, :], ALU.add)
                dve.drain()
            norm_end(1)
            ms(S1[:])
            ms(m1["td"][:])
            ms(att[:])
            dve.wait_ge(first_in, load_wait * len(FIRST))

            def take(i, dst):
                for s in range(2):
                    scaled(s, i, dst[:, s, :]).then_inc(acc_free[s], 1)
                dve.drain()
                dve.sem_inc(s1["z"], 1)

            take(0, z[:, 2:4, :])
            vtok = z[:, 14:16, :].rearrange("p (s t) c -> p s (t c)", s=1)[:, 0, :].rearrange("p (n c) -> p n c", n=NT)
            itok = z[:, 16:18, :].rearrange("p (s t) c -> p s (t c)", s=1)[:, 0, :].rearrange("p (n c) -> p n c", n=NT)
            khtok = m1["tc"][:].rearrange("p (s t) c -> p s (t c)", s=1)[:, 0, :].rearrange("p (n c) -> p n c", n=NT)
            vec = K["vec1"]

            def col(k):
                return vec[:, k:k + 1]

            for j in range(2):
                v.tensor_copy(m1["td"][:, j, 16:], z[:, 2 + j, :])
            dve.drain()
            for j in range(2):
                v.tensor_scalar(m1["ta"][:, j, :], m1["td"][:, j, 16:16 + T], col(U_CW + 4 * j + 3), col(U_CB + j), ALU.mult, ALU.add)
            dve.drain()
            for k in range(3):
                for j in range(2):
                    v.scalar_tensor_tensor(m1["ta"][:, j, :], m1["td"][:, j, 13 + k:13 + k + T], col(U_CW + 4 * j + k),
                                           m1["ta"][:, j, :], ALU.mult, ALU.add)
                dve.drain()
            dve.sem_inc(s1["conv"], 1)
            lam, lp = vec[:, U_LAM:U_LAM + 2], [sml[:, 8 + 2 * k:10 + 2 * k] for k in range(8)]
            v.tensor_scalar(lp[0], lam, -1.0, 0.0, ALU.mult, ALU.max)
            v.tensor_scalar(lp[1], lam, -1.0, None, ALU.mult)
            dve.drain()
            tt(lp[1], lp[1], lam, ALU.min)
            dve.drain()
            dve.sem_inc(s1["la"], 1)
            take(1, z[:, 4:6, :])
            tt(K["ws"][:], K["ws"][:], mid(K["causal"][:], 4)).then_inc(s1["wm"], 1)
            dve.wait_ge(s1["ea"], 1)
            v.tensor_scalar(lp[3], lp[2], 2.0, None, ALU.add)
            dve.drain()
            v.reciprocal(lp[3], lp[3])
            dve.drain()
            tt(lp[3], lp[3], lp[2])
            dve.drain()
            tt(lp[4], lp[3], lp[3])
            ms(lp[5], 1.0 / 19)
            dve.drain()
            for k in range(17, 0, -2):
                tt(lp[5], lp[5], lp[4])
                dve.drain()
                v.tensor_scalar(lp[5], lp[5], 1.0 / k, None, ALU.add)
                dve.drain()
            tt(lp[5], lp[5], lp[3])
            dve.drain()
            v.scalar_tensor_tensor(lp[0], lp[5], 2.0, lp[0], ALU.mult, ALU.add)
            dve.drain()
            v.tensor_scalar(lp[0], lp[0], 8.0, None, ALU.mult)
            take(2, m1["tg"])
            dve.wait_ge(s1["sig"], 1)
            for j in range(2):
                v.tensor_scalar(z[:, 2 + j, :], z[:, 2 + j, :], lp[0][:, j:j + 1], None, ALU.mult)
            tt(m1["ta"][:], m1["ta"][:], m1["te"][:])
            dve.drain()
            dve.sem_inc(s1["mlt"], 1)
            take(3, z[:, 0:2, :])
            dve.wait_ge(s1["act1"], 2)
            st = sml[:, 24:48].rearrange("p (n c) -> p n c", n=NT)
            ag = sml[:, 48:56].rearrange("p (n c) -> p n c", n=NT)
            for n in range(NT):
                v.bn_stats(st[:, n, :], vtok[:, n, :])
            dve.drain()
            for n in range(NT):
                v.bn_aggr(ag[:, n, :], st[:, n, :])
            dve.drain()
            dve.sem_inc(s1["lv"], 1)
            dve.wait_ge(s1["scan"], 1)
            tt(m1["tb"][:], m1["tb"][:], m1["td"][:, :, 0:T])
            dve.drain()
            dve.sem_inc(s1["hx"], 1)
            dve.wait_ge(s1["sqr"], 1)
            for n in range(NT):
                v.tensor_scalar(vtok[:, n, :], vtok[:, n, :], ag[:, n, 0:1], sml[:, n:n + 1], ALU.subtract, ALU.mult)
            dve.drain()
            tt(vtok, vtok, mid(K["lng"][:], NT))
            dve.drain()
            tt(vtok, vtok, mid(K["lnb"][:], NT), ALU.add)
            dve.drain()
            dve.sem_inc(s1["vn"], 1)
            take(4, z[:, 8:10, :])
            zf = z[:, 8:10, :]
            v.scalar_tensor_tensor(m1["tf"][:], zf, -1.0, zf, ALU.mult, ALU.min)
            dve.drain()
            dve.sem_inc(s1["lf"], 1)
            dve.wait_ge(s1["hl"], 1)
            tt(m1["ta"][:], m1["ta"][:], m1["tb"][:])
            dve.drain()
            for j in range(2):
                v.tensor_tensor_scan(m1["tb"][:, j, :], m1["tc"][:, j, :], m1["ta"][:, j, :], 0.0, ALU.mult, ALU.add)
            dve.drain()
            tt(m1["tb"][:], m1["tb"][:], z[:, 4:6, :])
            dve.drain()
            for j in range(2):
                splitted(y_hi[:, 2 + j, :], y_lo[:, 2 + j, :], m1["tb"][:, j, :])
            dve.wait_ge(s1["sil"], 1)
            v.scalar_tensor_tensor(m1["ta"][:], zf, 0.0, m1["tf"][:], ALU.min, ALU.subtract)
            dve.drain()
            lf = m1["td"][:, :, 0:T]
            for j in range(2):
                v.tensor_tensor_scan(lf[:, j, :], K["reset128"][:], m1["ta"][:, j, :], 0.0, ALU.mult, ALU.add)
            take(5, z[:, 6:8, :])
            dve.wait_ge(s1["act1"], 3)
            dve.wait_ge(s1["sv"], 1)
            for j in range(2):
                tt(r3(m1["tg"][:, j, :], NT), r3(bank[j][:], NT), mid(K["bs"][:, j, :], NT), ALU.add)
            dve.drain()
            dve.sem_inc(s1["gel"], 1)
            for j in range(2):
                tt(m1["tg"][:, j, :], m1["tg"][:, j, :], z[:, j, :])
            dve.drain()
            for j in range(2):
                splitted(y_hi[:, j, :], y_lo[:, j, :], m1["tg"][:, j, :])
            dve.drain()
            dve.sem_inc(y_ready, 4)
            take(6, m1["th"])
            def decays(lev):
                m, e = 1 << lev, m1[("ta", "tf")[lev % 2]]
                for j in range(2):
                    lj = lf[:, j, :].rearrange("p (b m) -> p b m", m=2 * m)
                    tt(e[:, j, :].rearrange("p (b m) -> p b m", m=2 * m), lj, lj[:, :, m - 1:m].to_broadcast([P, T // (2 * m), 2 * m]), ALU.subtract)
                dve.drain()
                v.scalar_tensor_tensor(e[:], e[:], -1.0, e[:], ALU.mult, ALU.min)
                dve.drain()
                dve.sem_inc(s1["ex"], 1)

            def decayed(lev):
                m, e, k = 1 << lev, m1[("ta", "tf")[lev % 2]], lev % 2
                for second, dst, src in ((1, ("tb", "tg")[k], z[:, 6:8, :]), (0, ("tc", "th")[k], m1["te"][:])):
                    o, a, b = m1[dst][:], e[:], src
                    if lev >= 2:
                        o, a, b = (t.rearrange("p j (b s m) -> p (j b) s m", s=2, m=m)[:, :, second, :] for t in (o, a, b))
                    tt(o, a, b)
                dve.drain()

            def chosen(lev):
                for half in range(2):
                    dve.wait_ge(s1["sc"], 2 * lev + half + 1)
                    for p in range(2):
                        v.copy_predicated(att[:, half, p], mid(K["hgmask"][:, lev, :], 4), r3(bank[2 * half + p][:], 4))
                    dve.drain()
                    dve.sem_inc(s1["scev"], 1)

            decays(0)
            for lev in range(7):
                if lev == 0:
                    take(7, z[:, 10:12, :])
                if lev == 1:
                    take(8, z[:, 12:14, :])
                if lev < 6:
                    decays(lev + 1)
                dve.wait_ge(s1["hl"], lev + 2)
                if lev == 1:
                    dve.wait_ge(s1["vT"], 2)
                decayed(lev)
                dve.sem_inc(s1["qk"], 1)
                if lev > 0:
                    chosen(lev - 1)
            dve.sem_inc(s1["qk"], 1)
            for j in range(2):
                lj = r3(lf[:, j, :], NT)
                tt(r3(m1["ta"][:, j, :], NT), lj[:, :, P - 1:P].to_broadcast([P, NT, P]), lj, ALU.subtract)
            dve.drain()
            dve.sem_inc(s1["ex"], 1)
            chosen(6)
            chosen(7)
            dve.wait_ge(s1["hl"], 9)
            for j in range(2):
                v.tensor_copy(sml[:, 56 + 4 * j:60 + 4 * j], r3(m1["tf"][:, j, :], NT)[:, :, P - 1])
            tt(m1["tb"][:], m1["ta"][:], m1["te"][:])
            dve.drain()
            dve.sem_inc(s1["kh"], 1)
            tt(m1["tf"][:], m1["tf"][:], z[:, 6:8, :])
            dve.wait_ge(s1["khT"], 1)
            for n in range(NT):
                v.tensor_copy(khtok[:, n, :], bank[n // 2][:, (n % 2) * 2 * P:(n % 2 + 1) * 2 * P])
            dve.drain()
            dve.sem_inc(s1["khv"], 1)
            dve.sem_inc(s1["st"], 1)
            dve.drain()
            ms(m1["td"][:, :, 0:16])
            pads = z[:, 0:3, :].rearrange("p (s t) c -> p s (t c)", s=1)[:, 0, 0:2 * (T + 16)].rearrange("p (j c) -> p j c", j=2)
            ms(pads[:, :, 0:16])
            v.tensor_copy(m1["td"][:, :, 16:], z[:, 12:14, :])
            dve.drain()

            def double(dst, src, w, rows, j):
                tt(dst[rows, j, 16:16 + T], src[rows, j, 16:16 + T], src[rows, j, 16 - w:16 - w + T], ALU.add)

            top, low, both = slice(0, HD), slice(HD, P), slice(0, P)
            A, B = m1["td"], pads
            double(B, A, 1, both, 0)
            double(B, A, 1, both, 1)
            dve.drain()
            v.tensor_copy(A[top, 0, 16:], B[top, 0, 16:])
            double(A, B, 2, low, 0)
            double(A, B, 2, both, 1)
            dve.drain()
            double(B, A, 4, both, 1)
            dve.drain()
            v.tensor_copy(A[top, 1, 16:], B[top, 1, 16:])
            double(A, B, 8, low, 1)
            dve.drain()
            for j in range(2):
                tt(m1["th"][:, j, :], A[:, j, 16:], K["invcnt"][:, j, :])
            dve.drain()
            tt(m1["th"][:], m1["th"][:], z[:, 12:14, :], ALU.subtract)
            dve.drain()
            dve.sem_inc(s1["pool"], 1)
            for n in range(NT):
                dve.wait_ge(s1["kv"], n + 1)
                if n < NT - 1:
                    for j in range(2):
                        for p in range(2):
                            r, c = slice(p * HD, (p + 1) * HD), slice(p * HD, (p + 1) * HD)
                            v.scalar_tensor_tensor(S1[r, j, c], S1[r, j, c], sml[r, 56 + 4 * j + n:57 + 4 * j + n],
                                                   bank[n % 2][r, j * P + p * HD:j * P + (p + 1) * HD], ALU.mult, ALU.add)
                    dve.drain()
                    dve.sem_inc(s1["st"], 1)
                if n == 1:
                    dve.wait_ge(s1["dwy"], 1)
                    for j in range(2):
                        v.tensor_scalar(m1["tg"][:, j, :], bank[4 + j][:], col(U_DS + j), None, ALU.mult)
                    dve.drain()
                    for j in range(2):
                        splitted(y_hi[:, 6 + j, :], y_lo[:, 6 + j, :], m1["tg"][:, j, :]).then_inc(y_ready, 1)
            for j in range(2):
                v.tensor_copy(m1["tb"][:, j, :], bank[2 + j][:])
            dve.drain()
            tt(m1["ta"][:], m1["tb"][:], m1["tb"][:])
            dve.drain()
            dve.sem_inc(s1["osq"], 1)
            dve.wait_ge(s1["o"], 1)
            tt(m1["tb"][:], m1["tb"][:], m1["ta"][:])
            dve.drain()
            for j in range(2):
                v.scalar_tensor_tensor(m1["tb"][:, j, :], m1["tb"][:, j, :], col(U_CN + j), z[:, 10 + j, :], ALU.mult, ALU.mult)
            dve.drain()
            for j in range(2):
                splitted(y_hi[:, 4 + j, :], y_lo[:, 4 + j, :], m1["tb"][:, j, :]).then_inc(y_ready, 1)
            dve.drain()
            ms(ffn["pad"][:, :, 0:2])
            add_to_x(B1_IN, G_N2)
            norm_end(2)
            I, pre = B1_IN + X_OUT, 0
            fw = vec[:, U_FW:U_FW + 6 * FFC].rearrange("p (i s k) -> p i s k", s=2, k=3)
            fb = vec[:, U_FB:U_FB + 2 * FFC].rearrange("p (i s) -> p i s", s=2)
            for k, n in enumerate(PARTS):
                if k == 1:
                    dve.wait_ge(first_in, load_wait * (len(FIRST) + 1))
                    for j in range(2):
                        splitted(emb_hi[:, j, :], emb_lo[:, j, :], emb[:, j, :])
                with dve.Fori(0, n) as i:
                    c = i + sum(PARTS[:k])
                    for s in range(2):
                        pad, cv = ffn["pad"][:, s, :], ffn["cv"][:, s, :]
                        if s == 0:
                            dve.wait_ge(h_act, pre + i) if k else None
                        scaled(s, I + i, pad[:, 2:]).then_inc(acc_free[s], 1)
                        dve.drain()
                        v.tensor_scalar(cv, pad[:, 2:], fw[:, bass.ds(c, 1), s, 2], fb[:, bass.ds(c, 1), s], ALU.mult, ALU.add)
                        for d in range(2):
                            dve.drain()
                            v.scalar_tensor_tensor(cv, pad[:, d:d + T], fw[:, bass.ds(c, 1), s, d], cv, ALU.mult, ALU.add)
                        dve.drain()
                        if s == 0:
                            dve.sem_inc(h_pre, 1)
                    dve.wait_ge(h_act, pre + i + 1)
                    hidden(i, ffn["act"][:], ffn["cv"][:, 1, :])
                    dve.drain()
                I, pre = I + n, pre + n
                dve.drain()
                add_to_x(I, G_N3 if k == len(PARTS) - 1 else None); I = I + X_OUT
            norm_end(3)
            ms(sumsq[:])
            ms(sumsq_fin)
            dve.drain()

            def embedding_gate(j):
                scaled(0, I + j, ffn["t"][:]).then_inc(acc_free[0], 1)
                dve.drain()
                dve.sem_inc(h_pre, 1)

            def embedding(j):
                dve.wait_ge(h_act, FFC + j + 1)
                done(1, I + j)
                tt(ffn["h"][:], acc[1][:], ffn["act"][:]).then_inc(acc_free[1], 1)
                dve.drain()

            def finished(j):
                tt(x[:, j, :], x[:, j, :], ffn["h"][:], ALU.add)
                dve.drain()
                tt(ffn["sq"][:], x[:, j, :], x[:, j, :])
                dve.drain()
                v.tensor_scalar(x[:, j, :], x[:, j, :], gain_of(G_FIN, j), None, ALU.mult)
                tt(sumsq[:], sumsq[:], ffn["sq"][:], ALU.add)
                dve.drain()
                tt(ffn["sq"][:], x[:, j, :], x[:, j, :])
                v.tensor_scalar(mixed[:, j, :], x[:, j, :], gain_of(G_L, j), None, ALU.mult)
                dve.drain()
                tt(sumsq_fin, sumsq_fin, ffn["sq"][:], ALU.add)

            embedding_gate(0)
            embedding(0)
            with dve.Fori(0, PE_PAIRS - 1) as j:
                embedding_gate(j + 1)
                finished(j)
                embedding(j + 1)
            with dve.Fori(PE_PAIRS - 1, PE_PAIRS) as j:
                finished(j)
            dve.drain()
            dve.sem_inc(sumsq_ready, 1)
            for c in range(DC):
                if c == DC // 2:
                    dve.wait_ge(root_ready, 4)
                    v.tensor_copy(rstd_fin, rstd[:])
                    tt(sumsq[:], sumsq_fin, rstd[:])
                    dve.drain()
                    tt(sumsq[:], sumsq[:], rstd[:])
                    dve.drain()
                    dve.sem_inc(sumsq_ready, 1)
                splitted(xg_hi[:, c, :], xg_lo[:, c, :], mixed[:, c, :]).then_inc(xg_ready, 1)
            for c in range(DC):
                tt(x[:, c, :], x[:, c, :], rstd_fin)
            dve.drain()
            vec2 = K["vec2"]

            def pcol(k, n=4):
                return vec2[:, k:k + n]

            with dve.Fori(0, LAYERS) as l:
                I = B1_PAIRS + l * LAYER_PAIRS
                dve.wait_ge(layer_in, load_wait * (1 + len(RWKV)) * (l + 1))
                dve.wait_ge(root_ready, 2 * l + 5)
                tt(rstd[:], rstd[:], rstd_fin)
                dve.drain()
                hz, dz = rw["SC"][:].rearrange("p (s a) b c -> p s (a b c)", s=4), rw["W"]
                for s in range(2):
                    ms(hz[:, s, 0:1])
                dve.drain()

                def shifted(i, s, j):
                    scaled(s, I + i, hz[:, s, 1:T + 1]).then_inc(acc_free[s], 1)
                    dve.drain()
                    tt(dz[:], hz[:, s, 0:T], hz[:, s, 1:T + 1], ALU.subtract)
                    dve.drain()
                    v.scalar_tensor_tensor(z_rw[:, bass.ds(j, 1), :].rearrange("p a b -> p (a b)"), dz[:], vec2[:, bass.ds(V_MU + j, 1)],
                                           hz[:, s, 1:T + 1], ALU.mult, ALU.add)
                    dve.drain()

                for s in range(2):
                    shifted(0, s, 12 + s)
                dve.sem_inc(s2["z"], 1)
                with dve.Fori(1, RW_PAIRS) as i:
                    for s in range(2):
                        shifted(i, s, 2 * i - 2 + s)
                I = I + RW_PAIRS
                ms(rw["S"][:])
                ms(rw["W"][:])
                ms(rw["U"][:])
                dve.drain()

                def after(name, it, k, per=1):
                    dve.wait_ge(s2[name], it * per + k)

                def say(name, k=1):
                    dve.drain()
                    dve.sem_inc(s2[name], k)

                def normalised(n):
                    after("yroot", l * NT + n, 1)
                    yv = tile_of(z_rw, 4, 4, n)
                    tt(yv, yv, r3(rw["U"][:], 4))

                def gated(n):
                    yv = tile_of(z_rw, 4, 4, n)
                    tt(yv, yv, bc(pcol(V_LNG), P))
                    dve.drain()
                    tt(yv, yv, bc(pcol(V_LNB), P), ALU.add)
                    dve.drain()
                    tt(yv, yv, tile_of(z_rw, 0, 4, n), ALU.add)
                    dve.drain()
                    tt(yv, yv, tile_of(z_rw, 8, 4, n))
                    dve.drain()
                    splitted(tile_of(y1_hi, 0, 4, n), tile_of(y1_lo, 0, 4, n), yv)
                    say("done")

                def rwkv_tile(n, before):
                    it, F = l * NT + n, I + 2 * n

                    def take(s, k):
                        scaled(s, F + k, z_rt[:, bass.ds(4 * n + 2 * k + s, 1), :].rearrange("p a b -> p (a b)")).then_inc(acc_free[s], 1)

                    zr, zk, zv = (tile_of(z_rw, a, 4, n) for a in (0, 4, 8))
                    say("stev")
                    tt(rw["kk"][:], zk, bc(pcol(V_KK), P))
                    dve.drain()
                    tt(rw["sq"][:], rw["kk"][:], rw["kk"][:])
                    after("lora", it, 1)
                    tt(rw["kp"][:], r3(bank[0][:], 4), bc(pcol(V_W0), P), ALU.add)
                    tt(rw["b"][:], r3(bank[1][:], 4), bc(pcol(V_A0), P), ALU.add)
                    say("pre")
                    if before is not None:
                        normalised(before)
                    after("sig", it, 1)
                    flat = [rw[k][:].rearrange("p a b -> p (a b)") for k in ("Lr", "kp")]
                    v.tensor_tensor_scan(flat[0], K["reset64"][:], flat[1], 0.0, ALU.mult, ALU.add)
                    dve.drain()
                    tt(rw["Lp"][:], rw["Lr"][:], rw["kp"][:], ALU.subtract)
                    lr = rw["Lr"][:].rearrange("p a (c t) -> p (a c) t", c=2)
                    tt(rw["Dl"][:].rearrange("p a (c t) -> p (a c) t", c=2), lr[:, :, CH - 1:CH].to_broadcast([P, 8, CH]), lr, ALU.subtract)
                    say("L")
                    v.scalar_tensor_tensor(rw["kp"][:], rw["b"][:], -1.0, bc(pcol(V_KA), P), ALU.add, ALU.mult)
                    dve.drain()
                    v.scalar_tensor_tensor(rw["kp"][:], rw["kp"][:], 1.0, zk, ALU.add, ALU.mult)
                    dve.drain()
                    tt(rw["bon"][:], zr, rw["kp"][:])
                    dve.drain()
                    tt(rw["bon"][:], rw["bon"][:], bc(pcol(V_RK), P))
                    say("nrm_in")
                    take(0, 0)
                    take(1, 0)
                    after("nrm", it, 1)
                    v.tensor_scalar(rw["sq"][:], r3(bank[0][:], 4), 1e-24, None, ALU.max)
                    say("rn")
                    after("exp", it, 1)
                    tt(rw["AR"][:, :, 1, :], zr, rw["eP"][:])
                    tt(rw["KH"][:], rw["kp"][:], rw["Dl"][:])
                    v.tensor_copy(rw["VT"][:], zv)
                    dve.drain()
                    tt(zr, r3(bank[1][:], 4), zv)
                    dve.drain()
                    v.tensor_copy(zv, r3(bank[2][:], 4))
                    say("opk")
                    tt(rw["KT"][:], rw["kp"][:], rw["eM"][:])
                    v.tensor_copy(rw["pc"][:], rw["eP"][:].rearrange("p a (c t) -> p a c t", c=2)[:, :, :, CH - 1])
                    after("root", it, 1)
                    tt(rw["kk"][:], rw["kk"][:], rw["sq"][:])
                    dve.drain()
                    v.scalar_tensor_tensor(rw["AR"][:, :, 0, :], rw["kk"][:], -1.0, rw["Lp"][:], ALU.mult, ALU.mult)
                    tt(rw["b"][:], rw["b"][:], rw["kk"][:])
                    dve.drain()
                    tt(rw["BH"][:], rw["b"][:], rw["Dl"][:])
                    tt(rw["BT"][:], rw["b"][:], rw["eM"][:])
                    say("ops")
                    take(0, 1)
                    take(1, 1)
                    tl = rw["SC"][:, :, 0, :]
                    for h in range(8):
                        after("sc", it, h + 1, 8)
                        tt(rw["SC"][:, h], r3(bank[3 + h % 2][:], 4), K["rwmask"][:])
                        say("scev")
                        if h % 4 == 3:
                            half = slice(h - 3, h + 1)
                            tt(rw["G"][:, half], tl[:, half], mid(K["lev"][:, 0, :], 4))
                            dve.drain()
                            tt(rw["G"][:, half], rw["G"][:, half], mid(K["ident"][:], 4), ALU.add)
                            say("g1")
                    after("tr", it, 1)

                    def blocks(lev):
                        tt(rw["TL"][:], tl, mid(K["lev"][:, lev, :], 8))
                        say("tl")

                    blocks(1)
                    for lev in range(1, 6):
                        for half in range(2):
                            after("y", it, 2 * (lev - 1) + half + 1, 10)
                            tt(rw["Y"][:, 4 * half:4 * half + 4], r3(bank[3 + half][:], 4), mid(K["ident"][:], 4), ALU.add)
                            say("yi")
                        if lev < 5:
                            blocks(lev + 1)
                            for half in range(2):
                                after("g", it, 2 * (lev - 1) + half + 1, 10)
                                dve.sem_inc(dve_turn, 1)
                                v.transpose(rw["X"][:, 4 * half:4 * half + 4].rearrange("p a b -> p (a b)"), bank[(2, 5)[half]][:])
                                say("xt")
                    if before is not None:
                        gated(before)
                    for c in range(2):
                        after("sread", it, c + 1, 2)
                        tt(rw["S"][:], rw["S"][:], bc(rw["pc"][:, :, c], P))
                        dve.drain()
                        after("st", it, c + 1, 2)
                        for p in range(2):
                            r = slice(p * HD, (p + 1) * HD)
                            tt(rw["S"][r, :, r], rw["S"][r, :, r], r3(bank[1][r, :], 4)[:, :, r], ALU.add)
                        say("stev")
                    after("yo", it, 1)
                    dve.sem_inc(dve_turn, 1)
                    v.tensor_copy(zk, r3(bank[0][:], 4))
                    say("ysb")
                    after("ysum", it, 1)
                    v.scalar_tensor_tensor(zk, r3(bank[2][:], 4), -1.0 / HD, zk, ALU.mult, ALU.add)
                    dve.drain()
                    tt(r3(rw["U"][:], 4), zk, zk)
                    say("ysq")

                rwkv_tile(0, None)
                with dve.Fori(1, NT) as n:
                    rwkv_tile(n, n - 1)
                normalised(NT - 1)
                dve.drain()
                gated(NT - 1)
                I = I + RET_PAIRS
                ms(an["k"][:, :, 0:P])

                def normalise_queries(i):
                    dve.wait_ge(s4["root"], AT_PAIRS * l + i + 1)
                    for c in (2 * i, 2 * i + 1):
                        v.scalar_tensor_tensor(z_at[:, c, :], z_at[:, c, :], pcol(V_GQ, 1), an["rs"][:, c, :], ALU.mult, ALU.mult)

                for i in range(AT_PAIRS):
                    for s in range(2):
                        scaled(s, I + i, z_at[:, 2 * i + s, :]).then_inc(acc_free[s], 1)
                    dve.drain()
                    for c in (2 * i, 2 * i + 1):
                        if c < 5:
                            tt(an["sq"][:, c, :], z_at[:, c, :], z_at[:, c, :])
                    dve.drain()
                    dve.sem_inc(s4["sq"], 1)
                    if i > 0:
                        normalise_queries(i - 1)
                I = I + AT_PAIRS

                def gate(i, first):
                    scaled(0, first + i, ffn["t"][:]).then_inc(acc_free[0], 1)
                    dve.drain()
                    dve.sem_inc(o_gate, 1)

                def branch(i, first, dst):
                    dve.wait_ge(o_sig, l * O_PAIRS + i + 1)
                    done(1, first + i)
                    tt(dst, acc[1][:], ffn["act"][:]).then_inc(acc_free[1], 1)
                    dve.drain()

                O = I
                dve.wait_ge(retat_in, load_wait * len(RETAT) * (l + 1))
                ms(rt["R"][:])
                dve.drain()
                dve.sem_inc(s3["z"], 1)
                with dve.Fori(0, NT) as n:
                    it = l * NT + n

                    def after(name, k, per=1):
                        dve.wait_ge(s3[name], it * per + k)

                    def say(name, k=1):
                        dve.drain()
                        dve.sem_inc(s3[name], k)

                    say("rev")
                    cosn, sinn = (mid(K[k][:, bass.ts(n, P)], 4) for k in ("cos", "sin"))
                    for a, dst in ((0, "qr"), (4, "kr")):
                        tt(rt["t1"][:], tile_of(z_rt, a, 4, n), cosn)
                        if a == 0:
                            after("sw", 1)
                        tt(rt["t2"][:], r3(bank[a // 4][:], 4), sinn)
                        dve.drain()
                        tt(rt[dst][:], rt["t1"][:], rt["t2"][:], ALU.add)
                        dve.drain()
                    tt(rt["qx"][:], rt["qr"][:], K["xi"][:])
                    say("rot")
                    gate(2 * n, O)
                    after("sc", 1)
                    for p in range(2):
                        tt(rt["ST"][:, p], r3(bank[2 + p][:], 4), K["dmat"][:, p])
                    tt(r3(rt["kz"][:], 8), r3(bank[4][:], 8), bc(K["zeta"][:], HD))
                    say("kz")
                    dve.wait_ge(s4["root"], AT_PAIRS * l + AT_PAIRS)
                    for kv in (1, 0):
                        r, at_n = slice(kv * HD, (kv + 1) * HD), bass.ds(n * P + P, P)
                        v.scalar_tensor_tensor(an["k"][r, kv, at_n], z_at[r, 4, bass.ts(n, P)], vec2[r, V_GK:V_GK + 1],
                                               an["k"][r, 0, at_n], ALU.mult, ALU.mult)
                    dve.drain()
                    dve.sem_inc(s4["kn"], 1)
                    branch(2 * n, O, mixed[:, 2 * n, :])
                    after("o", 1)
                    v.tensor_copy(rt["o"][:], r3(bank[0][:], 4))
                    dve.drain()
                    tt(rt["sq"][:], rt["o"][:], rt["o"][:])
                    say("osb")
                    tt(rt["R"][:], rt["R"][:], bc(K["cdecay"][:], P))
                    dve.drain()
                    for p in range(2):
                        r = slice(p * HD, (p + 1) * HD)
                        tt(rt["R"][r, :, r], rt["R"][r, :, r], r3(bank[1][r, :], 4)[:, :, r], ALU.add)
                    say("rev")
                    after("root", 1)
                    tt(rt["o"][:], rt["o"][:], rt["sq"][:])
                    dve.drain()
                    after("silu", 1)
                    tt(rt["o"][:], rt["o"][:], rt["gs"][:])
                    dve.drain()
                    gate(2 * n + 1, O)
                    splitted(tile_of(y2_hi, 0, 4, n), tile_of(y2_lo, 0, 4, n), rt["o"][:])
                    branch(2 * n + 1, O, mixed[:, 2 * n + 1, :])
                    say("done")
                ms(an["v"][:])
                dve.drain()
                with dve.Fori(0, NT) as n:
                    it = l * NT + n

                    def after(name, k, per=1):
                        dve.wait_ge(s4[name], it * per + k)

                    def add_branch(k):
                        j = 2 * n + k
                        branch(DC + j, O, ffn["sq"][:])
                        tt(mixed[:, j, :], mixed[:, j, :], ffn["sq"][:], ALU.add)
                        dve.drain()

                    def say(name, k=1):
                        dve.drain()
                        dve.sem_inc(s4[name], k)

                    v.tensor_copy(an["v"][:, 0, :], an["v"][:, 1, :])
                    dve.drain()
                    v.tensor_copy(an["v"][:, 1, :], z_at[:, 5, bass.ts(n, P)])
                    mask = K["atmask"][:, n, :]
                    for p in range(2):
                        hs = slice(4 * p, 4 * p + 4)
                        after("sc", p + 1, 2)
                        for b in range(2):
                            v.scalar_tensor_tensor(an["s"][:, p, 2 * b:2 * b + 2, :], r3(bank[2 * p + b][:], 2), HD ** -0.5, mid(mask, 2),
                                                   ALU.mult, ALU.add)
                        dve.drain()
                        v.tensor_reduce(an["mx"][:, hs], an["s"][:, p], AX.X, ALU.max)
                        dve.drain()
                        tt(an["mx"][:, hs], an["mx"][:, hs], pcol(V_SINK + 4 * p, 4), ALU.max)
                        dve.drain()
                        v.tensor_scalar(an["nm"][:, hs], an["mx"][:, hs], -1.0, None, ALU.mult)
                        tt(an["es"][:, hs], pcol(V_SINK + 4 * p, 4), an["mx"][:, hs], ALU.subtract)
                        say("mx")
                    gate(DC + 2 * n, O)
                    for p in range(2):
                        hs = slice(4 * p, 4 * p + 4)
                        after("p", p + 1, 2)
                        tt(an["sum"][:, hs], an["sum"][:, hs], an["es"][:, hs], ALU.add)
                        dve.drain()
                        v.reciprocal(an["sum"][:, hs], an["sum"][:, hs])
                        dve.drain()
                        tt(an["s"][:, p], an["s"][:, p], bc(an["sum"][:, hs], 2 * P))
                        say("pn")
                    add_branch(0)
                    gate(DC + 2 * n + 1, O)
                    add_branch(1)
                    after("o", 1)
                    v.tensor_copy(an["o"][:], r3(bank[4][:], 4))
                    dve.drain()
                    splitted(tile_of(y1_hi, 0, 4, n), tile_of(y1_lo, 0, 4, n), an["o"][:])
                    say("done")
                with dve.Fori(0, DC) as j:
                    gate(2 * DC + j, O)
                    branch(2 * DC + j, O, ffn["h"][:])
                    tt(ffn["h"][:], ffn["h"][:], mixed[:, j, :], ALU.add)
                    dve.drain()
                    splitted(hid_hi[:, j, :], hid_lo[:, j, :], ffn["h"][:]).then_inc(hid_ready, 1)
                I = I + O_PAIRS
                dve.drain()
                add_to_x(I, G_L + 1 + 2 * l); I = I + X_OUT
                norm_end(2 * l + 6)
                swiglu(I, FFC + PE_PAIRS + l * FFC, G_L + 2 + 2 * l)
                ms(rstd_fin, 1.0)
                dve.drain()
                dve.sem_inc(sumsq_ready, 1)

        @block.scalar
        def _(act):
            def fn(o, i, f, **kw):
                return nc.scalar.activation(o, i, f, **kw)

            def rsqrt(o, sums, n, eps=None):
                if eps is None:
                    fn(o, sums, ACT.Ln)
                else:
                    fn(o, sums, ACT.Ln, scale=1.0 / n, bias=K["eps"][:, eps:eps + 1])
                act.drain()
                return fn(o, o, ACT.Exp, scale=-0.5)

            def log_table():
                fn(junk[:], K["eps"][:, 0:1], ACT.Ln)

            def roots(count):
                log_table()
                act.wait_ge(stat_ready, count)
                act.sem_inc(act_turn, 1)
                rsqrt(rstd[:], bank[5][:], D, 0).then_inc(root_ready, 1)

            def gates(n, pre0, f, src="t"):
                with act.Fori(0, n) as i:
                    act.wait_ge(h_pre, pre0 + i + 1)
                    act.sem_inc(act_turn, 1)
                    fn(ffn["act"][:], ffn["t"][:] if src == "t" else ffn["cv"][:, 0, :], f).then_inc(h_act, 1)

            act.wait_ge(keep_in, load_wait * (len(KEEP) - 1))
            for c in range(DC):
                act.wait_ge(x_in[c], load_wait)
                fn(mixed[:, c, :], x[:, c, :], ACT.Square).then_inc(squared, 1)
            roots(1)
            act.wait_ge(first_in, load_wait * len(FIRST))
            vec = K["vec1"]
            lp = [sml[:, 8 + 2 * k:10 + 2 * k] for k in range(8)]
            act.wait_ge(s1["la"], 1)
            fn(lp[2], lp[1], ACT.Exp).then_inc(s1["ea"], 1)
            act.wait_ge(s1["z"], 2)
            fn(z[:, 4:6, :], z[:, 4:6, :], ACT.Gelu_apprx_tanh).then_inc(s1["act1"], 1)
            act.wait_ge(s1["ri"], 1)
            for j in range(2):
                fn(z[:, 2 + j, :], bank[2 + j][:], ACT.Sigmoid, bias=vec[:, U_BA + j:U_BA + j + 1])
            for j in range(2):
                last = fn(m1["te"][:, j, :], bank[4 + j][:], ACT.Sigmoid, bias=vec[:, U_BX + j:U_BX + j + 1])
            last.then_inc(s1["sig"], 1)
            act.wait_ge(s1["vT"], 1)
            for b in range(2):
                last = fn(z[:, 14 + b, :], bank[b][:], ACT.Gelu_apprx_tanh)
            last.then_inc(s1["act1"], 1)
            act.wait_ge(s1["z"], 4)
            fn(z[:, 0:2, :], z[:, 0:2, :], ACT.Gelu_apprx_tanh).then_inc(s1["act1"], 1)
            act.wait_ge(s1["mlt"], 1)
            fn(m1["tc"][:], z[:, 2:4, :], ACT.Exp, scale=-1.0)
            fn(m1["tb"][:], z[:, 2:4, :], ACT.Tanh)
            act.drain()
            inv = m1["td"][:, :, 0:T]
            fn(inv, m1["tb"][:], ACT.Ln, bias=1.0)
            act.drain()
            fn(inv, inv, ACT.Exp, scale=-1.0).then_inc(s1["scan"], 1)
            act.wait_ge(s1["lv"], 1)
            ag = sml[:, 48:56].rearrange("p (n c) -> p n c", n=NT)
            rsqrt(sml[:, 0:4], ag[:, :, 1], 1, 0).then_inc(s1["sqr"], 1)
            act.wait_ge(s1["hx"], 1)
            fn(m1["tb"][:], m1["tb"][:], ACT.Sqrt, scale=2.0).then_inc(s1["hl"], 1)
            act.wait_ge(s1["lf"], 1)
            fn(m1["te"][:], z[:, 8:10, :], ACT.Sigmoid, scale=-1.0)
            fn(m1["tf"][:], m1["tf"][:], ACT.Exp)
            act.drain()
            fn(m1["tf"][:], m1["tf"][:], ACT.Ln, bias=1.0).then_inc(s1["sil"], 1)
            act.wait_ge(s1["z"], 6)
            fn(z[:, 6:8, :], z[:, 6:8, :], ACT.Silu)
            act.wait_ge(s1["vT"], 2)
            for b in range(2):
                last = fn(z[:, 16 + b, :], bank[4 + b][:], ACT.Copy)
            last.then_inc(s1["iev"], 1)
            act.wait_ge(s1["z"], 8)
            fn(z[:, 10:12, :], z[:, 10:12, :], ACT.Silu)
            for lev in range(7):
                act.wait_ge(s1["ex"], lev + 1)
                e = m1[("ta", "tf")[lev % 2]]
                fn(e[:], e[:], ACT.Exp).then_inc(s1["hl"], 1)
            act.wait_ge(s1["ex"], 8)
            fn(m1["tf"][:], m1["td"][:, :, 0:T], ACT.Exp)
            fn(m1["ta"][:], m1["ta"][:], ACT.Exp).then_inc(s1["hl"], 1)
            act.wait_ge(s1["on"], 1)
            for j in range(2):
                last = rsqrt(m1["ta"][:, j, :], bank[j][:], HD, 0)
            last.then_inc(s1["o"], 1)
            roots(2)
            gates(FFC, 0, ACT.Gelu_apprx_tanh, "cv")
            roots(3)
            gates(PE_PAIRS, FFC, ACT.Sigmoid)
            roots(4)
            with act.Fori(0, LAYERS) as l:
                roots(2 * l + 5)
                act.wait_ge(s2["z"], l + 1)
                act.sem_inc(act_turn, 1)
                fn(z_rw[0:HD, 12, :], z_rw[0:HD, 12, :], ACT.Tanh)
                fn(z_rw[:, 13, :], z_rw[:, 13, :], ACT.Sigmoid).then_inc(s2["lora_in"], 1)
                with act.Fori(0, NT) as n:
                    it = l * NT + n

                    def after(name, k, per=1):
                        act.wait_ge(s2[name], it * per + k)
                        act.sem_inc(act_turn, 1)

                    after("pre", 1)
                    fn(rw["kp"][:], rw["kp"][:], ACT.Sigmoid)
                    fn(rw["b"][:], rw["b"][:], ACT.Sigmoid).then_inc(s2["sig"], 1)
                    after("L", 1)
                    fn(rw["eP"][:], rw["Lr"][:], ACT.Exp, scale=-DECAY)
                    fn(rw["eM"][:], rw["Lr"][:], ACT.Exp, scale=DECAY)
                    fn(rw["Lp"][:], rw["Lp"][:], ACT.Exp, scale=-DECAY)
                    fn(rw["Dl"][:], rw["Dl"][:], ACT.Exp, scale=-DECAY).then_inc(s2["exp"], 1)
                    log_table()
                    after("rn", 1)
                    rsqrt(rw["sq"][:], rw["sq"][:], 1).then_inc(s2["root"], 1)
                    after("tr", 1)
                    fn(rw["tokB"][:], bank[0][:], ACT.Copy)
                    fn(rw["tokK"][:], bank[1][:], ACT.Copy)
                    fn(rw["tokV"][:], bank[2][:], ACT.Copy)
                    fn(rw["tokA"][:], bank[5][:], ACT.Copy).then_inc(s2["tok"], 1)
                    for half in range(2):
                        after("x", half + 1, 2)
                        fn(rw["X"][:, 4 * half:4 * half + 4], r3(bank[half][:], 4), ACT.Copy).then_inc(s2["xev"], 1)
                    for lev in range(1, 6):
                        for half in range(2):
                            if lev < 5:
                                after("xt", 2 * (lev - 1) + half + 1, 8)
                            else:
                                after("g", 2 * (lev - 1) + half + 1, 10)
                            fn(rw["G"][:, 4 * half:4 * half + 4], r3(bank[(2, 5)[half]][:], 4), ACT.Copy).then_inc(s2["gev"], 1)
                    after("w", 1)
                    fn(rw["W"][:], bank[3][:], ACT.Copy).then_inc(s2["wev"], 1)
                    after("ah", 1)
                    fn(rw["bon"][:], r3(bank[5][:], 4), ACT.Copy).then_inc(s2["ahev"], 1)
                    for c in range(2):
                        cs = slice(c * CH, (c + 1) * CH)
                        after("u", c + 1, 2)
                        fn(rw["U"][cs, :], bank[(4, 3)[c]][cs, :], ACT.Copy).then_inc(s2["uev"], 1)
                    log_table()
                    after("yvar", 1)
                    rsqrt(rw["U"][:], bank[5][:], HD, 1).then_inc(s2["yroot"], 1)

                def gate_sigmoid(i):
                    act.wait_ge(o_gate, l * O_PAIRS + i + 1)
                    act.sem_inc(act_turn, 1)
                    fn(ffn["act"][:], ffn["t"][:], ACT.Sigmoid).then_inc(o_sig, 1)

                def root_of(count, pairs):
                    act.wait_ge(s4["ss"], AT_PAIRS * l + count)
                    act.sem_inc(act_turn, 1)
                    for o, b in pairs:
                        fn(o, bank[b][:], ACT.Ln, scale=1.0 / HD, bias=K["eps"][:, 0:1])
                    act.drain()
                    for o, b in pairs:
                        last = fn(o, o, ACT.Exp, scale=-0.5)
                    return last

                for i in range(2):
                    root_of(i + 1, [(an["rs"][:, c, :], c) for c in (2 * i, 2 * i + 1)]).then_inc(s4["root"], 1)
                root_of(3, [(an["k"][:, 0, P:], 4)])
                fn(z_at[:, 5, :], bank[5][:], ACT.Copy).then_inc(s4["root"], 1)
                act.wait_ge(s3["z"], l + 1)
                act.sem_inc(act_turn, 1)
                with act.Fori(0, NT) as n:
                    it = l * NT + n

                    def after(name, k, per=1):
                        act.wait_ge(s3[name], it * per + k)
                        act.sem_inc(act_turn, 1)

                    after("rev", 1, 2)
                    fn(rt["o"][:], tile_of(z_rt, 12, 4, n), ACT.Copy).then_inc(s3["vf"], 1)
                    fn(rt["gs"][:], tile_of(z_rt, 8, 4, n), ACT.Silu).then_inc(s3["silu"], 1)
                    after("vT", 1)
                    fn(rt["vt"][:], bank[5][:], ACT.Copy).then_inc(s3["vt"], 1)
                    gate_sigmoid(2 * n)
                    after("osum", 1)
                    rsqrt(rt["sq"][:], r3(bank[5][:], 4), HD, 0).then_inc(s3["root"], 1)
                    act.wait_ge(s4["kn"], it + 1)
                    act.sem_inc(act_turn, 1)
                    for kv in range(2):
                        r, q, at_n = slice(kv * HD, (kv + 1) * HD), slice((1 - kv) * HD, (2 - kv) * HD), bass.ds(n * P + P, P)
                        fn(an["k"][q, kv, at_n], an["k"][r, kv, at_n], ACT.Copy)
                    gate_sigmoid(2 * n + 1)
                act.drain()
                with act.Fori(0, NT) as n:
                    it = l * NT + n

                    def after(name, k, per=1):
                        act.wait_ge(s4[name], it * per + k)
                        act.sem_inc(act_turn, 1)

                    fn(an["kw"][:], an["k"][:, :, bass.ds(n * P, 2 * P)], ACT.Copy)
                    fn(an["q"][:], tile_of(z_at, 0, 4, n), ACT.Copy).then_inc(s4["qc"], 1)
                    for p in range(2):
                        after("mx", p + 1, 2)
                        fn(an["es"][:, 4 * p:4 * p + 4], an["es"][:, 4 * p:4 * p + 4], ACT.Exp)
                        for h in range(4 * p, 4 * p + 4):
                            s1h = an["s"][:, p, h % 4, :]
                            fn(s1h, s1h, ACT.Exp, bias=an["nm"][:, h:h + 1], accum_out=an["sum"][:, h:h + 1])
                        act.drain()
                        act.sem_inc(s4["p"], 1)
                    gate_sigmoid(DC + 2 * n)
                    gate_sigmoid(DC + 2 * n + 1)
                    for p in range(2):
                        after("pT", p + 1, 2)
                        for b in (2 * p, 2 * p + 1):
                            last = fn(an["pT"][:, 2 * b:2 * b + 2].rearrange("p a b c -> p (a b c)"), bank[b][:], ACT.Copy)
                    last.then_inc(s4["pTe"], 1)
                with act.Fori(0, DC) as i:
                    gate_sigmoid(2 * DC + i)
                roots(2 * l + 6)
                gates(FFC, FFC + PE_PAIRS + l * FFC, ACT.Silu)



def slots(w, order=None):
    k, n = w.shape[0] // P, w.shape[1] // P
    s = w.reshape(k, P, n, P).transpose(2, 1, 0, 3)
    if order is not None:
        s = s[np.asarray(order)]
    return np.ascontiguousarray(s).reshape(-1, 2, P, k * P)


def columns(v):
    return np.ascontiguousarray(v.reshape(-1, P).T)


def per_head(v):
    return np.concatenate([v, v]).reshape(P, 1)


def block_diagonal(w):
    o = np.zeros((P, 2, P), w.dtype)
    for h in range(4):
        p = slice((h % 2) * HD, (h % 2 + 1) * HD)
        o[p, h // 2, p] = w[h]
    return o


def lay_out(a):
    d = dict(shape_constants())
    x, f = a["x"][0], {k: v[0] for k, v in a.items() if not k.endswith("_2") and k not in ("x", "final_g")}
    d["x"] = np.ascontiguousarray(x.T).reshape(DC, P, T)
    d["p"] = np.ascontiguousarray(f["p"][0].T.reshape(2, P, T).transpose(1, 0, 2))
    g = [f["norm1_g"], f["norm2_g"], f["norm3_g"], a["final_g"]]
    for l in range(LAYERS):
        g += [a["norm1_g_2"][l], a["norm2_g_2"][l]]
    g.append(a["norm1_g_2"][0])
    d["gains"] = np.ascontiguousarray(np.stack([columns(v) for v in g], 1))
    d["w1_in"] = slots(f["w_in"], [4, 5, 6, 7, 2, 3, 0, 1, 10, 11, 8, 9, 12, 13, 14, 15, 16, 17])
    d["w1_out"] = slots(f["w_out"])
    both = [c for j in range(FFC) for c in (j, FFC + j)]

    def ffn(name, up, down):
        pairs, at = slots(up, both), 0
        for k, n in enumerate(PARTS):
            d[f"{name}_up{k}"] = np.ascontiguousarray(pairs[at:at + n])
            d[f"{name}_down{k}"] = slots(down[at * P:(at + n) * P])
            at += n

    ffn("w1", f["w_up"], f["w_down"])
    d["w1_pg"] = slots(f["w_pg"]).reshape(DC, P, DC * P)
    d["w1_pe"] = slots(f["w_pe"]).reshape(DC, P, 2 * P)
    conv = f["ffn_conv_w"].reshape(3, 2, FFC, P).transpose(3, 2, 1, 0).reshape(P, -1)
    convb = f["ffn_conv_b"].reshape(2, FFC, P).transpose(2, 1, 0).reshape(P, -1)
    d["vec1"] = np.ascontiguousarray(np.concatenate([
        f["b_conv_w"].reshape(4, 2, P).transpose(2, 1, 0).reshape(P, 8), columns(f["b_conv_b"]), columns(f["b_ba"]),
        columns(f["b_bx"]), columns(f["b_lam"]), per_head(f["c_norm_g"]), per_head(f["c_norm_g"]), columns(f["d_scale"]),
        conv, convb], 1))
    d["wa"], d["wx"], d["dw"] = (block_diagonal(f[k]) for k in ("b_wa", "b_wx", "d_w"))
    d["ws"] = np.ascontiguousarray(f["a_ws"].transpose(2, 0, 1))
    d["lng"], d["lnb"] = (np.ascontiguousarray(np.broadcast_to(f[k], (P, 2 * P))) for k in ("a_ln_g", "a_ln_b"))
    d["bs"] = np.ascontiguousarray(np.repeat(f["a_bs"].reshape(2, 2, P).transpose(1, 0, 2), HD, axis=0))

    per_layer = {}

    def keep(name, v):
        per_layer.setdefault(name, []).append(v)

    for l in range(LAYERS):
        w = {k[:-2]: v[l] for k, v in a.items() if k.endswith("_2")}
        s = slots(w["w_in"]).reshape(-1, P, DC * P)

        def take(order):
            return s[np.asarray(order)].reshape(-1, 2, P, DC * P)

        keep("w2_rw", take([18, 19, *range(6, 18)]))
        keep("w2_ret", take([*range(20, 28), *range(32, 36), *range(28, 32)]))
        keep("w2_at", take(range(0, 6)))
        keep("w2_gate", s[np.asarray([36 + b * DC + j for b in (1, 2, 0) for j in range(DC)])])
        o = np.stack([slots(w[k]).reshape(DC, P, 4 * P) for k in ("w_rwkv_o", "w_ret_o", "w_attn_o")])
        keep("w2_o", o.reshape(3 * DC, P, 4 * P))
        keep("w2_out", slots(w["w_out"]))
        gate, up = slots(w["w_ffn_gate"]).reshape(FFC, P, DC * P), slots(w["w_ffn_up"]).reshape(FFC, P, DC * P)
        pairs, at = np.stack([gate, up], 1), 0
        for k, n in enumerate(PARTS):
            keep(f"w2_up{k}", pairs[at:at + n])
            keep(f"w2_down{k}", slots(w["w_ffn_down"][at * P:(at + n) * P]))
            at += n
        sink = np.broadcast_to(w["attn_sinks"].reshape(4, 2).T.reshape(1, 8), (P, 8))
        keep("vec2", np.concatenate([columns(w["rwkv_shift_mu"]), *(columns(w["rwkv_" + k]) for k in (
            "w0", "a0", "k_k", "k_a")), columns(w["rwkv_r_k"]), columns(w["rwkv_lnx_g"]), columns(w["rwkv_lnx_b"]),
            per_head(w["attn_q_norm_g"]), per_head(w["attn_k_norm_g"]), sink], 1))
        zero = np.zeros((HD, T), np.float32)
        keep("w2", np.concatenate([w["rwkv_w2"], zero]).reshape(P, 4, P))
        keep("a2", np.concatenate([zero, w["rwkv_a2"]]).reshape(P, 4, P))
        keep("g2", w["rwkv_g2"].reshape(P, 4, P))
    for name, v in per_layer.items():
        d[name] = np.ascontiguousarray(np.stack(v))
    return d


def kernel(**inputs):
    import concourse.bacc as bacc
    from concourse.bass_utils import run_bass_kernel_spmd

    nc = bacc.Bacc("TRN2", target_bir_lowering=False, num_devices=1)
    arrays, dram = {}, {}
    for name, v in lay_out({k: np.asarray(v) for k, v in inputs.items()}).items():
        arrays["in_" + name] = v
        dram[name] = nc.dram_tensor("in_" + name, v.shape, mybir.dt.from_np(v.dtype), kind="ExternalInput").ap()
    out = nc.dram_tensor("out_x", (DC, P, T), F32, kind="ExternalOutput").ap()
    build(nc, dram, out)
    r = run_bass_kernel_spmd(nc, [arrays], core_ids=[0])
    return np.ascontiguousarray(r.results[0]["out_x"].reshape(D, T).T).reshape(1, T, D)
```
